# Optimizing a Trainium2 kernel written in Bass

```python
import math
import jax, jax.numpy as jnp
from jax import lax
import numpy as np

D_MODEL = 1024
BATCH = 1
SEQ = 256
DEPTH = 2

HEAD_DIM = 64
N_RWKV_HEADS = 8
D_RWKV = N_RWKV_HEADS * HEAD_DIM
N_DIFF_HEADS = 4
D_DIFF = N_DIFF_HEADS * 2 * HEAD_DIM
DECAY_LORA = 64
AAA_LORA = 64
GATE_LORA = 128
RWKV_COLS = 3 * D_RWKV + DECAY_LORA + AAA_LORA + GATE_LORA
AB_COLS = RWKV_COLS + 3 * D_DIFF
RWKV_GN_EPS = 64e-5
ROPE_THETA = 500000.0
ROPE_DIM = HEAD_DIM // 4
Q_BLOCK = 128
CHUNK = 128
GMLP_GROUPS = 8
D_GMLP = D_MODEL
D_FF = 2816
CONV_W = 3
N_AB = (DEPTH + 1) // 2
N_C = DEPTH // 2
DEEPNORM_ALPHA = (2 * DEPTH) ** 0.25
DEEPNORM_BETA = (8 * DEPTH) ** -0.25


def layer_norm(x, g, b, eps=1e-5):
    xf = x.astype(jnp.float32)
    mu = jnp.mean(xf, axis=-1, keepdims=True)
    var = jnp.mean(jnp.square(xf - mu), axis=-1, keepdims=True)
    y = (xf - mu) * lax.rsqrt(var + eps)
    return (y * g.astype(jnp.float32) + b.astype(jnp.float32)).astype(x.dtype)

def rms_norm(x, g, eps=1e-5):
    xf = x.astype(jnp.float32)
    y = xf * lax.rsqrt(jnp.mean(jnp.square(xf), axis=-1, keepdims=True) + eps)
    return (y * g.astype(jnp.float32)).astype(x.dtype)

def shift_prev(t):
    return jnp.pad(t[:, :-1], ((0, 0), (1, 0), (0, 0)))

def rope_tables(seq):
    inv_freq = ROPE_THETA ** (-jnp.arange(0, ROPE_DIM, 2, dtype=jnp.float32) / ROPE_DIM)
    ang = jnp.arange(seq, dtype=jnp.float32)[:, None] * inv_freq[None, :]
    return jnp.cos(ang), jnp.sin(ang)

def apply_partial_rope(t, cos, sin):
    half = ROPE_DIM // 2
    c = cos[None, :, None, None, :].astype(t.dtype)
    s = sin[None, :, None, None, :].astype(t.dtype)
    t1, t2, rest = t[..., :half], t[..., half:ROPE_DIM], t[..., ROPE_DIM:]
    return jnp.concatenate([t1 * c - t2 * s, t1 * s + t2 * c, rest], axis=-1)

def wkv7_scan(r, decay, k, v, a_vec, b_vec):
    B, S, H, N = r.shape
    xs = tuple(jnp.moveaxis(t.astype(jnp.float32), 1, 0) for t in (r, decay, k, v, a_vec, b_vec))

    def step(state, inp):
        r_t, w_t, k_t, v_t, a_t, b_t = inp
        sa = jnp.einsum('bhvk,bhk->bhv', state, a_t)
        state = (state * w_t[:, :, None, :] + sa[..., None] * b_t[:, :, None, :]
                 + v_t[..., None] * k_t[:, :, None, :])
        y_t = jnp.einsum('bhvk,bhk->bhv', state, r_t)
        return state, y_t

    s0 = jnp.zeros((B, H, N, N), jnp.float32)
    _, y = lax.scan(step, s0, xs)
    return jnp.moveaxis(y, 0, 1)

def rwkv7_mix(pr, mu, w0, w2, a0, a2, g2, k_k, k_a, r_k, lnx_g, lnx_b):
    B, S, _ = pr.shape

    def heads(t):
        return t.reshape(B, S, N_RWKV_HEADS, HEAD_DIM)

    xs = pr + mu * (shift_prev(pr) - pr)
    r, k, v, xw, xa, xg = jnp.split(
        xs, [D_RWKV, 2 * D_RWKV, 3 * D_RWKV, 3 * D_RWKV + DECAY_LORA,
             3 * D_RWKV + DECAY_LORA + AAA_LORA], axis=-1)
    w = -jax.nn.softplus(-(w0 + jnp.tanh(xw) @ w2)) - 0.5
    decay = jnp.exp(-jnp.exp(w.astype(jnp.float32)))
    a = jax.nn.sigmoid(a0 + xa @ a2)
    g = jax.nn.sigmoid(xg) @ g2
    kk = heads(k * k_k).astype(jnp.float32)
    kk = kk / jnp.maximum(jnp.sqrt(jnp.sum(jnp.square(kk), axis=-1, keepdims=True)), 1e-12)
    k = k * (1.0 + (a - 1.0) * k_a)
    r_h, k_h, v_h, a_h = heads(r), heads(k), heads(v), heads(a)
    y = wkv7_scan(r_h, heads(decay), k_h, v_h, -kk, kk * a_h.astype(jnp.float32))
    mu_y = jnp.mean(y, axis=-1, keepdims=True)
    var_y = jnp.mean(jnp.square(y - mu_y), axis=-1, keepdims=True)
    yn = ((y - mu_y) * lax.rsqrt(var_y + RWKV_GN_EPS)).reshape(B, S, D_RWKV)
    yn = (yn * lnx_g.astype(jnp.float32) + lnx_b.astype(jnp.float32)).astype(pr.dtype)
    bonus = jnp.sum(r_h * k_h * r_k, axis=-1, keepdims=True) * v_h
    return (yn + bonus.reshape(B, S, D_RWKV)) * g

def diff_attention(pd, lam_q1, lam_k1, lam_q2, lam_k2, subln_g, lam_init, cos, sin):
    B, S, _ = pd.shape
    q, k, v = jnp.split(pd, 3, axis=-1)
    q = q.reshape(B, S, N_DIFF_HEADS, 2, HEAD_DIM)
    k = k.reshape(B, S, N_DIFF_HEADS, 2, HEAD_DIM)
    v = v.reshape(B, S, N_DIFF_HEADS, 2 * HEAD_DIM)
    q = apply_partial_rope(q, cos, sin) * (HEAD_DIM ** -0.5)
    k = apply_partial_rope(k, cos, sin)
    lam = (jnp.exp(jnp.sum(lam_q1.astype(jnp.float32) * lam_k1.astype(jnp.float32)))
           - jnp.exp(jnp.sum(lam_q2.astype(jnp.float32) * lam_k2.astype(jnp.float32)))
           + lam_init)
    n_blocks = S // Q_BLOCK
    qb = jnp.moveaxis(q.reshape(B, n_blocks, Q_BLOCK, N_DIFF_HEADS, 2, HEAD_DIM), 1, 0)
    k_pos = jnp.arange(S)

    def block(args):
        q_blk, i = args
        q_pos = i * Q_BLOCK + jnp.arange(Q_BLOCK)
        s = jnp.einsum('bqhcd,bkhcd->bhcqk', q_blk, k).astype(jnp.float32)
        mask = k_pos[None, :] <= q_pos[:, None]
        s = jnp.where(mask[None, None, None], s, -jnp.inf)
        p = jax.nn.softmax(s, axis=-1)
        attn = p[:, :, 0] - lam * p[:, :, 1]
        return jnp.einsum('bhqk,bkhd->bqhd', attn.astype(v.dtype), v)

    o = lax.map(block, (qb, jnp.arange(n_blocks)))
    o = jnp.moveaxis(o, 0, 1).reshape(B, S, N_DIFF_HEADS, 2 * HEAD_DIM)
    o = rms_norm(o, subln_g) * (1.0 - lam_init)
    return o.reshape(B, S, D_DIFF)

def chunked_spatial_gating(x, w_in, b_in, ln_g, ln_b, w_s, b_s):
    B, S, _ = x.shape
    h = jax.nn.gelu(x @ w_in + b_in, approximate=False)
    u, v = jnp.split(h, 2, axis=-1)
    v = layer_norm(v, ln_g, ln_b)
    vc = v.reshape(B, S // CHUNK, CHUNK, GMLP_GROUPS, D_GMLP // GMLP_GROUPS)
    ws = w_s * jnp.tril(jnp.ones((CHUNK, CHUNK), w_s.dtype))
    mixed = jnp.einsum('gts,bcsgd->bctgd', ws, vc) + b_s.T[None, None, :, :, None]
    return u * mixed.reshape(B, S, D_GMLP)

def conv_ffn(x, w_up, conv_w, conv_b, w_down):
    S = x.shape[1]
    gate, val = jnp.split(x @ w_up, 2, axis=-1)
    gp = jnp.pad(gate, ((0, 0), (CONV_W - 1, 0), (0, 0)))
    conv = conv_b
    for j in range(CONV_W):
        conv = conv + conv_w[j] * gp[:, j:j + S]
    return (jax.nn.silu(conv) * val) @ w_down

def first_inputs(seed: int = 0) -> dict:
    key = jax.random.key(seed)
    keys = jax.random.split(key, 48)
    counter = [0]
    f32 = jnp.float32

    def nxt():
        kk = keys[counter[0]]
        counter[0] += 1
        return kk

    def nrm(shape, scale):
        return jax.random.normal(nxt(), shape, f32) * scale

    def unif(shape, lo, hi):
        return jax.random.uniform(nxt(), shape, f32, lo, hi)

    D = D_MODEL
    return {
        'x': nrm((BATCH, SEQ, D), 1.0),
        'ab_w_in': nrm((N_AB, D, AB_COLS), D ** -0.5),
        'ab_shift_mu': unif((N_AB, RWKV_COLS), 0.0, 1.0),
        'ab_w0': unif((N_AB, D_RWKV), -6.0, -1.0),
        'ab_w2': nrm((N_AB, DECAY_LORA, D_RWKV), 0.1),
        'ab_a0': nrm((N_AB, D_RWKV), 0.5),
        'ab_a2': nrm((N_AB, AAA_LORA, D_RWKV), AAA_LORA ** -0.5),
        'ab_g2': nrm((N_AB, GATE_LORA, D_RWKV), GATE_LORA ** -0.5),
        'ab_k_k': 0.85 + nrm((N_AB, D_RWKV), 0.05),
        'ab_k_a': 1.0 + nrm((N_AB, D_RWKV), 0.05),
        'ab_r_k': nrm((N_AB, N_RWKV_HEADS, HEAD_DIM), 0.1),
        'ab_lnx_g': 1.0 + nrm((N_AB, D_RWKV), 0.05),
        'ab_lnx_b': nrm((N_AB, D_RWKV), 0.01),
        'ab_lam_q1': nrm((N_AB, HEAD_DIM), 0.1),
        'ab_lam_k1': nrm((N_AB, HEAD_DIM), 0.1),
        'ab_lam_q2': nrm((N_AB, HEAD_DIM), 0.1),
        'ab_lam_k2': nrm((N_AB, HEAD_DIM), 0.1),
        'ab_subln_g': 1.0 + nrm((N_AB, 2 * HEAD_DIM), 0.05),
        'ab_w_out': nrm((N_AB, D_RWKV + D_DIFF, D), (D_RWKV + D_DIFF) ** -0.5 * DEEPNORM_BETA),
        'c_w_in': nrm((N_C, D, 2 * D_GMLP), D ** -0.5),
        'c_b_in': nrm((N_C, 2 * D_GMLP), 0.01),
        'c_ln_g': 1.0 + nrm((N_C, D_GMLP), 0.05),
        'c_ln_b': nrm((N_C, D_GMLP), 0.01),
        'c_w_s': nrm((N_C, GMLP_GROUPS, CHUNK, CHUNK), CHUNK ** -0.5),
        'c_b_s': 1.0 + nrm((N_C, GMLP_GROUPS, CHUNK), 0.05),
        'c_w_out': nrm((N_C, D_GMLP, D), D_GMLP ** -0.5 * DEEPNORM_BETA),
        'ln1_g': 1.0 + nrm((DEPTH, D), 0.05),
        'ln1_b': nrm((DEPTH, D), 0.01),
        'ffn_w_up': nrm((DEPTH, D, 2 * D_FF), D ** -0.5),
        'ffn_conv_w': nrm((DEPTH, CONV_W, D_FF), CONV_W ** -0.5),
        'ffn_conv_b': nrm((DEPTH, D_FF), 0.01),
        'ffn_w_down': nrm((DEPTH, D_FF, D), D_FF ** -0.5 * DEEPNORM_BETA),
        'ln2_g': 1.0 + nrm((DEPTH, D), 0.05),
        'ln2_b': nrm((DEPTH, D), 0.01),
    }

def first_block(x, ab_w_in, ab_shift_mu, ab_w0, ab_w2, ab_a0, ab_a2, ab_g2, ab_k_k, ab_k_a,
              ab_r_k, ab_lnx_g, ab_lnx_b, ab_lam_q1, ab_lam_k1, ab_lam_q2, ab_lam_k2,
              ab_subln_g, ab_w_out, c_w_in, c_b_in, c_ln_g, c_ln_b, c_w_s, c_b_s, c_w_out,
              ln1_g, ln1_b, ffn_w_up, ffn_conv_w, ffn_conv_b, ffn_w_down, ln2_g, ln2_b):
    S = x.shape[1]
    cos, sin = rope_tables(S)
    for i in range(DEPTH):
        j = i // 2
        if i % 2 == 0:
            p = x @ ab_w_in[j]
            y_r = rwkv7_mix(p[..., :RWKV_COLS], ab_shift_mu[j], ab_w0[j], ab_w2[j], ab_a0[j],
                            ab_a2[j], ab_g2[j], ab_k_k[j], ab_k_a[j], ab_r_k[j],
                            ab_lnx_g[j], ab_lnx_b[j])
            lam_init = 0.8 - 0.6 * math.exp(-0.3 * i)
            y_d = diff_attention(p[..., RWKV_COLS:], ab_lam_q1[j], ab_lam_k1[j], ab_lam_q2[j],
                                 ab_lam_k2[j], ab_subln_g[j], lam_init, cos, sin)
            mix = jnp.concatenate([y_r, y_d], axis=-1) @ ab_w_out[j]
        else:
            mix = chunked_spatial_gating(x, c_w_in[j], c_b_in[j], c_ln_g[j], c_ln_b[j],
                                         c_w_s[j], c_b_s[j]) @ c_w_out[j]
        x = layer_norm(DEEPNORM_ALPHA * x + mix, ln1_g[i], ln1_b[i])
        ffn = conv_ffn(x, ffn_w_up[i], ffn_conv_w[i], ffn_conv_b[i], ffn_w_down[i])
        x = layer_norm(DEEPNORM_ALPHA * x + ffn, ln2_g[i], ln2_b[i])
    return x


GRID_W = 64
CTX_LEN = 256
EPS = 1e-6
NEG_BIG = -1e30
LB_FLOOR = 1e-30

N_BRANCH = 3
BRANCH_WIDTH = D_MODEL // 2

FOURIER_GROUPS = 4
FOURIER_WIDTH = BRANCH_WIDTH
FOURIER_GROUP_DIM = FOURIER_WIDTH // FOURIER_GROUPS

ATTN_HEADS = BRANCH_WIDTH // HEAD_DIM
ATTN_KV_HEADS = ATTN_HEADS // 4
ATTN_WIDTH = ATTN_HEADS * HEAD_DIM
KV_WIDTH = ATTN_KV_HEADS * HEAD_DIM
WINDOW = 128
BLOCK = 128
ROPE_THETA_2 = 10000.0

HGRN_HEADS = 4
HGRN_DK = BRANCH_WIDTH // HGRN_HEADS
HGRN_DV = BRANCH_WIDTH // HGRN_HEADS
HGRN_KW = HGRN_HEADS * HGRN_DK
HGRN_VW = HGRN_HEADS * HGRN_DV
CHUNK_2 = 64

D_FF_2 = 4 * D_MODEL

_SEG_SIZES = (KV_WIDTH, KV_WIDTH, HGRN_VW, HGRN_KW, HGRN_KW,
              ATTN_WIDTH, HGRN_KW, HGRN_VW, FOURIER_WIDTH, N_BRANCH * D_MODEL)
IN_SPLITS = [sum(_SEG_SIZES[:i + 1]) for i in range(len(_SEG_SIZES) - 1)]
D_IN = sum(_SEG_SIZES)
N_STATE_COLS = sum(_SEG_SIZES[:5])
STATE_SPLITS = IN_SPLITS[:4]


F32 = jnp.float32

def rms_norm_2(x, g):
    xf = x.astype(F32)
    y = xf * lax.rsqrt(jnp.mean(xf * xf, axis=-1, keepdims=True) + EPS)
    return (y * g.astype(F32)).astype(x.dtype)

def adaln_norm(x, g, shift, scale):
    return rms_norm_2(x, g) * (1 + scale) + shift

def modulation(cond, w, b):
    m = jax.nn.silu(cond) @ w + b
    return jnp.split(m, 6, axis=-1)

def _heads(a, n):
    return a.reshape(a.shape[:-1] + (n, a.shape[-1] // n))

def _to_bhtd(a, n):
    return jnp.swapaxes(_heads(a, n), 1, 2)

def _flip_t(a):
    return jnp.flip(a, axis=2)

def axial_rope_tables(n_tok):
    n_rows = n_tok // GRID_W
    row = jnp.repeat(jnp.arange(n_rows), GRID_W).astype(F32)
    col = jnp.tile(jnp.arange(GRID_W), n_rows).astype(F32)
    axis_dim = HEAD_DIM // 2
    inv_freq = ROPE_THETA_2 ** (-jnp.arange(0, axis_dim, 2, dtype=F32) / axis_dim)
    ang_r = row[:, None] * inv_freq
    ang_c = col[:, None] * inv_freq
    return (jnp.cos(ang_r), jnp.sin(ang_r), jnp.cos(ang_c), jnp.sin(ang_c))

def apply_axial_rope(t, rope):
    cos_r, sin_r, cos_c, sin_c = rope

    def rot(u, cos, sin):
        u1, u2 = jnp.split(u, 2, axis=-1)
        cos = cos[None, :, None, :]
        sin = sin[None, :, None, :]
        return jnp.concatenate([u1 * cos - u2 * sin, u2 * cos + u1 * sin], axis=-1)

    tr, tc = jnp.split(t, 2, axis=-1)
    return jnp.concatenate([rot(tr, cos_r, sin_r), rot(tc, cos_c, sin_c)], axis=-1).astype(t.dtype)

def _sink_column(sink, ref):
    g = ATTN_HEADS // ATTN_KV_HEADS
    return jnp.broadcast_to(sink.astype(F32).reshape(ATTN_KV_HEADS, g, 1, 1), ref.shape[:-1] + (1,))

def window_attention(q, k, v, kc, vc, sink):
    b, s, _, dh = q.shape
    nb = s // BLOCK
    g = ATTN_HEADS // ATTN_KV_HEADS
    scale = dh ** -0.5
    qb = q.reshape(b, nb, BLOCK, ATTN_KV_HEADS, g, dh)
    pad = ((0, 0), (BLOCK, BLOCK), (0, 0), (0, 0))
    kp = jnp.pad(k, pad).reshape(b, nb + 2, BLOCK, ATTN_KV_HEADS, dh)
    vp = jnp.pad(v, pad).reshape(b, nb + 2, BLOCK, ATTN_KV_HEADS, dh)
    kw = jnp.concatenate([kp[:, :-2], kp[:, 1:-1], kp[:, 2:]], axis=2)
    vw = jnp.concatenate([vp[:, :-2], vp[:, 1:-1], vp[:, 2:]], axis=2)
    s_win = jnp.einsum('bnqhgd,bnkhd->bnhgqk', qb, kw).astype(F32) * scale
    s_ctx = jnp.einsum('bnqhgd,bchd->bnhgqc', qb, kc).astype(F32) * scale
    t_pos = jnp.arange(nb)[:, None, None] * BLOCK + jnp.arange(BLOCK)[None, :, None]
    k_pos = jnp.arange(nb)[:, None, None] * BLOCK - BLOCK + jnp.arange(3 * BLOCK)[None, None, :]
    valid = (jnp.abs(k_pos - t_pos) <= WINDOW) & (k_pos >= 0) & (k_pos < s)
    s_win = jnp.where(valid[None, :, None, None], s_win, NEG_BIG)
    logits = jnp.concatenate([s_win, s_ctx, _sink_column(sink, s_win)], axis=-1)
    p = jax.nn.softmax(logits, axis=-1)
    nw = 3 * BLOCK
    nc = kc.shape[1]
    o = (jnp.einsum('bnhgqk,bnkhd->bnqhgd', p[..., :nw].astype(v.dtype), vw)
         + jnp.einsum('bnhgqc,bchd->bnqhgd', p[..., nw:nw + nc].astype(v.dtype), vc))
    return o.reshape(b, s, ATTN_HEADS * dh)

def context_attention(qc, kc, vc, sink):
    b, lc, _, dh = qc.shape
    g = ATTN_HEADS // ATTN_KV_HEADS
    qg = qc.reshape(b, lc, ATTN_KV_HEADS, g, dh)
    s = jnp.einsum('bqhgd,bkhd->bhgqk', qg, kc).astype(F32) * dh ** -0.5
    p = jax.nn.softmax(jnp.concatenate([s, _sink_column(sink, s)], axis=-1), axis=-1)
    o = jnp.einsum('bhgqk,bkhd->bqhgd', p[..., :lc].astype(vc.dtype), vc)
    return o.reshape(b, lc, ATTN_HEADS * dh)

def fourier_mix(a):
    b, t, _ = a.shape
    ag = a.astype(F32).reshape(b, t, FOURIER_GROUPS, FOURIER_GROUP_DIM)
    y = jnp.fft.fft2(ag, axes=(1, 3), norm='ortho').real
    return y.reshape(b, t, FOURIER_WIDTH).astype(a.dtype)

def hgrn_forget(z, lb):
    zf = z.astype(F32)
    lbf = lb.astype(F32)
    k = (1.0 - lbf) * jax.nn.sigmoid(-zf)
    logf = jnp.logaddexp(jax.nn.log_sigmoid(zf),
                         jnp.log(jnp.maximum(lbf, LB_FLOOR)) + jax.nn.log_sigmoid(-zf))
    return k, logf

def hgrn_kv(i_raw, ff_raw, fb_raw, lb):
    v = _to_bhtd(i_raw.astype(F32), HGRN_HEADS)
    kf, lff = hgrn_forget(ff_raw, lb[0])
    kb, lfb = hgrn_forget(fb_raw, lb[1])
    return (v, _to_bhtd(kf, HGRN_HEADS), _to_bhtd(lff, HGRN_HEADS),
            _to_bhtd(kb, HGRN_HEADS), _to_bhtd(lfb, HGRN_HEADS))

def hgrn_q(q_raw):
    return _to_bhtd(jax.nn.silu(q_raw).astype(F32), HGRN_HEADS)

def gla_chunked(q, k, v, logf, s0):
    b, h, t, dk = q.shape
    dv = v.shape[-1]
    n = t // CHUNK_2

    def to_chunks(a):
        return jnp.moveaxis(a.reshape(b, h, n, CHUNK_2, a.shape[-1]), 2, 0)

    lower = jnp.tril(jnp.ones((CHUNK_2, CHUNK_2), dtype=bool))[:, :, None]

    def step(state, inp):
        qc, kc, vc, lc = inp
        g = jnp.cumsum(lc, axis=2)
        o_inter = jnp.einsum('bhtk,bhkv->bhtv', qc * jnp.exp(g), state)
        diff = g[:, :, :, None, :] - g[:, :, None, :, :]
        decay = jnp.where(lower, jnp.exp(jnp.where(lower, diff, 0.0)), 0.0)
        a = jnp.einsum('bhtsk,bhsk->bhts', qc[:, :, :, None, :] * decay, kc)
        o = o_inter + jnp.einsum('bhts,bhsv->bhtv', a, vc)
        g_last = g[:, :, -1:, :]
        new_state = (jnp.exp(g_last[:, :, 0, :])[..., None] * state
                     + jnp.einsum('bhsk,bhsv->bhkv', kc * jnp.exp(g_last - g), vc))
        return new_state, o

    s_fin, o = lax.scan(step, s0, (to_chunks(q), to_chunks(k), to_chunks(v), to_chunks(logf)))
    o = jnp.moveaxis(o, 0, 2).reshape(b, h, t, dv)
    return o, s_fin

def gla_final_state(k, v, logf):
    g = jnp.cumsum(logf, axis=2)
    return jnp.einsum('bhsk,bhsv->bhkv', k * jnp.exp(g[:, :, -1:, :] - g), v)

def hgrn_bidir(q, kf, lff, kb, lfb, v, s_f, s_b):
    o_f, s_f_new = gla_chunked(q, kf, v, lff, s_f)
    o_b, s_b_new = gla_chunked(_flip_t(q), _flip_t(kb), _flip_t(v), _flip_t(lfb), s_b)
    return o_f + _flip_t(o_b), s_f_new, s_b_new

def hgrn_readout(o, g_raw, norm_g):
    o = rms_norm_2(jnp.swapaxes(o, 1, 2), norm_g)
    return o.reshape(g_raw.shape).astype(g_raw.dtype) * jax.nn.silu(g_raw)

def merge_branches(o_four, o_attn, o_hgrn, gate_raw, w_branch, w_out):
    br = jnp.stack([o_four, o_attn, o_hgrn], axis=-2)
    proj = jnp.einsum('btnc,ncd->btnd', br, w_branch)
    gates = jax.nn.sigmoid(gate_raw.reshape(gate_raw.shape[:-1] + (N_BRANCH, D_MODEL)))
    return jnp.sum(gates * proj, axis=-2) @ w_out

def sq_relu_mlp(h, w1, w2):
    return jnp.square(jax.nn.relu(h @ w1)) @ w2

def second_inputs(seed: int = 0) -> dict:
    key = jax.random.key(seed)
    ks = jax.random.split(key, 18)

    def nrm(k, shape, s):
        return jax.random.normal(k, shape, F32) * s

    return {
        "x": nrm(ks[0], (BATCH, SEQ, D_MODEL), 1.0),
        "c": nrm(ks[1], (BATCH, D_MODEL), 1.0),
        "ctx": nrm(ks[2], (BATCH, CTX_LEN, D_MODEL), 1.0),
        "c_ctx": nrm(ks[3], (D_MODEL,), 1.0),
        "w_mod": nrm(ks[4], (DEPTH, D_MODEL, 6 * D_MODEL), 0.5 * D_MODEL ** -0.5),
        "b_mod": nrm(ks[5], (DEPTH, 6 * D_MODEL), 0.02),
        "norm1_g": 1.0 + nrm(ks[6], (DEPTH, D_MODEL), 0.02),
        "norm2_g": 1.0 + nrm(ks[7], (DEPTH, D_MODEL), 0.02),
        "w_in": nrm(ks[8], (DEPTH, D_MODEL, D_IN), D_MODEL ** -0.5),
        "q_norm_g": 1.0 + nrm(ks[9], (DEPTH, HEAD_DIM), 0.02),
        "k_norm_g": 1.0 + nrm(ks[10], (DEPTH, HEAD_DIM), 0.02),
        "attn_sink": nrm(ks[11], (DEPTH, ATTN_HEADS), 0.5),
        "hgrn_lb_logits": nrm(ks[12], (DEPTH, 2, HGRN_KW), 0.5),
        "hgrn_norm_g": 1.0 + nrm(ks[13], (DEPTH, HGRN_DV), 0.02),
        "w_branch": nrm(ks[14], (DEPTH, N_BRANCH, BRANCH_WIDTH, D_MODEL), BRANCH_WIDTH ** -0.5),
        "w_out": nrm(ks[15], (DEPTH, D_MODEL, D_MODEL), D_MODEL ** -0.5),
        "w_ff1": nrm(ks[16], (DEPTH, D_MODEL, D_FF_2), D_MODEL ** -0.5),
        "w_ff2": nrm(ks[17], (DEPTH, D_FF_2, D_MODEL), D_FF_2 ** -0.5),
    }

def second_block(x, c, ctx, c_ctx, w_mod, b_mod, norm1_g, norm2_g, w_in, q_norm_g, k_norm_g,
              attn_sink, hgrn_lb_logits, hgrn_norm_g, w_branch, w_out, w_ff1, w_ff2):
    bsz, n_tok, _ = x.shape
    rope = axial_rope_tables(n_tok)
    lb_p = jax.nn.softmax(hgrn_lb_logits.astype(F32), axis=0)
    lb_all = jnp.cumsum(lb_p, axis=0) - lb_p[0:1]
    xc = ctx
    for l in range(DEPTH):
        last = l == DEPTH - 1
        mx = [m[:, None, :] for m in modulation(c, w_mod[l], b_mod[l])]
        mc = modulation(c_ctx, w_mod[l], b_mod[l])
        h = adaln_norm(x, norm1_g[l], mx[0], mx[1])
        hc = adaln_norm(xc, norm1_g[l], mc[0], mc[1])

        if last:
            kc_raw, vc_raw, ic_raw, fcf_raw, fcb_raw = jnp.split(
                hc @ w_in[l][:, :N_STATE_COLS], STATE_SPLITS, axis=-1)
        else:
            (kc_raw, vc_raw, ic_raw, fcf_raw, fcb_raw, qc_raw, qhc_raw, ghc_raw,
             fourc_raw, gatec_raw) = jnp.split(hc @ w_in[l], IN_SPLITS, axis=-1)
        kc = rms_norm_2(_heads(kc_raw, ATTN_KV_HEADS), k_norm_g[l])
        vc = _heads(vc_raw, ATTN_KV_HEADS)
        vhc, kfc, lffc, kbc, lfbc = hgrn_kv(ic_raw, fcf_raw, fcb_raw, lb_all[l])
        if last:
            s_f = gla_final_state(kfc, vhc, lffc)
            s_b = gla_final_state(_flip_t(kbc), _flip_t(vhc), _flip_t(lfbc))
        else:
            zeros = jnp.zeros((bsz, HGRN_HEADS, HGRN_DK, HGRN_DV), F32)
            oc_h, s_f, s_b = hgrn_bidir(hgrn_q(qhc_raw), kfc, lffc, kbc, lfbc, vhc, zeros, zeros)
            qc = rms_norm_2(_heads(qc_raw, ATTN_HEADS), q_norm_g[l])
            oc_a = context_attention(qc, kc, vc, attn_sink[l])
            oc_f = fourier_mix(fourc_raw)
            oc_hr = hgrn_readout(oc_h, ghc_raw, hgrn_norm_g[l])
            yc = merge_branches(oc_f, oc_a, oc_hr, gatec_raw, w_branch[l], w_out[l])
            xc = xc + mc[2] * yc
            hc2 = adaln_norm(xc, norm2_g[l], mc[3], mc[4])
            xc = xc + mc[5] * sq_relu_mlp(hc2, w_ff1[l], w_ff2[l])

        (k_raw, v_raw, i_raw, ff_raw, fb_raw, q_raw, qh_raw, gh_raw,
         four_raw, gate_raw) = jnp.split(h @ w_in[l], IN_SPLITS, axis=-1)
        q = apply_axial_rope(rms_norm_2(_heads(q_raw, ATTN_HEADS), q_norm_g[l]), rope)
        k = apply_axial_rope(rms_norm_2(_heads(k_raw, ATTN_KV_HEADS), k_norm_g[l]), rope)
        v = _heads(v_raw, ATTN_KV_HEADS)
        o_a = window_attention(q, k, v, kc, vc, attn_sink[l])
        vh, kf, lff, kb, lfb = hgrn_kv(i_raw, ff_raw, fb_raw, lb_all[l])
        o_h, _, _ = hgrn_bidir(hgrn_q(qh_raw), kf, lff, kb, lfb, vh, s_f, s_b)
        o_hr = hgrn_readout(o_h, gh_raw, hgrn_norm_g[l])
        o_f = fourier_mix(four_raw)
        y = merge_branches(o_f, o_a, o_hr, gate_raw, w_branch[l], w_out[l])
        x = x + mx[2] * y
        h2 = adaln_norm(x, norm2_g[l], mx[3], mx[4])
        x = x + mx[5] * sq_relu_mlp(h2, w_ff1[l], w_ff2[l])
    return x


def setup_inputs(seed=0):
    out = dict(first_inputs(seed))
    for name, value in second_inputs(seed + 1).items():
        if name != "x":
            out[name + "_2"] = value
    return out


def reference(
    x, ab_w_in, ab_shift_mu, ab_w0, ab_w2, ab_a0, ab_a2, ab_g2, ab_k_k, ab_k_a, ab_r_k,
    ab_lnx_g, ab_lnx_b, ab_lam_q1, ab_lam_k1, ab_lam_q2, ab_lam_k2, ab_subln_g, ab_w_out,
    c_w_in, c_b_in, c_ln_g, c_ln_b, c_w_s, c_b_s, c_w_out, ln1_g, ln1_b, ffn_w_up, ffn_conv_w,
    ffn_conv_b, ffn_w_down, ln2_g, ln2_b, c_2, ctx_2, c_ctx_2, w_mod_2, b_mod_2, norm1_g_2,
    norm2_g_2, w_in_2, q_norm_g_2, k_norm_g_2, attn_sink_2, hgrn_lb_logits_2, hgrn_norm_g_2,
    w_branch_2, w_out_2, w_ff1_2, w_ff2_2,
):
    x = first_block(
        x, ab_w_in, ab_shift_mu, ab_w0, ab_w2, ab_a0, ab_a2, ab_g2, ab_k_k, ab_k_a, ab_r_k,
        ab_lnx_g, ab_lnx_b, ab_lam_q1, ab_lam_k1, ab_lam_q2, ab_lam_k2, ab_subln_g, ab_w_out,
        c_w_in, c_b_in, c_ln_g, c_ln_b, c_w_s, c_b_s, c_w_out, ln1_g, ln1_b, ffn_w_up,
        ffn_conv_w, ffn_conv_b, ffn_w_down, ln2_g, ln2_b,
    )
    return second_block(
        x, c_2, ctx_2, c_ctx_2, w_mod_2, b_mod_2, norm1_g_2, norm2_g_2, w_in_2, q_norm_g_2,
        k_norm_g_2, attn_sink_2, hgrn_lb_logits_2, hgrn_norm_g_2, w_branch_2, w_out_2, w_ff1_2,
        w_ff2_2,
    )


_drawn_inputs = setup_inputs


def setup_inputs(seed=0):
    import zlib

    import numpy as np

    out = dict(_drawn_inputs(seed))
    spreads = {}
    factors = {'ab_w2': 8.0,
     'ab_k_k': 8.0,
     'ab_k_a': 7.64,
     'ab_lnx_g': 7.168,
     'ab_lnx_b': 8.0,
     'ab_lam_q1': 4.671,
     'ab_lam_k1': 7.075,
     'ab_lam_q2': 4.602,
     'ab_lam_k2': 6.369,
     'ab_subln_g': 5.317,
     'c_b_in': 8.0,
     'c_ln_g': 6.485,
     'c_ln_b': 8.0,
     'c_b_s': 4.903,
     'ln1_b': 3.574,
     'ffn_conv_b': 8.0,
     'ln2_b': 3.637,
     'ctx_2': 3.973,
     'norm1_g_2': 8.0,
     'norm2_g_2': 4.62,
     'q_norm_g_2': 8.0,
     'k_norm_g_2': 8.0,
     'attn_sink_2': 8.0,
     'hgrn_lb_logits_2': 8.0,
     'hgrn_norm_g_2': 8.0}
    for name, (base, spread) in spreads.items():
        noise = np.random.default_rng([zlib.crc32(name.encode()), seed]).standard_normal(out[name].shape)
        drawn = base * np.exp(spread * noise) if base else spread * noise
        out[name] = __import__('jax').numpy.asarray(drawn.astype(out[name].dtype))
    for name, factor in factors.items():
        out[name] = (out[name] * factor).astype(out[name].dtype)
    return out
```

```python
from contextlib import ExitStack

import concourse.bass as bass
from concourse import mybir

F32 = mybir.dt.float32
U8 = mybir.dt.uint8
ALU = mybir.AluOpType
ACT = mybir.ActivationFunctionType
AXX = mybir.AxisListType.X

P = 128
D = 1024
KD = D // P
T = 256
HD = 64
DFF = 2816
NFF = DFF // P
DFF2 = 4096
RWKV_TILES, AB_TILES = 14, 26
STATE_BLOCKS = 7
IN2_TILES = 30
GATE0 = IN2_TILES * P
DEEPNORM = (2 * 2) ** 0.25
LAM_INIT = 0.2
SCALE = HD ** -0.5
EXP_MINUS_HALF = 0.6065306597126334
LN_FLOOR = -69.07755278982137
LN_SMALL = 1e-15
LN_LN_SMALL = -34.538776394910684
LEVELS = 7

CHUNKS = ((2, 3, 0), (3, 2, 1))
ENTERS = ({3: 0, 0: 1, 1: 2}, {2: 0, 1: 1, 0: 2})
MOD_BLOCKS = 6 * D // 256
LVL_BASE = (0, 4 * (2 * LEVELS + 1))
RING, BLK = 4, 256
NBANK = 4

PARAMS = [("mu", 14), ("w0", 4), ("a0", 4), ("k_k", 4), ("k_a", 4), ("r_k", 4), ("lnx_g", 4), ("lnx_b", 4),
          ("lam_q", 2), ("lam_k", 2), ("subln_g", 1), ("c_b_in", 16), ("c_ln_g", 8), ("c_ln_b", 8),
          ("ln1_g", 16), ("ln1_b", 16), ("ln2_g", 16), ("ln2_b", 16), ("conv_w", 6 * NFF), ("conv_b", 2 * NFF),
          ("cond", 16), ("b_mod", 96), ("norm1_g", 16), ("norm2_g", 16), ("q_norm", 2), ("k_norm", 2),
          ("sink", 16), ("lb", 16), ("hgrn_g", 2), ("eps5", 1), ("eps6", 1), ("eps_gn", 1), ("one", 1), ("half", 2)]
PCOL, NPAR = {}, 0
for _name, _n in PARAMS:
    PCOL[_name] = NPAR
    NPAR += _n

CONSTS = [("ident", 128), ("ones", 128), ("block64", 128), ("rope_a", 128), ("rope_b", 128), ("dup", 256),
          ("cos_a", 256), ("sin_a", 256), ("cos_b", 256), ("sin_b", 256), ("reset", 512),
          ("causal", 512), ("window", 512), ("dft_d", 256), ("dft_t", 1024)]
CCOL, NCONST = {}, 0
for _name, _n in CONSTS:
    CCOL[_name] = NCONST
    NCONST += _n
MASKS = [("rwkv", 512), ("fwd", LEVELS * 128), ("bwd", LEVELS * 128), ("diag", 128)]
MCOL, NMASK = {}, 0
for _name, _n in MASKS:
    MCOL[_name] = NMASK
    NMASK += _n


class Gemm:

    def __init__(self, w, blocks, col, n, groups=((0, 8),), nf=2, width=None):
        self.w, self.blocks, self.col, self.n, self.groups, self.nf = w, blocks, col, n, groups, nf
        self.width = width or nf * P
        self.g = len(groups)
        self.unroll = 1
        while self.unroll * self.g % RING or self.unroll * nf % NBANK:
            self.unroll += 1


def plan(gemms):
    chunk = step = tile = 0
    ends = []
    for g in gemms:
        g.chunk0, g.step0, g.tile0 = chunk, step, tile
        for _ in range(g.blocks * g.g):
            step += g.nf
            ends.append(step)
        chunk += g.blocks * g.g
        tile += g.blocks * g.nf
    return ends


class Waits:

    def __init__(self):
        self.seen = {}

    def __call__(self, name, n=1):
        self.seen[name] = self.seen.get(name, 0) + n
        return self.seen[name]


class Steps:

    def __init__(self):
        self.n = 0

    def one(self):
        self.n += 1
        return 1


SEMS = """
x_landed par_landed const_landed mask_landed lora_landed ws_landed ctx_landed out_landed
gemm_step tile_free vbank_full vbank_free abank_full abank_free vec_chain act_chain pool_chain
cond_silu lb_shifted lb_exp lb_floored lb_ln lam_prod lam_exp pad_zero
rope_ready scores_ready exp_ready attn_ready o_squares o_rstd yd_ready
masks_ready inv_first four_done xs_ready xs_pool hats_act h_pool lora_in decay_ready a_ready g_out log_ready exp_factors kk_squares kk_root hats_ready pr_zero inv_init
gn_sq gn_rstd bonus_in yr_ready centered squared rstd_ready x_ready
conv_ready silu_ready hid_ready v_ready mix_in
xsq_ready xrstd_ready h_ready n_squares n_rstd qk_ready qz_ready w_scores w_exp w_probs vz_zero
sp_first sp_sum sp_second k_raw dir_done tot_ready e_tot lf_ready ks_diff ks_exp ks_ready st_ready
lvl_diff lvl_exp lvl_ready qi_diff qi_exp qi_ready q_silu o_sq o_rs hgrn_done
merge_used ff_ready xo_ready
""".split()


def build(nc, xT, ctxT, par, cst, msk, lora, wsT, bsr, ab_w_in, ab_w_out, c_w_in, c_w_out, ffn_up, ffn_down,
          w_mod, w_in2, w_branch, w_out2, w_ff1, w_ff2, out):
    down_groups = ((0, 8), (8, 8), (16, 6))
    G = {}
    G["ab_in"] = Gemm(ab_w_in[0], 13, lambda b, u: b * BLK, T)
    G["ab_out"] = Gemm(ab_w_out[0], 4, lambda b, u: b * BLK, T)

    def up_col(b, u):
        return (b - u) * (BLK // 2) + (u // 2) * BLK + (u % 2) * DFF

    order = ["ab_in", ("mod", 0), "ab_out"]
    for l in range(2):
        G["up", l] = Gemm(ffn_up[l], 22, up_col, T)
        G["down", l] = Gemm(ffn_down[l], 4, lambda b, u: b * BLK, T, down_groups)
    G["c_in"] = Gemm(c_w_in[0], 8, lambda b, u: b * BLK, T)
    G["c_out"] = Gemm(c_w_out[0], 4, lambda b, u: b * BLK, T)
    order += [("up", 0), ("down", 0), "c_in", "c_out", ("up", 1), ("down", 1)]
    for l in range(2):
        full = 2 * T if l == 0 else T
        G["mod", l] = Gemm(w_mod[l], MOD_BLOCKS, lambda b, u: b * BLK, BLK, nf=1, width=BLK)
        G["in_state", l] = Gemm(w_in2[l], STATE_BLOCKS, lambda b, u: b * BLK, 2 * T)
        G["in_rest", l] = Gemm(w_in2[l], 15 - STATE_BLOCKS, lambda b, u: (b + STATE_BLOCKS) * BLK, full)
        order += [("in_state", l), ("in_rest", l)] + [("mod", 1)] * (l == 0)
        for n in range(3):
            for half in range(2):
                G["gate", l, n, half] = Gemm(
                    w_in2[l], 2, lambda b, u, c=GATE0 + n * D + half * 512: c + b * BLK, full)
                G["proj", l, n, half] = Gemm(
                    w_branch[l, n], 1, lambda b, u, c=half * 512: c, full, ((0, 4),), 4)
                order += [("gate", l, n, half), ("proj", l, n, half)]
        G["out2", l] = Gemm(w_out2[l], 4, lambda b, u: b * BLK, full)
        G["ff1", l] = Gemm(w_ff1[l], 16, lambda b, u: b * BLK, full)
        G["ff2", l] = Gemm(w_ff2[l], 4, lambda b, u: b * BLK, full, ((0, 8), (8, 8), (16, 8), (24, 8)))
        order += [("out2", l), ("ff1", l), ("ff2", l)]
    chunk_end = plan([G[o] for o in order])

    with ExitStack() as ctx:
        def sb(name, shape, dt=F32):
            return ctx.enter_context(nc.sbuf_tensor(name, shape, dt))

        ring = sb("ring", [P, RING, 8 * BLK])
        X = sb("X", [P, KD, 2 * T])
        arena = sb("arena", [P, 32768])
        prm = sb("prm", [P, NPAR])
        con = sb("con", [P, NCONST])
        mk = sb("mk", [P, NMASK], U8)
        sm = sb("sm", [P, 512])
        mod_row = sb("mod_row", [2, 2, BLK])
        bank = [ctx.enter_context(nc.psum_tensor(f"bank{i}", [P, 512], F32)) for i in range(NBANK)]
        vbank = [ctx.enter_context(nc.psum_tensor(f"vbank{i}", [P, 512], F32)) for i in range(2)]
        abank = [ctx.enter_context(nc.psum_tensor(f"abank{i}", [P, 512], F32)) for i in range(2)]
        S = {n: ctx.enter_context(nc.semaphore(n)) for n in SEMS}
        landed = [ctx.enter_context(nc.semaphore(f"slot_landed{i}")) for i in range(RING)]
        block = ctx.enter_context(nc.Block())

        def ar(off, *shape):
            n = 1
            for s in shape:
                n *= s
            v = arena[:, off:off + n]
            if len(shape) == 1:
                return v
            names = "abcde"[:len(shape)]
            return v.rearrange(f"p ({' '.join(names)}) -> p {' '.join(names)}",
                               **{c: s for c, s in zip(names, shape)})

        def pcol(name, i=0, n=1):
            return prm[:, PCOL[name] + i:PCOL[name] + i + n]

        def cc(name, *shape):
            n = dict(CONSTS)[name]
            v = con[:, CCOL[name]:CCOL[name] + n]
            if shape:
                names = "abcd"[:len(shape)]
                v = v.rearrange(f"p ({' '.join(names)}) -> p {' '.join(names)}", **{c: s for c, s in zip(names, shape)})
            return v

        def mask(name, i=0, n=128):
            return mk[:, MCOL[name] + i * 128:MCOL[name] + i * 128 + n]

        def rep(ap, n):
            return ap.unsqueeze(1).to_broadcast([P, n, ap.shape[-1]])

        ident, ones, block64 = cc("ident"), cc("ones"), cc("block64")

        PRJ = ar(0, AB_TILES, T + 1)
        PR = ar(0, 16, 4, P)
        XS = ar(8192, RWKV_TILES, T)
        DT = ar(11776, RWKV_TILES, T)
        GG, BH, KH = ar(11776, 4, T), ar(12800, 4, T), ar(13824, 4, T)
        TW, SG = ar(14848, T), ar(15104, T)
        LD, AA, LL, LP = (ar(15360 + 1024 * i, 4, T) for i in range(4))
        E1, E2, E3, KK = (ar(19456 + 1024 * i, 4, T) for i in range(4))
        KSQ, BON = ar(23552, 4, T), ar(15360, 4, T)
        XI, YI, T1 = (ar(15360 + 2048 * i, 16, P) for i in range(3))
        RH, UU, SB = ar(21504, 512), ar(22016, 2, 512), ar(23040, 4, P)
        AR = ar(23552, 8, 2, P)
        BZ, KZ = ar(25600, 4, 2, T), ar(27648, 4, 2, T)
        WL = ar(27648, 3, 512)
        VT, BT, KT = ar(29696, 2, 512), ar(30720, 512), ar(31232, 512)
        YT, YF = ar(25600, 2, 512), ar(26624, 4, T)
        GSQ, GRS = ar(27648, 4, T), ar(28672, 4, T)
        MKF = ar(20480, NMASK)
        QZ1, KR1, R2, R3 = ar(15360, 4, 2, T), ar(17408, 4, T), ar(18432, 2, T), ar(18944, 2, T)
        VT1 = ar(19456, 2, 4, P)
        SM1, EE1, AT1 = ar(20480, 2, 2, T), ar(21504, 2, 2, T), ar(22528, 2, T)
        PT1, OO1, OSQ, ORS = ar(23552, 2, 2, T), ar(24576, 4, T), ar(25600, 4, T), ar(26624, 4, T)
        YAB = X[:, :, T:2 * T]
        Z, ZSQ, ZRS = ar(0, KD, T), ar(2048, KD, T), ar(4096, T)
        HF = ar(8192, NFF, T)
        GP = ar(14336, 4, T + 2)
        CV, VAL = ar(15872, 4, T), ar(16896, 4, T)
        UV = ar(8192, 16, T)
        WS, BS = ar(20480, 8, P), ar(21504, 1024)
        VTC, MU = ar(14336, 2, 1024), ar(18432, 8, T)
        P2 = ar(0, IN2_TILES, 2 * T)
        SCR = 15360
        HB = ar(28672, KD, 2 * T)
        XSQ = ar(24576, KD, 2 * T)
        XRS = ar(23552, 2 * T)
        QZ2, KD2, VZ = ar(SCR, 4, 2, 2 * T), ar(SCR + 4096, 2, 2 * T), ar(SCR + 5120, 4, 2, 2, P)
        SM2, EE2 = ar(SCR + 7168, 2, 2 * T), ar(SCR + 8192, 2, 2 * T)
        PT2 = ar(SCR + 9216, 4, 4, P)
        NSQ, NRS = ar(SCR + 7168, 5, 2 * T), ar(SCR + 10240, 5, 2 * T)
        RT = ar(SCR, 2, T)
        FB = ar(SCR + 11264, 2, 2, 2, P)
        LF = ar(SCR, 8, 2 * T)
        TA, TB, TC, TD = (ar(SCR + 4096 + 2048 * i, 4, 2 * T) for i in range(4))
        VTK = ar(SCR + 4096, 4, 4, P)
        KST = ar(SCR + 6144, 2, 3, 4, P)
        KSF = ar(SCR + 9216, 4, 2 * T)
        LDF, LQE, LKE = (ar(SCR + 9216 + 1024 * i, 2, 2 * T) for i in range(3))
        ATT = ar(SCR + 12288, 2, 4, P)
        QI = ar(SCR + 6144, 2, 2, 2 * T)
        HSQ, HRS = ar(SCR + 9216, 4, 2 * T), ar(SCR + 6144, 4, 2 * T)
        ACC = ar(SCR, KD, 2 * T)
        GB, PB = ar(SCR + 4096, 2, 4, 2 * T), ar(SCR + 8192, 2, 4, 2 * T)
        HF2 = ar(0, DFF2 // P, 2 * T)
        STATE = ar(0, 2, 3, 4, P)

        MOD = [sm[:, 96 * l:96 * l + 96].rearrange("p (a b) -> p a b", b=2) for l in range(2)]
        SC = [sm[:, 192 + 16 * i:208 + 16 * i].rearrange("p (a b) -> p a b", b=2) for i in range(4)]
        CS = sm[:, 256:272]
        LAMP, NLAM, OMKA = sm[:, 272:274], sm[:, 275:276], sm[:, 276:280]
        LAME, G08, LAME2 = sm[:, 280:282], sm[:, 282:283], sm[:, 440:442]
        GMS = sm[:, 442:450]
        EGM, FST = sm[:, 284:292], sm[:, 292:296]
        MX, NM, SU = sm[:, 296:300], sm[:, 300:304], sm[:, 304:308]
        ES = sm[:, 308:312]
        TOT, ETOT = sm[:, 312:344], sm[:, 344:376]
        LB, OMLB, LLB, LBT = (sm[:, 376 + 16 * i:392 + 16 * i] for i in range(4))

        def rows(w, k0, nk, c0, n):
            v = w.rearrange("(k p) f -> p k f", p=P)
            return v[:, k0:k0 + nk, bass.ds(c0, n)]

        def each_block(eng, g, emit, peel):
            rounds = g.blocks // g.unroll
            first = min(peel, rounds)
            for i in range(first):
                for u in range(g.unroll):
                    emit(i, u)
            if rounds - first >= 2:
                with eng.Fori(first, rounds, 1) as i:
                    for u in range(g.unroll):
                        emit(i, u)
            else:
                for i in range(first, rounds):
                    for u in range(g.unroll):
                        emit(i, u)
            for u in range(g.blocks - rounds * g.unroll):
                emit(rounds, u)

        @block.sync
        def _(sp):
            def stream(g):
                per_round = g.unroll * g.g

                def emit(i, u):
                    for n, (k0, nk) in enumerate(g.groups):
                        c = g.chunk0 + u * g.g + n
                        slot = c % RING
                        if isinstance(i, int):
                            cc_ = c + i * per_round
                            if cc_ >= RING:
                                sp.wait_ge(S["gemm_step"], chunk_end[cc_ - RING])
                        else:
                            done = g.step0 + (c - RING - g.chunk0 + 1) * g.nf
                            sp.wait_ge(S["gemm_step"], i * (per_round * g.nf) + done)
                        width = g.width
                        col = g.col(i * g.unroll + u, u)
                        dst = ring[:, slot, 0:nk * width].rearrange("p (k f) -> p k f", f=width)
                        sp.dma_start(dst, rows(g.w, k0, nk, col, width)).then_inc(landed[slot], 16)

                each_block(sp, g, emit, 1)

            for o in order:
                stream(G[o])
            w = Waits()
            sp.wait_ge(S["xo_ready"], w("xo_ready"))
            sp.dma_start(out.rearrange("(k p) t -> p k t", p=P), X[:, :, 0:T]).then_inc(S["out_landed"], 16)
            sp.wait_ge(S["out_landed"], 16)

        @block.tensor
        def _(pe):
            w = Waits()
            jobs = {"v": 0, "a": 0}

            def take(kind):
                n = jobs[kind]
                jobs[kind] += 1
                if n >= 2:
                    pe.wait_ge(S[kind + "bank_free"], n - 1)
                return (vbank if kind == "v" else abank)[n % 2]

            def post(kind, ins):
                ins.then_inc(S[kind + "bank_full"], 1)
                return jobs[kind]

            def gemm(key, act, wait_free=True):
                g = G[key]
                if wait_free and g.tile0:
                    pe.wait_ge(S["tile_free"], g.tile0)
                per_round = g.unroll * g.g

                def emit(i, u):
                    for n, (k0, nk) in enumerate(g.groups):
                        c = g.chunk0 + u * g.g + n
                        slot = c % RING
                        pe.wait_ge(landed[slot], i * (16 * per_round // RING) + 16 * (c // RING + 1))
                        for f in range(g.nf):
                            t = g.tile0 + u * g.nf + f
                            if n == 0 and (not isinstance(i, int) or t + i * g.unroll * g.nf >= NBANK):
                                pe.wait_ge(S["tile_free"], i * (g.unroll * g.nf) + t - NBANK + 1)
                            wt = ring[:, slot, 0:nk * g.nf * P].rearrange("p (k f) -> p k f", k=nk)
                            for k in range(nk):
                                mm = pe.matmul(bank[t % NBANK][:, 0:g.n], wt[:, k, f * P:(f + 1) * P],
                                               act(k0 + k), start=(n == 0 and k == 0),
                                               stop=(n == g.g - 1 and k == nk - 1))
                            mm.then_inc(S["gemm_step"], 1)

                each_block(pe, g, emit, 1 if g.tile0 == 0 else 0)

            def mod_fill(l, k):
                g = G["mod", l]
                if 2 <= k < g.blocks + 2:
                    pe.wait_ge(S["tile_free"], g.tile0 + k - 1)
                    b = take("v")
                    for i in range(2):
                        mm = pe.transpose(b[:, 2 * i:2 * i + 2], mod_row[:, k % 2, i * P:(i + 1) * P], ident[0:2, 0:2])
                    post("v", mm)
                if k < g.blocks:
                    c, t = g.chunk0 + k, g.tile0 + k
                    pe.wait_ge(landed[c % RING], 16 * (c // RING + 1))
                    pe.wait_ge(S["tile_free"], t - NBANK + 1)
                    wt = ring[:, c % RING, :].rearrange("p (k f) -> p k f", k=KD)
                    for i in range(KD):
                        mm = pe.matmul(bank[t % NBANK][0:2, 0:BLK], CS[:, 2 * i:2 * i + 2], wt[:, i, :],
                                       start=(i == 0), stop=(i == KD - 1))
                    mm.then_inc(S["gemm_step"], 1)

            def column_sum(kind, src, n, mat=ones):
                b = take(kind)
                for k in range(KD):
                    mm = pe.matmul(b[:, 0:n], mat, src(k), start=(k == 0), stop=(k == KD - 1))
                post(kind, mm)

            def one(kind, lhs, rhs, n):
                b = take(kind)
                post(kind, pe.matmul(b[:, 0:n], lhs, rhs, start=True, stop=True))

            def turn(kind, srcs):
                b = take(kind)
                for i, s in enumerate(srcs):
                    mm = pe.transpose(b[:, i * P:(i + 1) * P], s, ident)
                post(kind, mm)

            def layer_norm(z, key):
                pe.wait_ge(S["tile_free"], G[key].tile0 + G[key].blocks * G[key].nf)
                column_sum("v", z, T)
                pe.wait_ge(S["squared"], w("squared"))
                column_sum("a", lambda k: ZSQ[:, k, :], T)

            def rms(n):
                pe.wait_ge(S["xsq_ready"], w("xsq_ready"))
                column_sum("a", lambda k: XSQ[:, k, 0:n], n)

            pe.wait_ge(S["const_landed"], 16)
            pe.wait_ge(S["x_landed"], 16)
            gemm("ab_in", lambda k: X[:, k, 0:T])

            pe.wait_ge(S["cond_silu"], w("cond_silu"))

            pe.wait_ge(S["lam_prod"], w("lam_prod"))
            one("a", ones, LAMP, 2)
            pe.wait_ge(S["tile_free"], AB_TILES)
            for i in range(4):
                b = take("v")
                for j in range(2):
                    mm = pe.matmul(b[:, j * T:(j + 1) * T], cc("rope_a"), PRJ[:, 14 + 2 * i + j, 1:T + 1],
                                   start=True, stop=True)
                post("v", mm)
            for j in range(2):
                turn("a", [PRJ[:, 22 + h, 1 + j * P:1 + (j + 1) * P] for h in range(4)])
            pe.wait_ge(S["rope_ready"], w("rope_ready"))

            def score(u):
                h, qt = u // 2, u % 2
                b = take("v")
                for c in range(2):
                    mm = pe.matmul(b[:, c * T:(c + 1) * T], QZ1[:, h, c, qt * P:(qt + 1) * P], KR1[:, h, :],
                                   start=True, stop=True)
                post("v", mm)

            score(0)
            pe.wait_ge(S["abank_free"], jobs["a"])
            for u in range(8):
                h, qt = u // 2, u % 2
                if u < 7:
                    score(u + 1)
                mod_fill(0, u)
                pe.wait_ge(S["attn_ready"], w("attn_ready"))
                turn("a", [AT1[:, u % 2, k * P:(k + 1) * P] for k in range(2)])
                if qt == 1:
                    pe.wait_ge(S["abank_free"], jobs["a"])
                    b = take("v")
                    for k in range(2):
                        mm = pe.matmul(b[:, 0:T], VT1[:, k, h, :], PT1[:, h % 2, k, :], start=(k == 0), stop=(k == 1))
                    post("v", mm)
            pe.wait_ge(S["o_squares"], w("o_squares"))
            for i in range(2):
                one("a", ones, OSQ[:, 2 * i:2 * i + 2, :], 512)

            for k in range(8, 12):
                mod_fill(0, k)
            pe.wait_ge(S["lora_in"], w("lora_in", 2))
            pe.wait_ge(S["lora_landed"], 16)
            for i, src in ((0, TW), (1, XS[:, 12, :]), (2, SG)):
                for f in range(2):
                    b = take("a")
                    for j in range(2):
                        mm = pe.matmul(b[:, j * T:(j + 1) * T], WL[:, i, (2 * f + j) * P:(2 * f + j + 1) * P], src,
                                       start=True, stop=True)
                    post("a", mm)
            pe.wait_ge(S["kk_squares"], w("kk_squares"))
            for i in range(2):
                one("a", block64, KSQ[:, 2 * i:2 * i + 2, :], 512)
            for k in range(12, MOD_BLOCKS + 2):
                mod_fill(0, k)
            pe.wait_ge(S["hats_ready"], w("hats_ready"))
            for j in range(2):
                turn("a", [XS[:, 8 + t, j * P:(j + 1) * P] for t in range(4)])
            turn("a", [BH[:, t, 0:P] for t in range(4)])
            turn("a", [KH[:, t, 0:P] for t in range(4)])
            pe.wait_ge(S["pr_zero"], w("pr_zero"))
            for u in range(16):
                h, j = u // 2, u % 2
                t, par = h // 2, h % 2
                b = take("v")
                rhs = AR[:, 2 * t + j, :, :]
                pe.matmul(b[:, 0:256], BZ[:, t, par, j * P:(j + 1) * P], rhs, start=True, stop=True)
                post("v", pe.matmul(b[:, 256:512], KZ[:, t, par, j * P:(j + 1) * P], rhs, start=True, stop=True))
            pe.wait_ge(S["inv_init"], w("inv_init", 2))
            pe.wait_ge(S["vbank_free"], jobs["v"])
            y_in, t1_in = [0] * 4, [0] * 4
            for l in range(LEVELS):
                for q in range(4):
                    if l == 1:
                        pe.wait_ge(S["inv_first"], w("inv_first"))
                    elif l:
                        pe.wait_ge(S["vbank_free"], y_in[q])
                    b = take("v")
                    for i in range(4):
                        u = 4 * q + i
                        mm = pe.matmul(b[:, i * P:(i + 1) * P], PR[:, u, 0, :], XI[:, u, :], start=True, stop=True)
                    t1_in[q] = post("v", mm)
                for q in range(4 if l else 0):
                    pe.wait_ge(S["vbank_free"], t1_in[q])
                    if l < LEVELS - 1:
                        b = take("v")
                        for i in range(4):
                            u = 4 * q + i
                            mm = pe.matmul(b[:, i * P:(i + 1) * P], YI[:, u, :], T1[:, u, :], start=True, stop=True)
                        post("v", mm)
                    b = take("v")
                    for i in range(4):
                        u = 4 * q + i
                        mm = pe.matmul(b[:, i * P:(i + 1) * P], T1[:, u, :], YI[:, u, :], start=True, stop=True)
                    y_in[q] = post("v", mm)
            pe.wait_ge(S["vbank_free"], jobs["v"])
            pe.wait_ge(S["abank_free"], jobs["a"])

            def head(h):
                return slice(h * HD, (h + 1) * HD)

            def solve(j):
                b = take("a")
                for h in range(8):
                    mm = pe.matmul(b[:, head(h)], YI[:, 2 * h + j, :], RH[:, head(h)], start=True, stop=True)
                post("a", mm)

            def outputs(j):
                b = take("a")
                for t in range(4):
                    if j:
                        pe.matmul(b[:, t * P:(t + 1) * P], AR[:, 2 * t + 1, 1, :], SB[:, t, :],
                                  start=True, stop=False, skip_group_check=True)
                    for h in (2 * t, 2 * t + 1):
                        pe.matmul(b[:, head(h)], PR[:, 2 * h + j, 1, :], UU[:, j, head(h)],
                                  start=(j == 0), stop=False, skip_group_check=True)
                        mm = pe.matmul(b[:, head(h)], PR[:, 2 * h + j, 3, :], VT[:, j, head(h)],
                                       start=False, stop=True, skip_group_check=True)
                post("a", mm)

            b = take("a")
            for h in range(8):
                mm = pe.matmul(b[:, head(h)], PR[:, 2 * h, 2, :], VT[:, 0, head(h)], start=True, stop=True)
            post("a", mm)
            pe.wait_ge(S["abank_free"], jobs["a"])
            solve(0)
            pe.wait_ge(S["abank_free"], jobs["a"])
            b = take("v")
            for t in range(4):
                pe.matmul(b[:, t * P:(t + 1) * P], BT[:, t * P:(t + 1) * P], UU[:, 0, t * P:(t + 1) * P],
                          start=True, stop=False)
                mm = pe.matmul(b[:, t * P:(t + 1) * P], KT[:, t * P:(t + 1) * P], VT[:, 0, t * P:(t + 1) * P],
                               start=False, stop=True)
            post("v", mm)
            outputs(0)
            pe.wait_ge(S["vbank_free"], jobs["v"])
            b = take("a")
            for t in range(4):
                pe.matmul(b[:, t * P:(t + 1) * P], AR[:, 2 * t + 1, 0, :], SB[:, t, :],
                          start=True, stop=False, skip_group_check=True)
                for h in (2 * t, 2 * t + 1):
                    mm = pe.matmul(b[:, head(h)], PR[:, 2 * h + 1, 2, :], VT[:, 1, head(h)],
                                   start=False, stop=True, skip_group_check=True)
            post("a", mm)
            pe.wait_ge(S["abank_free"], jobs["a"])
            solve(1)
            pe.wait_ge(S["abank_free"], jobs["a"])
            outputs(1)
            pe.wait_ge(S["abank_free"], jobs["a"])
            for j in range(2):
                turn("a", [YT[:, j, t * P:(t + 1) * P] for t in range(4)])
            pe.wait_ge(S["abank_free"], jobs["a"])
            for i in range(2):
                one("v", block64, YF[:, 2 * i:2 * i + 2, :], 512)
            pe.wait_ge(S["gn_sq"], w("gn_sq"))
            for i in range(2):
                one("a", block64, GSQ[:, 2 * i:2 * i + 2, :], 512)
            pe.wait_ge(S["bonus_in"], w("bonus_in"))
            for i in range(2):
                one("v", block64, BON[:, 2 * i:2 * i + 2, :], 512)
            pe.wait_ge(S["yr_ready"], w("yr_ready"))
            pe.wait_ge(S["yd_ready"], w("yd_ready"))
            gemm("ab_out", lambda k: YAB[:, k, :])
            layer_norm(lambda k: Z[:, k, :], "ab_out")

            def ffn(l):
                pe.wait_ge(S["x_ready"], w("x_ready"))
                gemm(("up", l), lambda k: X[:, k, 0:T])
                pe.wait_ge(S["hid_ready"], w("hid_ready", NFF))
                gemm(("down", l), lambda k: HF[:, k, :])
                layer_norm(lambda k: Z[:, k, :], ("down", l))

            ffn(0)
            pe.wait_ge(S["x_ready"], w("x_ready"))
            gemm("c_in", lambda k: X[:, k, 0:T])
            layer_norm(lambda k: UV[:, 8 + k, :], "c_in")
            pe.wait_ge(S["v_ready"], w("v_ready"))
            for j in range(2):
                for q in range(2):
                    turn("a", [UV[:, 8 + 4 * q + g, j * P:(j + 1) * P] for g in range(4)])
            pe.wait_ge(S["mix_in"], w("mix_in"))
            pe.wait_ge(S["abank_free"], jobs["a"])
            for j in range(2):
                for q in range(2):
                    b = take("v")
                    for i in range(4):
                        g = 4 * q + i
                        pe.matmul(b[:, i * P:(i + 1) * P], ones[0:1, :], BS[0:1, g * P:(g + 1) * P],
                                  start=True, stop=False)
                        mm = pe.matmul(b[:, i * P:(i + 1) * P], VTC[:, j, g * P:(g + 1) * P], WS[:, g, :],
                                       start=False, stop=True)
                    post("v", mm)
            pe.wait_ge(S["vbank_free"], jobs["v"])
            gemm("c_out", lambda k: MU[:, k, :])
            layer_norm(lambda k: Z[:, k, :], "c_out")
            ffn(1)

            for l in range(2):
                last = l == 1
                n = T if last else 2 * T
                rms(2 * T)
                pe.wait_ge(S["h_ready"], w("h_ready"))
                gemm(("in_state", l), lambda k: HB[:, k, :])
                gemm(("in_rest", l), lambda k, n=n: HB[:, k, 0:n])
                pe.wait_ge(S["tile_free"], G["in_rest", l].tile0 + 2 * G["in_rest", l].blocks)

                pe.wait_ge(S["n_squares"], w("n_squares", 2))
                for i in range(5):
                    m = n if i < 4 else 2 * T
                    one("a", block64, NSQ[:, i, 0:m], m)
                pe.wait_ge(S["qk_ready"], w("qk_ready"))
                for i in range(5):
                    one("v", cc("rope_b"), P2[:, (14 + i) if i < 4 else 0, 0:T], T)
                turn("v", [P2[:, 1, c * P:(c + 1) * P] for c in range(4)])
                pe.wait_ge(S["qz_ready"], w("qz_ready"))
                for kv in range(2):
                    one("a", cc("dup", 2, P)[:, kv, :], P2[:, 0, :], 2 * T)
                pe.wait_ge(S["abank_free"], jobs["a"])
                pe.wait_ge(S["vbank_free"], jobs["v"])
                units = [(s, t, q, h) for s in range(2 if not last else 1) for t in range(4) for q in range(2)
                         for h in range(2)]

                def wscore(s, t, q, h):
                    kv = t // 2
                    lhs = QZ2[:, t, h, s * T + q * P:s * T + (q + 1) * P]
                    if s == 0:
                        one("v", lhs, KD2[:, kv, :], 2 * T)
                    else:
                        one("v", lhs, KD2[:, kv, T:2 * T], T)

                wscore(*units[0])
                for i, (s, t, q, h) in enumerate(units):
                    if i + 1 < len(units):
                        wscore(*units[i + 1])
                    if l == 0 and i < MOD_BLOCKS + 2:
                        mod_fill(1, i)
                    pe.wait_ge(S["w_probs"], w("w_probs"))
                    nk = 4 if s == 0 else 2
                    turn("a", [EE2[:, i % 2, k * P:(k + 1) * P] for k in range(nk)])
                    if h == 1:
                        pe.wait_ge(S["abank_free"], jobs["a"])
                        b = take("v")
                        for hh in range(2):
                            for k in range(nk):
                                c = k + (4 - nk)
                                mm = pe.matmul(b[:, 0:P], VZ[:, c, t // 2, hh, :], PT2[:, (i - 1 + hh) % 4, k, :],
                                               start=(hh == 0 and k == 0), stop=(hh == 1 and k == nk - 1))
                        post("v", mm)

                for s in range(1 if last else 2):
                    for g in range(4):
                        b = take("a")
                        for j in range(2):
                            c0 = s * T + j * P
                            mm = pe.matmul(b[:, j * T:(j + 1) * T], P2[:, 26 + g, c0:c0 + P], cc("dft_d"),
                                           start=True, stop=True)
                        post("a", mm)
                        pe.wait_ge(S["abank_free"], jobs["a"])
                        i = (s * 4 + g) % 2
                        b = take("v")
                        for j in range(2):
                            for m in range(2):
                                mm = pe.matmul(b[:, 0:T], FB[:, i, j, m, :], cc("dft_t", 2, 2, T)[:, j, m, :],
                                               start=(j == 0 and m == 0), stop=(j == 1 and m == 1))
                        post("v", mm)

                pe.wait_ge(S["lf_ready"], w("lf_ready"))
                for c in range(4):
                    turn("a", [P2[:, 2 + h, c * P:(c + 1) * P] for h in range(4)])
                for d in range(2):
                    pe.wait_ge(S["ks_ready"], w("ks_ready"))
                    for c in CHUNKS[d]:
                        turn("a", [KSF[:, h, c * P:(c + 1) * P] for h in range(4)])
                pe.wait_ge(S["abank_free"], jobs["a"])
                for st in range(3):
                    for d in range(2):
                        b = take("v")
                        for h in range(4):
                            mm = pe.matmul(b[:, h * P:(h + 1) * P], KST[:, d, st, h, :],
                                           VTK[:, CHUNKS[d][st], h, :], start=True, stop=True)
                        post("v", mm)
                nc_ = n // P
                for h in range(4):
                    for i in range(2 * LEVELS + 1):
                        pe.wait_ge(S["lvl_ready"], w("lvl_ready"))
                        b = take("v")
                        for c in range(nc_):
                            tok = slice(c * P, (c + 1) * P)
                            rhs = LQE[:, i % 2, tok] if i < 2 * LEVELS else P2[:, 18 + h, tok]
                            mm = pe.matmul(b[:, tok], LKE[:, i % 2, tok], rhs, start=True, stop=True)
                        post("v", mm)
                    pe.wait_ge(S["vbank_free"], jobs["v"])
                    pe.wait_ge(S["qi_ready"], w("qi_ready"))
                    b = take("a")
                    for c in range(nc_):
                        tok = slice(c * P, (c + 1) * P)
                        mm = pe.matmul(b[:, tok], VTK[:, c, h, :], ATT[:, h % 2, c, :], start=True, stop=False)
                        for d in range(2):
                            st = ENTERS[d].get(c)
                            if st is not None:
                                lastd = d == 1 or ENTERS[1].get(c) is None
                                mm = pe.matmul(b[:, tok], STATE[:, d, st, h, :], QI[:, h % 2, d, tok],
                                               start=False, stop=lastd)
                    post("a", mm)
                pe.wait_ge(S["o_sq"], w("o_sq"))
                for h in range(4):
                    one("a", ones, HSQ[:, h, 0:n], n)
                pe.wait_ge(S["hgrn_done"], w("hgrn_done"))

                for br in range(3):
                    src = (26, 14, 18)[br]
                    for half in range(2):
                        gemm(("gate", l, br, half), lambda k, n=n: HB[:, k, 0:n], wait_free=br + half == 0)
                        gemm(("proj", l, br, half), lambda k, n=n, src=src: P2[:, src + k, 0:n], wait_free=False)
                pe.wait_ge(S["merge_used"], w("merge_used", 6))
                gemm(("out2", l), lambda k, n=n: ACC[:, k, 0:n])
                rms(n)
                pe.wait_ge(S["h_ready"], w("h_ready"))
                gemm(("ff1", l), lambda k, n=n: HB[:, k, 0:n])
                pe.wait_ge(S["ff_ready"], w("ff_ready", DFF2 // P))
                gemm(("ff2", l), lambda k, n=n: HF2[:, k, 0:n])

        class Reader:

            def __init__(self, eng, banks):
                self.eng, self.banks, self.n = eng, banks, 0

            def take(self):
                self.n += 1
                return self.n

            def bank(self):
                return self.banks[(self.n - 1) % 2]

            def tiles(self, key, read):
                g = G[key]
                for b in range(g.blocks):
                    for f in range(g.nf):
                        self.eng.wait_ge(S["gemm_step"], g.step0 + (b * g.g + g.g - 1) * g.nf + f + 1)
                        k = b * g.nf + f
                        read(k, bank[(g.tile0 + k) % NBANK]).then_inc(S["tile_free"], 1)

            def tiles_read(self, key, n=None):
                g = G[key]
                self.eng.wait_ge(S["tile_free"], g.tile0 + (g.blocks * g.nf if n is None else n))

        @block.scalar
        def _(act):
            w = Waits()
            st = Steps()
            rd = Reader(act, abank)

            def fn(out_, in_, f, **kw):
                return act.activation(out_, in_, f, **kw)

            def copy_bank(out_, n=512, shape=None):
                act.wait_ge(S["abank_full"], rd.take())
                b = rd.bank()[:, 0:n]
                if shape:
                    b = b.rearrange(shape[0], **shape[1])
                fn(out_, b, ACT.Copy).then_inc(S["abank_free"], 1)

            def rstd_of(out_, n, scale, eps):
                act.wait_ge(S["abank_full"], rd.take())
                fn(out_, rd.bank()[:, 0:n], ACT.Ln, scale=scale, bias=pcol(eps)).then_inc(S["abank_free"], 1)

            def layer_norm(z):
                act.wait_ge(S["centered"], w("centered"))
                fn(ZSQ[:, :, :], z, ACT.Square).then_inc(S["squared"], 1)
                rstd_of(ZRS, T, 1.0 / D, "eps5")
                act.wait_ge(S["abank_free"], rd.n)
                fn(ZRS, ZRS, ACT.Exp, scale=-0.5).then_inc(S["rstd_ready"], 1)

            act.dma_start(con[:, :], cst).then_inc(S["const_landed"], 16)
            act.dma_start(X[:, :, 0:T], xT.rearrange("(k p) t -> p k t", p=P)).then_inc(S["x_landed"], 16)
            act.dma_start(WL, lora.rearrange("i p n -> p i n")).then_inc(S["lora_landed"], 16)
            act.wait_ge(S["par_landed"], 16)
            fn(CS, pcol("cond", 0, 16), ACT.Silu).then_inc(S["cond_silu"], 1)
            act.wait_ge(S["lb_shifted"], w("lb_shifted"))
            fn(LB, LB, ACT.Exp).then_inc(S["lb_exp"], 1)
            act.wait_ge(S["lb_floored"], w("lb_floored"))
            fn(LLB, LBT, ACT.Ln).then_inc(S["lb_ln"], 1)

            rd.tiles("ab_in", lambda k, b: fn(PRJ[:, k, 1:T + 1], b[:, 0:T], ACT.Copy))

            act.wait_ge(S["abank_full"], rd.take())
            fn(LAME, rd.bank()[:, 0:2], ACT.Exp).then_inc(S["abank_free"], 1)
            act.wait_ge(S["abank_free"], rd.n)
            fn(LAME2, LAME, ACT.Copy).then_inc(S["lam_exp"], 1)
            for j in range(2):
                copy_bank(VT1[:, j, :, :].rearrange("p a b -> p (a b)"))

            def exps(u):
                act.wait_ge(S["scores_ready"], w("scores_ready"))
                for c in range(2):
                    i = 2 * (u % 2) + c
                    ins = fn(EE1[:, u % 2, c, :], SM1[:, u % 2, c, :], ACT.Exp, scale=SCALE, bias=NM[:, i:i + 1],
                             accum_out=SU[:, i:i + 1])
                    ins.then_inc(S["exp_ready"], 1)

            exps(0)
            for u in range(8):
                if u < 7:
                    exps(u + 1)
                h, qt = u // 2, u % 2
                copy_bank(PT1[:, h % 2, :, qt * P:(qt + 1) * P], 2 * P, ("p (a b) -> p a b", dict(a=2)))
            for i in range(2):
                rstd_of(ORS[:, 2 * i:2 * i + 2, :].rearrange("p a b -> p (a b)"), 512, 1.0 / P, "eps5")
            act.wait_ge(S["abank_free"], rd.n)
            fn(ORS[:, :, :], ORS[:, :, :], ACT.Exp, scale=-0.5).then_inc(S["o_rstd"], 1)

            act.wait_ge(S["xs_ready"], w("xs_ready"))
            fn(TW, XS[:, 12, :], ACT.Tanh).then_inc(S["lora_in"], 1)
            fn(SG, XS[:, 13, :], ACT.Sigmoid).then_inc(S["lora_in"], 1)
            for dst, name, said in ((LD, "w0", "decay_ready"), (AA, "a0", "a_ready"), (GG, None, "g_out")):
                for f in range(2):
                    act.wait_ge(S["abank_full"], rd.take())
                    b = rd.bank()
                    if name is None:
                        fn(dst[:, 2 * f:2 * f + 2, :].rearrange("p a b -> p (a b)"), b[:, :], ACT.Copy)\
                            .then_inc(S["abank_free"], 1)
                        continue
                    fn(dst[:, 2 * f, :], b[:, 0:T], ACT.Sigmoid, bias=pcol(name, 2 * f))\
                        .then_inc(S["act_chain"], st.one())
                    fn(dst[:, 2 * f + 1, :], b[:, T:2 * T], ACT.Sigmoid, bias=pcol(name, 2 * f + 1))\
                        .then_inc(S["abank_free"], 1)
                act.wait_ge(S["act_chain"], st.n)
                act.wait_ge(S["abank_free"], rd.n)
                act.sem_inc(S[said], 1)
            for i in range(2):
                act.wait_ge(S["abank_full"], rd.take())
                fn(E1[:, 2 * i:2 * i + 2, :].rearrange("p a b -> p (a b)"), rd.bank()[:, :], ACT.Sqrt)\
                    .then_inc(S["abank_free"], 1)
            act.wait_ge(S["abank_free"], rd.n)
            act.sem_inc(S["kk_root"], 1)
            act.wait_ge(S["log_ready"], w("log_ready"))
            fn(E1, LL, ACT.Exp).then_inc(S["act_chain"], st.one())
            fn(E2, LL, ACT.Exp, scale=-1.0).then_inc(S["act_chain"], st.one())
            fn(E3, LP, ACT.Exp).then_inc(S["act_chain"], st.one())
            fn(EGM, GMS, ACT.Exp).then_inc(S["act_chain"], st.one())
            act.wait_ge(S["act_chain"], st.n)
            act.sem_inc(S["exp_factors"], 1)
            act.wait_ge(S["hats_act"], w("hats_act"))
            for dst in (VT[:, 0, :], VT[:, 1, :], BT, KT):
                copy_bank(dst)
            for dst in (RH, UU[:, 0, :], YT[:, 0, :], RH, UU[:, 1, :], YT[:, 1, :]):
                copy_bank(dst)
            for j in range(2):
                copy_bank(YF[:, :, j * P:(j + 1) * P], 512, ("p (a b) -> p a b", dict(a=4)))
            act.wait_ge(S["gn_sq"], w("gn_sq"))
            for i in range(2):
                rstd_of(GRS[:, 2 * i:2 * i + 2, :].rearrange("p a b -> p (a b)"), 512, 1.0 / HD, "eps_gn")
            act.wait_ge(S["abank_free"], rd.n)
            fn(GRS, GRS, ACT.Exp, scale=-0.5).then_inc(S["gn_rstd"], 1)
            layer_norm(Z)

            def ffn(l):
                g = G["up", l]

                def tile_in(k, dst):
                    act.wait_ge(S["gemm_step"], g.step0 + k + 1)
                    fn(dst, bank[(g.tile0 + k) % NBANK][:, 0:T], ACT.Copy).then_inc(S["tile_free"], 1)

                for pair in range(NFF // 2):
                    for f in range(2):
                        tile_in(4 * pair + f, GP[:, (2 * pair + f) % 4, 2:T + 2])
                    for f in range(2):
                        if pair >= 2:
                            act.wait_ge(S["hid_ready"], w("hid_ready"))
                        tile_in(4 * pair + 2 + f, VAL[:, (2 * pair + f) % 4, :])
                    for f in range(2):
                        act.wait_ge(S["conv_ready"], w("conv_ready"))
                        c = CV[:, (2 * pair + f) % 4, :]
                        fn(c, c, ACT.Silu).then_inc(S["silu_ready"], 1)
                act.wait_ge(S["hid_ready"], w("hid_ready", 4))
                layer_norm(Z)

            ffn(0)
            rd.tiles("c_in", lambda k, b: fn(UV[:, k, :], b[:, 0:T], ACT.Gelu, bias=pcol("c_b_in", k)))
            layer_norm(UV[:, 8:16, :])
            for j in range(2):
                for q in range(2):
                    copy_bank(VTC[:, j, q * 512:(q + 1) * 512])
            layer_norm(Z)
            ffn(1)

            act.wait_ge(S["ctx_landed"], 16)
            act.wait_ge(S["x_ready"], w("x_ready", 4))
            for l in range(2):
                last = l == 1
                n = T if last else 2 * T

                def rms(m):
                    fn(XSQ[:, :, 0:m], X[:, :, 0:m], ACT.Square).then_inc(S["xsq_ready"], 1)
                    rstd_of(XRS[:, 0:m], m, 1.0 / D, "eps6")
                    act.wait_ge(S["abank_free"], rd.n)
                    fn(XRS[:, 0:m], XRS[:, 0:m], ACT.Exp, scale=-0.5).then_inc(S["xrstd_ready"], 1)

                rms(2 * T)
                rd.tiles(("in_state", l), lambda k, b: fn(P2[:, k, :], b[:, :], ACT.Copy))
                rd.tiles(("in_rest", l),
                         lambda k, b, n=n: fn(P2[:, 2 * STATE_BLOCKS + k, 0:n], b[:, 0:n], ACT.Copy))
                rd.tiles_read(("in_rest", l))

                fn(NSQ[:, 0:4, 0:n], P2[:, 14:18, 0:n], ACT.Square).then_inc(S["n_squares"], 1)
                fn(NSQ[:, 4, :], P2[:, 0, :], ACT.Square).then_inc(S["n_squares"], 1)
                for i in range(5):
                    m = n if i < 4 else 2 * T
                    rstd_of(NRS[:, i, 0:m], m, 1.0 / HD, "eps6")
                act.wait_ge(S["abank_free"], rd.n)
                fn(NRS[:, 0:4, 0:n], NRS[:, 0:4, 0:n], ACT.Exp, scale=-0.5).then_inc(S["n_rstd"], 1)
                fn(NRS[:, 4, :], NRS[:, 4, :], ACT.Exp, scale=-0.5).then_inc(S["n_rstd"], 1)
                for kv in range(2):
                    copy_bank(KD2[:, kv, :])
                units = [(s, t, q, h) for s in range(1 if last else 2) for t in range(4) for q in range(2)
                         for h in range(2)]

                def exps2(i):
                    s, t, q, h = units[i]
                    m = 2 * T if s == 0 else T
                    act.wait_ge(S["w_scores"], w("w_scores"))
                    c = i % 2
                    fn(ES[:, c:c + 1], pcol("sink", 8 * l + 2 * t + h), ACT.Exp, bias=NM[:, c:c + 1])\
                        .then_inc(S["act_chain"], st.one())
                    act.wait_ge(S["act_chain"], st.n)
                    fn(EE2[:, c, 0:m], SM2[:, c, 0:m], ACT.Exp, scale=SCALE, bias=NM[:, c:c + 1],
                       accum_out=SU[:, c:c + 1]).then_inc(S["w_exp"], 1)

                exps2(0)
                for i, (s, t, q, h) in enumerate(units):
                    if i + 1 < len(units):
                        exps2(i + 1)
                    nk = 4 if s == 0 else 2
                    copy_bank(PT2[:, i % 4, 0:nk, :].rearrange("p a b -> p (a b)"), nk * P)

                for s in range(1 if last else 2):
                    for g in range(4):
                        copy_bank(FB[:, (s * 4 + g) % 2].rearrange("p a b c -> p (a b c)"))

                act.wait_ge(S["four_done"], w("four_done"))
                for d in range(2):
                    z = P2[:, 6 + 4 * d:10 + 4 * d, :]
                    if d:
                        act.wait_ge(S["dir_done"], w("dir_done"))
                    fn(TA, z, ACT.Abs).then_inc(S["act_chain"], st.one())
                    act.wait_ge(S["act_chain"], st.n)
                    fn(TA, TA, ACT.Exp, scale=-1.0).then_inc(S["act_chain"], st.one())
                    act.wait_ge(S["act_chain"], st.n)
                    fn(TB, z, ACT.Relu, scale=-1.0).then_inc(S["act_chain"], st.one())
                    fn(TA, TA, ACT.Ln, bias=pcol("one")).then_inc(S["sp_first"], 1)
                    act.wait_ge(S["act_chain"], st.n)
                    for h in range(4):
                        lb = LLB[:, 8 * l + 4 * d + h:8 * l + 4 * d + h + 1]
                        fn(TC[:, h, :], z[:, h, :], ACT.Abs, scale=-1.0, bias=lb).then_inc(S["act_chain"], st.one())
                        fn(TD[:, h, :], z[:, h, :], ACT.Relu, scale=-1.0, bias=lb).then_inc(S["act_chain"], st.one())
                    act.wait_ge(S["act_chain"], st.n)
                    fn(TC, TC, ACT.Exp, scale=-1.0).then_inc(S["act_chain"], st.one())
                    act.wait_ge(S["act_chain"], st.n)
                    fn(TC, TC, ACT.Ln, bias=pcol("one")).then_inc(S["sp_second"], 1)
                    act.wait_ge(S["sp_sum"], w("sp_sum"))
                    fn(TB, TB, ACT.Exp, scale=-1.0).then_inc(S["k_raw"], 1)
                act.wait_ge(S["dir_done"], w("dir_done"))
                act.wait_ge(S["tot_ready"], w("tot_ready"))
                fn(ETOT, TOT, ACT.Exp).then_inc(S["e_tot"], 1)
                fn(P2[:, 22:26, 0:n], P2[:, 22:26, 0:n], ACT.Silu).then_inc(S["act_chain"], st.one())
                fn(P2[:, 18:22, 0:n], P2[:, 18:22, 0:n], ACT.Silu).then_inc(S["q_silu"], 1)
                for c in range(4):
                    copy_bank(VTK[:, c].rearrange("p a b -> p (a b)"))
                for d in range(2):
                    if d == 0:
                        act.wait_ge(S["ks_diff"], w("ks_diff"))
                        fn(KSF, KSF, ACT.Exp).then_inc(S["ks_exp"], 1)
                    else:
                        fn(KSF, LF[:, 4:8, :], ACT.Exp).then_inc(S["ks_exp"], 1)
                    for i in range(3):
                        copy_bank(KST[:, d, i].rearrange("p a b -> p (a b)"))
                for h in range(4):
                    act.wait_ge(S["qi_diff"], w("qi_diff"))
                    fn(QI[:, h % 2, 0, 0:n], LF[:, h, 0:n], ACT.Exp).then_inc(S["qi_exp"], 1)
                    fn(QI[:, h % 2, 1, 0:n], QI[:, h % 2, 1, 0:n], ACT.Exp).then_inc(S["qi_exp"], 1)
                    for i in range(2 * LEVELS):
                        act.wait_ge(S["lvl_diff"], w("lvl_diff", 2))
                        fn(LDF[:, i % 2, 0:n], LDF[:, i % 2, 0:n], ACT.Exp).then_inc(S["lvl_exp"], 1)
                    copy_bank(P2[:, 18 + h, 0:n], n)
                act.wait_ge(S["abank_free"], rd.n)
                fn(HSQ[:, :, 0:n], P2[:, 18:22, 0:n], ACT.Square).then_inc(S["o_sq"], 1)
                for h in range(4):
                    rstd_of(HRS[:, h, 0:n], n, 1.0 / P, "eps6")
                act.wait_ge(S["abank_free"], rd.n)
                fn(HRS[:, :, 0:n], HRS[:, :, 0:n], ACT.Exp, scale=-0.5).then_inc(S["o_rs"], 1)

                for br in range(3):
                    for half in range(2):
                        i = 2 * br + half
                        if i >= 2:
                            act.wait_ge(S["merge_used"], w("merge_used"))
                        rd.tiles(("gate", l, br, half),
                                 lambda k, b, i=i, n=n: fn(GB[:, i % 2, k, 0:n], b[:, 0:n], ACT.Sigmoid))
                        rd.tiles(("proj", l, br, half),
                                 lambda k, b, i=i, n=n: fn(PB[:, i % 2, k, 0:n], b[:, 0:n], ACT.Copy))
                act.wait_ge(S["merge_used"], w("merge_used", 2))
                act.wait_ge(S["x_ready"], w("x_ready"))
                rms(n)
                rd.tiles(("ff1", l), lambda k, b, n=n: fn(HF2[:, k, 0:n], b[:, 0:n], ACT.Relu))
                if not last:
                    act.wait_ge(S["x_ready"], w("x_ready"))

        @block.vector
        def _(ve):
            w = Waits()
            st = Steps()
            rd = Reader(ve, vbank)
            tt, ts, stt = ve.tensor_tensor, ve.tensor_scalar, ve.scalar_tensor_tensor
            MUL, ADD, SUB, MAX = ALU.mult, ALU.add, ALU.subtract, ALU.max

            def say(sem):
                ve.drain().then_inc(sem, 1)

            def layer_norm(z, gain, bias, dst, sem):
                ve.wait_ge(S["vbank_full"], rd.take())
                b = rd.bank()[:, 0:T]
                stt(z, rep(b, KD), -1.0 / D, z, MUL, ADD).then_inc(S["vbank_free"], 1)
                ve.wait_ge(S["vbank_free"], rd.n)
                say(S["centered"])
                ve.wait_ge(S["rstd_ready"], w("rstd_ready"))
                tt(z, z, rep(ZRS, KD), MUL).then_inc(S["vec_chain"], st.one())
                ve.wait_ge(S["vec_chain"], st.n)
                for k in range(KD):
                    ins = ts(dst(k), z[:, k, :], pcol(*gain(k)), pcol(*bias(k)), MUL, ADD)
                    if k < KD - 1:
                        ins.then_inc(S["vec_chain"], st.one())
                ins.then_inc(sem, 1)

            def residual(key):
                rd.tiles(key, lambda k, b: stt(Z[:, k, :], X[:, k, 0:T], DEEPNORM, b[:, 0:T], MUL, ADD))
                rd.tiles_read(key)

            def mod_fill(l, k):
                g = G["mod", l]
                if 1 <= k <= g.blocks:
                    ve.wait_ge(S["gemm_step"], g.step0 + k)
                    ve.tensor_copy(mod_row[:, (k - 1) % 2, :], bank[(g.tile0 + k - 1) % NBANK][0:2, 0:BLK])\
                        .then_inc(S["tile_free"], 1)
                if 2 <= k < g.blocks + 2:
                    j = 2 * (k - 2)
                    ve.wait_ge(S["vbank_full"], rd.take())
                    b = rd.bank()[:, 0:4].rearrange("p (a b) -> p a b", b=2)
                    tt(MOD[l][:, j:j + 2, :], b, pcol("b_mod", 48 * l + j, 2).unsqueeze(2).to_broadcast([P, 2, 2]),
                       ADD).then_inc(S["vbank_free"], 1)

            ve.wait_ge(S["par_landed"], 16)
            tt(LAMP, pcol("lam_q", 0, 2), pcol("lam_k", 0, 2), MUL).then_inc(S["lam_prod"], 1)
            ts(OMKA, pcol("k_a", 0, 4), -1.0, 1.0, MUL, ADD).then_inc(S["vec_chain"], st.one())
            ts(G08, pcol("subln_g"), 1.0 - LAM_INIT, None, MUL).then_inc(S["vec_chain"], st.one())
            tt(LBT[:, 0:8], pcol("lb", 0, 8), pcol("lb", 8, 8), MAX).then_inc(S["vec_chain"], st.one())
            ve.wait_ge(S["vec_chain"], st.n)
            tt(LB[:, 0:8], pcol("lb", 0, 8), LBT[:, 0:8], SUB).then_inc(S["vec_chain"], st.one())
            tt(LB[:, 8:16], pcol("lb", 8, 8), LBT[:, 0:8], SUB).then_inc(S["lb_shifted"], 1)
            ve.wait_ge(S["lb_exp"], w("lb_exp"))
            tt(LBT[:, 0:8], LB[:, 0:8], LB[:, 8:16], ADD).then_inc(S["vec_chain"], st.one())
            ve.wait_ge(S["vec_chain"], st.n)
            ve.reciprocal(LBT[:, 8:16], LBT[:, 0:8]).then_inc(S["vec_chain"], st.one())
            ve.wait_ge(S["vec_chain"], st.n)
            tt(LB[:, 0:8], LB[:, 0:8], LBT[:, 8:16], MUL).then_inc(S["vec_chain"], st.one())
            tt(LB[:, 8:16], LB[:, 8:16], LBT[:, 8:16], MUL).then_inc(S["vec_chain"], st.one())
            ve.wait_ge(S["vec_chain"], st.n)
            tt(LB[:, 8:16], LB[:, 8:16], LB[:, 0:8], ADD).then_inc(S["vec_chain"], st.one())
            ve.wait_ge(S["vec_chain"], st.n)
            tt(LB[:, 8:16], LB[:, 8:16], LB[:, 0:8], SUB).then_inc(S["vec_chain"], st.one())
            ve.wait_ge(S["vec_chain"], st.n)
            tt(LB[:, 0:8], LB[:, 0:8], LB[:, 0:8], SUB).then_inc(S["vec_chain"], st.one())
            ve.wait_ge(S["vec_chain"], st.n)
            ts(OMLB, LB, -1.0, 1.0, MUL, ADD).then_inc(S["vec_chain"], st.one())
            ts(LBT, LB, LN_SMALL, None, MAX).then_inc(S["lb_floored"], 1)
            ve.wait_ge(S["lb_ln"], w("lb_ln"))
            ts(LBT, LB, LN_SMALL, LN_FLOOR - LN_LN_SMALL, ALU.is_lt, MUL).then_inc(S["vec_chain"], st.one())
            ve.wait_ge(S["vec_chain"], st.n)
            tt(LLB, LLB, LBT, ADD).then_inc(S["vec_chain"], st.one())
            ve.wait_ge(S["vec_chain"], st.n)

            ve.wait_ge(S["lam_exp"], w("lam_exp"))
            tt(NLAM, LAME2[:, 1:2], LAME2[:, 0:1], SUB).then_inc(S["vec_chain"], st.one())
            ve.wait_ge(S["vec_chain"], st.n)
            ts(NLAM, NLAM, -LAM_INIT, None, ADD).then_inc(S["vec_chain"], st.one())
            ve.wait_ge(S["const_landed"], 16)
            ve.wait_ge(S["masks_ready"], w("masks_ready"))
            for i in range(4):
                ve.wait_ge(S["vbank_full"], rd.take())
                b = rd.bank()[:, :].rearrange("p (a b) -> p a b", a=2)
                tt(R2, PRJ[:, 14 + 2 * i:16 + 2 * i, 1:T + 1], rep(cc("cos_a"), 2), MUL)\
                    .then_inc(S["vec_chain"], st.one())
                tt(R3, b, rep(cc("sin_a"), 2), MUL).then_inc(S["vbank_free"], 1)
                ve.wait_ge(S["vec_chain"], st.n)
                ve.wait_ge(S["vbank_free"], rd.n)
                if i >= 2:
                    tt(KR1[:, 2 * i - 4:2 * i - 2, :], R2, R3, ADD).then_inc(S["vec_chain"], st.one())
                    ve.wait_ge(S["vec_chain"], st.n)
                else:
                    tt(R2, R2, R3, ADD).then_inc(S["vec_chain"], st.one())
                    ve.wait_ge(S["vec_chain"], st.n)
                    for c in range(2):
                        ts(QZ1[:, 2 * i:2 * i + 2, c, :], R2, pcol("half", c), None, MUL)\
                            .then_inc(S["vec_chain"], st.one())
                        ve.wait_ge(S["vec_chain"], st.n)
            say(S["rope_ready"])

            def score(u):
                ve.wait_ge(S["vbank_full"], rd.take())
                b = rd.bank()[:, :].rearrange("p (a b) -> p a b", a=2)
                c = 2 * (u % 2)
                tt(SM1[:, u % 2], b, rep(cc("causal", 2, T)[:, u % 2, :], 2), ADD).then_inc(S["vbank_free"], 1)
                ve.wait_ge(S["vbank_free"], rd.n)
                ve.tensor_reduce(MX[:, c:c + 2], SM1[:, u % 2], AXX, MAX).then_inc(S["vec_chain"], st.one())
                ve.wait_ge(S["vec_chain"], st.n)
                ts(NM[:, c:c + 2], MX[:, c:c + 2], -SCALE, None, MUL).then_inc(S["scores_ready"], 1)

            score(0)
            for u in range(8):
                if u < 7:
                    score(u + 1)
                mod_fill(0, u)
                h, qt = u // 2, u % 2
                c = 2 * qt
                ve.wait_ge(S["exp_ready"], w("exp_ready", 2))
                ve.reciprocal(SU[:, c:c + 2], SU[:, c:c + 2]).then_inc(S["vec_chain"], st.one())
                ve.wait_ge(S["vec_chain"], st.n)
                tt(SU[:, c + 1:c + 2], SU[:, c + 1:c + 2], NLAM, MUL).then_inc(S["vec_chain"], st.one())
                ts(AT1[:, qt, :], EE1[:, qt, 0, :], SU[:, c:c + 1], None, MUL).then_inc(S["vec_chain"], st.one())
                ve.wait_ge(S["vec_chain"], st.n)
                stt(AT1[:, qt, :], EE1[:, qt, 1, :], SU[:, c + 1:c + 2], AT1[:, qt, :], MUL, ADD)\
                    .then_inc(S["attn_ready"], 1)
                if qt:
                    ve.wait_ge(S["vbank_full"], rd.take())
                    b = rd.bank()
                    ve.tensor_copy(OO1[:, h, :], b[:, 0:T]).then_inc(S["vbank_free"], 1)
            ve.wait_ge(S["vbank_free"], rd.n)
            tt(OSQ, OO1, OO1, MUL).then_inc(S["o_squares"], 1)
            ve.wait_ge(S["o_rstd"], w("o_rstd"))
            for h in range(4):
                ins = stt(YAB[:, 4 + h, :], OO1[:, h, :], G08, ORS[:, h, :], MUL, MUL)
                if h < 3:
                    ins.then_inc(S["vec_chain"], st.one())
            ins.then_inc(S["yd_ready"], 1)

            mod_fill(0, 8)
            ve.wait_ge(S["pad_zero"], w("pad_zero"))
            tt(DT, PRJ[:, 0:RWKV_TILES, 0:T], PRJ[:, 0:RWKV_TILES, 1:T + 1], SUB).then_inc(S["vec_chain"], st.one())
            ve.wait_ge(S["vec_chain"], st.n)
            for t in range(RWKV_TILES):
                stt(XS[:, t, :], DT[:, t, :], pcol("mu", t), PRJ[:, t, 1:T + 1], MUL, ADD)\
                    .then_inc(S["vec_chain"], st.one())
            ve.wait_ge(S["vec_chain"], st.n)
            ve.sem_inc(S["xs_ready"], 1)
            ve.sem_inc(S["xs_pool"], 1)
            for k in range(9, 12):
                mod_fill(0, k)
            for t in range(4):
                ts(KK[:, t, :], XS[:, 4 + t, :], pcol("k_k", t), None, MUL).then_inc(S["vec_chain"], st.one())
            ve.wait_ge(S["vec_chain"], st.n)
            tt(KSQ, KK, KK, MUL).then_inc(S["kk_squares"], 1)
            mod_fill(0, 12)
            ve.wait_ge(S["kk_root"], w("kk_root"))
            ts(E1, E1, 1e-12, None, MAX).then_inc(S["vec_chain"], st.one())
            ve.wait_ge(S["vec_chain"], st.n)
            ve.reciprocal(E1, E1).then_inc(S["vec_chain"], st.one())
            ve.wait_ge(S["vec_chain"], st.n)
            tt(KK, KK, E1, MUL).then_inc(S["vec_chain"], st.one())
            ve.wait_ge(S["vec_chain"], st.n)
            mod_fill(0, 13)
            ve.wait_ge(S["decay_ready"], w("decay_ready"))
            ts(LD, LD, -EXP_MINUS_HALF, None, MUL).then_inc(S["vec_chain"], st.one())
            ve.wait_ge(S["vec_chain"], st.n)
            for t in range(4):
                ve.tensor_tensor_scan(LL[:, t, :], cc("reset")[:, 0:T], LD[:, t, :], 0.0, MUL, ADD)\
                    .then_inc(S["vec_chain"], st.one())
            ve.wait_ge(S["vec_chain"], st.n)
            for k in (14, 15):
                mod_fill(0, k)
            LL8, LP8 = (v.rearrange("p a (c b) -> p (a c) b", c=2) for v in (LL, LP))
            tt(LP, LL, LD, SUB).then_inc(S["vec_chain"], st.one())
            ve.tensor_copy(GMS.unsqueeze(2), LL8[:, :, 63:64]).then_inc(S["vec_chain"], st.one())
            ve.wait_ge(S["vec_chain"], st.n)
            mid = GMS.unsqueeze(2).to_broadcast([P, 8, P])
            tt(LL8, LL8, mid, SUB).then_inc(S["vec_chain"], st.one())
            tt(LP8, LP8, mid, SUB).then_inc(S["log_ready"], 1)
            for k in (16, 17):
                mod_fill(0, k)
            ve.wait_ge(S["a_ready"], w("a_ready"))
            for t in range(4):
                ts(LD[:, t, :], AA[:, t, :], pcol("k_a", t), OMKA[:, t:t + 1], MUL, ADD)\
                    .then_inc(S["vec_chain"], st.one())
            ve.wait_ge(S["vec_chain"], st.n)
            tt(XS[:, 4:8, :], XS[:, 4:8, :], LD, MUL).then_inc(S["vec_chain"], st.one())
            ve.wait_ge(S["vec_chain"], st.n)
            for k in (18, 19):
                mod_fill(0, k)
            ve.wait_ge(S["exp_factors"], w("exp_factors"))
            stt(AR[:, :, 0, :], KK.rearrange("p a (c b) -> p (a c) b", c=2), -1.0,
                E3.rearrange("p a (c b) -> p (a c) b", c=2), MUL, MUL).then_inc(S["vec_chain"], st.one())
            tt(AR[:, :, 1, :], XS[:, 0:4, :].rearrange("p a (c b) -> p (a c) b", c=2),
               E1.rearrange("p a (c b) -> p (a c) b", c=2), MUL).then_inc(S["vec_chain"], st.one())
            tt(BH, KK, AA, MUL).then_inc(S["vec_chain"], st.one())
            tt(KH, XS[:, 4:8, :], E2, MUL).then_inc(S["vec_chain"], st.one())
            ve.wait_ge(S["vec_chain"], st.n)
            tt(BH, BH, E2, MUL).then_inc(S["vec_chain"], st.one())
            ve.wait_ge(S["vec_chain"], st.n)
            for k in (20, 21):
                mod_fill(0, k)
            ve.wait_ge(S["g_out"], w("g_out"))
            for par_ in range(2):
                ts(BZ[:, :, par_, :], BH, pcol("half", par_), None, MUL).then_inc(S["vec_chain"], st.one())
                ts(KZ[:, :, par_, :], KH, pcol("half", par_), None, MUL).then_inc(S["vec_chain"], st.one())
            tt(FST.unsqueeze(2), E1[:, :, P - 1:P], EGM.rearrange("p (a b) -> p a b", b=2)[:, :, 1:2], MUL)\
                .then_inc(S["vec_chain"], st.one())
            ve.wait_ge(S["vec_chain"], st.n)
            ve.sem_inc(S["hats_ready"], 1)
            ve.sem_inc(S["hats_act"], 1)
            for k in range(22, MOD_BLOCKS + 2):
                mod_fill(0, k)
            for dst in (XI, YI):
                ve.tensor_copy(dst, rep(ident, 16)).then_inc(S["inv_init"], 1)
            ve.wait_ge(S["pr_zero"], w("pr_zero"))
            for u in range(16):
                ve.wait_ge(S["vbank_full"], rd.take())
                b = rd.bank()
                ve.copy_predicated(PR[:, u].rearrange("p a b -> p (a b)"), mask("rwkv", 0, 512), b[:, :])\
                    .then_inc(S["vbank_free"], 1)
            for l in range(LEVELS):
                for q in range(4):
                    four = slice(4 * q, 4 * q + 4)
                    ve.wait_ge(S["vbank_full"], rd.take())
                    b = rd.bank()[:, :].rearrange("p (a b) -> p a b", a=4)
                    tt(T1[:, four, :], b, rep(mask("bwd", l), 4), MUL).then_inc(S["vbank_free"], 1)
                    if l == 0:
                        ve.wait_ge(S["vbank_free"], rd.n)
                        tt(XI[:, four, :], XI[:, four, :], T1[:, four, :], ADD).then_inc(S["vec_chain"], st.one())
                        ve.wait_ge(S["vec_chain"], st.n)
                        tt(T1[:, four, :], PR[:, four, 0, :], rep(mask("fwd", 0), 4), MUL)\
                            .then_inc(S["vec_chain"], st.one())
                        ve.wait_ge(S["vec_chain"], st.n)
                        tt(YI[:, four, :], YI[:, four, :], T1[:, four, :], ADD).then_inc(S["inv_first"], 1)
                for q in range(4 if l else 0):
                    four = slice(4 * q, 4 * q + 4)
                    for dst in ((XI, YI) if l < LEVELS - 1 else (YI,)):
                        ve.wait_ge(S["vbank_full"], rd.take())
                        b = rd.bank()[:, :].rearrange("p (a b) -> p a b", a=4)
                        tt(dst[:, four, :], dst[:, four, :], b, ADD).then_inc(S["vbank_free"], 1)
            ve.wait_ge(S["vbank_full"], rd.take())
            b = rd.bank()
            for t in range(4):
                ins = stt(SB[:, t, :], b[:, t * P:(t + 1) * P], FST[:, t:t + 1], block64, MUL, MUL)
                if t < 3:
                    ins.then_inc(S["vec_chain"], st.one())
            ins.then_inc(S["vbank_free"], 1)
            for t in range(4):
                ins = stt(BON[:, t, :], XS[:, t, :], pcol("r_k", t), XS[:, 4 + t, :], MUL, MUL)
                if t < 3:
                    ins.then_inc(S["vec_chain"], st.one())
            ins.then_inc(S["bonus_in"], 1)
            for i in range(2):
                ve.wait_ge(S["vbank_full"], rd.take())
                b = rd.bank()[:, :].rearrange("p (a b) -> p a b", a=2)
                y = YF[:, 2 * i:2 * i + 2, :]
                stt(y, b, -1.0 / HD, y, MUL, ADD).then_inc(S["vbank_free"], 1)
            ve.wait_ge(S["vbank_free"], rd.n)
            tt(GSQ, YF, YF, MUL).then_inc(S["gn_sq"], 1)
            for i in range(2):
                ve.wait_ge(S["vbank_full"], rd.take())
                b = rd.bank()[:, :].rearrange("p (a b) -> p a b", a=2)
                tt(BON[:, 2 * i:2 * i + 2, :], b, XS[:, 8 + 2 * i:10 + 2 * i, :], MUL).then_inc(S["vbank_free"], 1)
            ve.wait_ge(S["gn_rstd"], w("gn_rstd"))
            tt(YF, YF, GRS, MUL).then_inc(S["vec_chain"], st.one())
            ve.wait_ge(S["vec_chain"], st.n)
            for t in range(4):
                ts(YF[:, t, :], YF[:, t, :], pcol("lnx_g", t), pcol("lnx_b", t), MUL, ADD)\
                    .then_inc(S["vec_chain"], st.one())
            ve.wait_ge(S["vec_chain"], st.n)
            ve.wait_ge(S["vbank_free"], rd.n)
            tt(YF, YF, BON, ADD).then_inc(S["vec_chain"], st.one())
            ve.wait_ge(S["vec_chain"], st.n)
            tt(YAB[:, 0:4, :], YF, GG, MUL).then_inc(S["yr_ready"], 1)
            residual("ab_out")
            layer_norm(Z, lambda k: ("ln1_g", k), lambda k: ("ln1_b", k), lambda k: X[:, k, 0:T], S["x_ready"])

            def ffn(l):
                g = G["up", l]
                ve.memset(GP[:, :, 0:2], 0.0).then_inc(S["vec_chain"], st.one())
                ve.wait_ge(S["vec_chain"], st.n)
                for pair in range(NFF // 2):
                    for f in range(2):
                        k = 2 * pair + f
                        i = k % 4
                        ve.wait_ge(S["tile_free"], g.tile0 + 4 * pair + f + 1)
                        cw = [pcol("conv_w", (3 * l + j) * NFF + k) for j in range(3)]
                        ts(CV[:, i, :], GP[:, i, 2:T + 2], cw[2], pcol("conv_b", l * NFF + k), MUL, ADD)\
                            .then_inc(S["vec_chain"], st.one())
                        ve.wait_ge(S["vec_chain"], st.n)
                        stt(CV[:, i, :], GP[:, i, 1:T + 1], cw[1], CV[:, i, :], MUL, ADD)\
                            .then_inc(S["vec_chain"], st.one())
                        ve.wait_ge(S["vec_chain"], st.n)
                        stt(CV[:, i, :], GP[:, i, 0:T], cw[0], CV[:, i, :], MUL, ADD).then_inc(S["conv_ready"], 1)
                    for f in range(2):
                        k = 2 * pair + f
                        ve.wait_ge(S["silu_ready"], w("silu_ready"))
                        ve.wait_ge(S["tile_free"], g.tile0 + 4 * pair + 2 + f + 1)
                        tt(HF[:, k, :], CV[:, k % 4, :], VAL[:, k % 4, :], MUL).then_inc(S["hid_ready"], 1)
                residual(("down", l))
                layer_norm(Z, lambda k: ("ln2_g", 8 * l + k), lambda k: ("ln2_b", 8 * l + k),
                           lambda k: X[:, k, 0:T], S["x_ready"])

            ffn(0)
            rd.tiles_read("c_in")
            layer_norm(UV[:, 8:16, :], lambda k: ("c_ln_g", k), lambda k: ("c_ln_b", k), lambda k: UV[:, 8 + k, :],
                       S["v_ready"])
            ve.wait_ge(S["ws_landed"], 32)
            tt(WS, WS, rep(mask("rwkv", 1), 8), MUL).then_inc(S["mix_in"], 1)
            for j in range(2):
                for q in range(2):
                    ve.wait_ge(S["vbank_full"], rd.take())
                    b = rd.bank()[:, :].rearrange("p (a b) -> p a b", a=4)
                    tok = slice(j * P, (j + 1) * P)
                    tt(MU[:, 4 * q:4 * q + 4, tok], UV[:, 4 * q:4 * q + 4, tok], b, MUL).then_inc(S["vbank_free"], 1)
            residual("c_out")
            layer_norm(Z, lambda k: ("ln1_g", 8 + k), lambda k: ("ln1_b", 8 + k), lambda k: X[:, k, 0:T],
                       S["x_ready"])
            ffn(1)

            for l in range(2):
                last = l == 1
                n = T if last else 2 * T
                streams = 1 if last else 2
                mod = MOD[l]
                for i, name in enumerate(("norm1_g", "norm2_g")):
                    sc = SC[2 * l + i]
                    ts(sc, mod[:, 8 + 24 * i:16 + 24 * i, :], 1.0, None, ADD).then_inc(S["vec_chain"], st.one())
                    ve.wait_ge(S["vec_chain"], st.n)
                    tt(sc, sc, pcol(name, 8 * l, 8).unsqueeze(2).to_broadcast([P, 8, 2]), MUL)\
                        .then_inc(S["vec_chain"], st.one())
                    ve.wait_ge(S["vec_chain"], st.n)

                def adaln(which, m):
                    ve.wait_ge(S["xrstd_ready"], w("xrstd_ready"))
                    tt(HB[:, :, 0:m], X[:, :, 0:m], rep(XRS[:, 0:m], KD), MUL).then_inc(S["vec_chain"], st.one())
                    ve.wait_ge(S["vec_chain"], st.n)
                    for k in range(KD):
                        for s in range(m // T):
                            h = HB[:, k, s * T:(s + 1) * T]
                            ins = ts(h, h, SC[2 * l + which][:, k, s:s + 1], mod[:, 24 * which + k, s:s + 1],
                                     MUL, ADD)
                            ins.then_inc(S["vec_chain"], st.one())
                    ve.wait_ge(S["vec_chain"], st.n)
                    ve.sem_inc(S["h_ready"], 1)
                    ve.sem_inc(S["h_pool"], 1)

                def gated(key, gate):
                    def read(k, b):
                        for s in range(streams):
                            x = X[:, k, s * T:(s + 1) * T]
                            ins = stt(x, b[:, s * T:(s + 1) * T], mod[:, gate + k, s:s + 1], x, MUL, ADD)
                            if s < streams - 1:
                                ins.then_inc(S["vec_chain"], st.one())
                        return ins
                    rd.tiles(key, read)
                    rd.tiles_read(key)
                    ve.wait_ge(S["vec_chain"], st.n)

                adaln(0, 2 * T)

                ve.wait_ge(S["n_rstd"], w("n_rstd", 2))
                for i in range(5):
                    m = n if i < 4 else 2 * T
                    t = 14 + i if i < 4 else 0
                    name = "q_norm" if i < 4 else "k_norm"
                    stt(P2[:, t, 0:m], P2[:, t, 0:m], pcol(name, l), NRS[:, i, 0:m], MUL, MUL)\
                        .then_inc(S["vec_chain"], st.one())
                ve.wait_ge(S["vec_chain"], st.n)
                ve.sem_inc(S["qk_ready"], 1)
                for i in range(5):
                    ve.wait_ge(S["vbank_full"], rd.take())
                    b = rd.bank()
                    x = P2[:, 14 + i if i < 4 else 0, 0:T]
                    tt(RT[:, 0, :], x, cc("cos_b"), MUL).then_inc(S["vec_chain"], st.one())
                    tt(RT[:, 1, :], b[:, 0:T], cc("sin_b"), MUL).then_inc(S["vbank_free"], 1)
                    ve.wait_ge(S["vec_chain"], st.n)
                    ve.wait_ge(S["vbank_free"], rd.n)
                    tt(x, RT[:, 0, :], RT[:, 1, :], ADD).then_inc(S["vec_chain"], st.one())
                    ve.wait_ge(S["vec_chain"], st.n)
                ve.wait_ge(S["vz_zero"], w("vz_zero"))
                ve.wait_ge(S["vbank_full"], rd.take())
                b = rd.bank()[:, :].rearrange("p (c v d) -> p c v d", c=4, v=2)
                ve.tensor_copy(VZ[:, :, :, 0, 0:HD], b).then_inc(S["vec_chain"], st.one())
                ve.tensor_copy(VZ[:, :, :, 1, HD:2 * HD], b).then_inc(S["vbank_free"], 1)
                for par_ in range(2):
                    ts(QZ2[:, :, par_, 0:n], P2[:, 14:18, 0:n], pcol("half", par_), None, MUL)\
                        .then_inc(S["vec_chain"], st.one())
                ve.wait_ge(S["vec_chain"], st.n)
                ve.sem_inc(S["qz_ready"], 1)
                units = [(s, t, q, h) for s in range(streams) for t in range(4) for q in range(2) for h in range(2)]

                def score2(i):
                    s, t, q, h = units[i]
                    c = i % 2
                    ve.wait_ge(S["vbank_full"], rd.take())
                    b = rd.bank()
                    m = T
                    if s == 0:
                        m = 2 * T
                        tt(SM2[:, c, 0:T], b[:, 0:T], cc("window", 2, T)[:, q, :], ADD)\
                            .then_inc(S["vec_chain"], st.one())
                        ve.tensor_copy(SM2[:, c, T:m], b[:, T:m]).then_inc(S["vbank_free"], 1)
                        ve.wait_ge(S["vec_chain"], st.n)
                    else:
                        ve.tensor_copy(SM2[:, c, 0:T], b[:, 0:T]).then_inc(S["vbank_free"], 1)
                    ve.wait_ge(S["vbank_free"], rd.n)
                    ve.tensor_reduce(MX[:, c:c + 1], SM2[:, c, 0:m], AXX, MAX).then_inc(S["vec_chain"], st.one())
                    ve.wait_ge(S["vec_chain"], st.n)
                    ts(MX[:, c:c + 1], MX[:, c:c + 1], SCALE, pcol("sink", 8 * l + 2 * t + h), MUL, MAX)\
                        .then_inc(S["vec_chain"], st.one())
                    ve.wait_ge(S["vec_chain"], st.n)
                    ts(NM[:, c:c + 1], MX[:, c:c + 1], -1.0, None, MUL).then_inc(S["w_scores"], 1)

                score2(0)
                for i, (s, t, q, h) in enumerate(units):
                    if i + 1 < len(units):
                        score2(i + 1)
                    if l == 0 and i < MOD_BLOCKS + 2:
                        mod_fill(1, i)
                    c = i % 2
                    m = 2 * T if s == 0 else T
                    ve.wait_ge(S["w_exp"], w("w_exp"))
                    tt(SU[:, c:c + 1], SU[:, c:c + 1], ES[:, c:c + 1], ADD).then_inc(S["vec_chain"], st.one())
                    ve.wait_ge(S["vec_chain"], st.n)
                    ve.reciprocal(SU[:, c:c + 1], SU[:, c:c + 1]).then_inc(S["vec_chain"], st.one())
                    ve.wait_ge(S["vec_chain"], st.n)
                    ts(EE2[:, c, 0:m], EE2[:, c, 0:m], SU[:, c:c + 1], None, MUL).then_inc(S["w_probs"], 1)
                    if h:
                        ve.wait_ge(S["vbank_full"], rd.take())
                        b = rd.bank()
                        c0 = s * T + q * P
                        ve.tensor_copy(P2[:, 14 + t, c0:c0 + P], b[:, 0:P]).then_inc(S["vbank_free"], 1)

                for s in range(streams):
                    for g in range(4):
                        ve.wait_ge(S["vbank_full"], rd.take())
                        b = rd.bank()
                        ve.tensor_copy(P2[:, 26 + g, s * T:(s + 1) * T], b[:, 0:T]).then_inc(S["vbank_free"], 1)
                say(S["four_done"])

                for d in range(2):
                    z = P2[:, 6 + 4 * d:10 + 4 * d, :]
                    ve.wait_ge(S["sp_first"], w("sp_first"))
                    tt(TA, TA, TB, ADD).then_inc(S["vec_chain"], st.one())
                    ve.wait_ge(S["vec_chain"], st.n)
                    tt(TB, TA, z, ADD).then_inc(S["vec_chain"], st.one())
                    ve.wait_ge(S["sp_second"], w("sp_second"))
                    tt(TC, TC, TD, ADD).then_inc(S["vec_chain"], st.one())
                    ve.wait_ge(S["vec_chain"], st.n)
                    ve.sem_inc(S["sp_sum"], 1)
                    tt(LF[:, 4 * d:4 * d + 4, :], TC, TA, SUB).then_inc(S["vec_chain"], st.one())
                    ve.wait_ge(S["k_raw"], w("k_raw"))
                    for h in range(4):
                        ts(z[:, h, :], TB[:, h, :], OMLB[:, 8 * l + 4 * d + h:8 * l + 4 * d + h + 1],
                           None, MUL).then_inc(S["vec_chain"], st.one())
                    ve.wait_ge(S["vec_chain"], st.n)
                    src = LF if d == 0 else TA
                    for h in range(4):
                        dst = LF[:, h, :] if d == 0 else TA[:, h, :]
                        ve.tensor_tensor_scan(dst, cc("reset"), LF[:, 4 * d + h, :], 0.0, MUL, ADD)\
                            .then_inc(S["vec_chain"], st.one())
                    ve.wait_ge(S["vec_chain"], st.n)
                    tot = TOT.rearrange("p (h c b) -> p h c b", c=4, b=1)[:, 4 * d:4 * d + 4]
                    ve.tensor_copy(tot, src[:, 0:4, :].rearrange("p h (c b) -> p h c b", c=4)[:, :, :, P - 1:P])\
                        .then_inc(S["vec_chain"], st.one())
                    if d:
                        tt(LF[:, 4:8, :], TA, LF[:, 4:8, :], SUB).then_inc(S["vec_chain"], st.one())
                    ve.wait_ge(S["vec_chain"], st.n)
                    ve.sem_inc(S["dir_done"], 1)
                ve.sem_inc(S["tot_ready"], 1)
                ve.sem_inc(S["lf_ready"], 1)
                tot0 = TOT.rearrange("p (h c b) -> p h c b", c=4, b=1)[:, 0:4].to_broadcast([P, 4, 4, P])
                tt(KSF.rearrange("p h (c b) -> p h c b", c=4), tot0,
                   LF[:, 0:4, :].rearrange("p h (c b) -> p h c b", c=4), SUB).then_inc(S["ks_diff"], 1)
                for d in range(2):
                    ve.wait_ge(S["ks_exp"], w("ks_exp"))
                    tt(KSF, KSF, P2[:, 6 + 4 * d:10 + 4 * d, :], MUL).then_inc(S["ks_ready"], 1)
                ve.wait_ge(S["e_tot"], w("e_tot"))
                for i in range(3):
                    for d in range(2):
                        ve.wait_ge(S["vbank_full"], rd.take())
                        b = rd.bank()
                        if i == 0:
                            ve.tensor_copy(STATE[:, d, 0].rearrange("p h b -> p (h b)"), b[:, :])\
                                .then_inc(S["vbank_free"], 1)
                            continue
                        for h in range(4):
                            col = 4 * (4 * d + h) + CHUNKS[d][i]
                            ins = stt(STATE[:, d, i, h, :], STATE[:, d, i - 1, h, :], ETOT[:, col:col + 1],
                                      b[:, h * P:(h + 1) * P], MUL, ADD)
                            if h < 3:
                                ins.then_inc(S["vec_chain"], st.one())
                        ins.then_inc(S["vbank_free"], 1)
                say(S["st_ready"])
                ve.wait_ge(S["q_silu"], w("q_silu"))

                def halves(v, b_):
                    v = v[:, 0:n].rearrange("p (m s b) -> p m s b", s=2, b=b_)
                    return v[:, :, 0, :], v[:, :, 1, :]

                def level(h, i):
                    q, kf, kb = P2[:, 18 + h, :], P2[:, 6 + h, :], P2[:, 10 + h, :]
                    c = i % 2
                    if i == 2 * LEVELS:
                        tt(LKE[:, c, 0:n], kf[:, 0:n], kb[:, 0:n], ADD).then_inc(S["lvl_ready"], 1)
                        return
                    b_ = 1 << (i % LEVELS)
                    ve.wait_ge(S["lvl_exp"], w("lvl_exp"))
                    ki, qi = (0, 1) if i < LEVELS else (1, 0)
                    e, k = halves(LDF[:, c, :], b_), halves(kf if i < LEVELS else kb, b_)
                    tt(halves(LKE[:, c, :], b_)[ki], k[ki], e[ki], MUL).then_inc(S["vec_chain"], st.one())
                    tt(halves(LQE[:, c, :], b_)[qi], halves(q, b_)[qi], e[qi], MUL).then_inc(S["lvl_ready"], 1)

                for h in range(4):
                    ve.wait_ge(S["qi_exp"], w("qi_exp", 2))
                    tt(QI[:, h % 2, 0, 0:n], QI[:, h % 2, 0, 0:n], P2[:, 18 + h, 0:n], MUL)\
                        .then_inc(S["vec_chain"], st.one())
                    tt(QI[:, h % 2, 1, 0:n], QI[:, h % 2, 1, 0:n], P2[:, 18 + h, 0:n], MUL).then_inc(S["qi_ready"], 1)
                    level(h, 0)
                    for i in range(2 * LEVELS + 1):
                        if i < 2 * LEVELS:
                            level(h, i + 1)
                        m = mask("fwd", i) if i < LEVELS else mask("bwd", i - LEVELS) if i < 2 * LEVELS \
                            else mask("diag")
                        ve.wait_ge(S["vbank_full"], rd.take())
                        b = rd.bank()[:, 0:n].rearrange("p (c t) -> p c t", t=P)
                        ve.wait_ge(S["vbank_free"], rd.n - 1)
                        ve.copy_predicated(ATT[:, h % 2, 0:n // P, :], rep(m, n // P), b).then_inc(S["vbank_free"], 1)
                ve.wait_ge(S["o_rs"], w("o_rs"))
                for h in range(4):
                    o = P2[:, 18 + h, 0:n]
                    stt(o, o, pcol("hgrn_g", l), HRS[:, h, 0:n], MUL, MUL).then_inc(S["vec_chain"], st.one())
                ve.wait_ge(S["vec_chain"], st.n)
                tt(P2[:, 18:22, 0:n], P2[:, 18:22, 0:n], P2[:, 22:26, 0:n], MUL).then_inc(S["hgrn_done"], 1)

                for br in range(3):
                    for half in range(2):
                        i = 2 * br + half
                        rd.tiles_read(("proj", l, br, half))
                        acc = ACC[:, 4 * half:4 * half + 4, 0:n]
                        gb, pb = GB[:, i % 2, :, 0:n], PB[:, i % 2, :, 0:n]
                        if br == 0:
                            tt(acc, gb, pb, MUL).then_inc(S["merge_used"], 1)
                        else:
                            tt(pb, gb, pb, MUL).then_inc(S["vec_chain"], st.one())
                            ve.wait_ge(S["vec_chain"], st.n)
                            tt(acc, acc, pb, ADD).then_inc(S["merge_used"], 1)
                gated(("out2", l), 16)
                say(S["x_ready"])
                adaln(1, n)
                for k in range(DFF2 // P):
                    rd.tiles_read(("ff1", l), k + 1)
                    tt(HF2[:, k, 0:n], HF2[:, k, 0:n], HF2[:, k, 0:n], MUL).then_inc(S["ff_ready"], 1)
                gated(("ff2", l), 40)
                say(S["xo_ready"] if last else S["x_ready"])

        @block.gpsimd
        def _(pool):
            w = Waits()
            pool.dma_start(prm[:, :], par).then_inc(S["par_landed"], 16)
            pool.dma_start(MKF, msk).then_inc(S["mask_landed"], 16)
            pool.memset(PRJ[:, :, 0:1], 0.0).then_inc(S["pad_zero"], 1)
            pool.wait_ge(S["mask_landed"], 16)
            pool.tensor_copy(mk[:, :], MKF).then_inc(S["masks_ready"], 1)
            pool.wait_ge(S["xs_pool"], w("xs_pool"))
            pool.memset(ar(0, 8192), 0.0).then_inc(S["pr_zero"], 1)
            pool.wait_ge(S["x_ready"], w("x_ready"))
            pool.dma_start(WS, wsT.rearrange("g s t -> s g t")).then_inc(S["ws_landed"], 16)
            pool.dma_start(BS[0:1, :], bsr).then_inc(S["ws_landed"], 16)
            pool.dma_start(X[:, :, T:2 * T], ctxT.rearrange("(k p) t -> p k t", p=P)).then_inc(S["ctx_landed"], 16)
            for l in range(2):
                n = 2 * T if l == 0 else T
                pool.wait_ge(S["h_pool"], w("h_pool"))
                pool.memset(VZ[:, :, :, :, :].rearrange("p a b c d -> p (a b c d)"), 0.0).then_inc(S["vz_zero"], 1)
                pool.wait_ge(S["st_ready"], w("st_ready"))
                lvl = 0
                for h in range(4):
                    gf, gb = LF[:, h, 0:n], LF[:, 4 + h, 0:n]
                    tot = TOT.rearrange("p (h c b) -> p h c b", c=4, b=1)[:, 4 + h, 0:n // P, :]
                    pool.tensor_tensor(QI[:, h % 2, 1, 0:n].rearrange("p (c t) -> p c t", t=P),
                                       tot.to_broadcast([P, n // P, P]), gb.rearrange("p (c t) -> p c t", t=P),
                                       ALU.subtract).then_inc(S["qi_diff"], 1)
                    for i in range(2 * LEVELS):
                        b_ = 1 << (i % LEVELS)
                        if lvl >= 2:
                            pool.wait_ge(S["lvl_ready"], LVL_BASE[l] + h * (2 * LEVELS + 1) + i - 1 if i >= 2 else
                                         LVL_BASE[l] + h * (2 * LEVELS + 1) + i - 2)
                        lvl += 1
                        g = (gf if i < LEVELS else gb).rearrange("p (m s b) -> p m s b", s=2, b=b_)
                        dd = LDF[:, i % 2, 0:n].rearrange("p (m s b) -> p m s b", s=2, b=b_)
                        first, second = g[:, :, 0, :], g[:, :, 1, :]
                        mid = (first[:, :, b_ - 1:b_] if i < LEVELS else second[:, :, 0:1])\
                            .to_broadcast([P, n // (2 * b_), b_])
                        pool.tensor_tensor(dd[:, :, 0, :], mid, first, ALU.subtract).then_inc(S["lvl_diff"], 1)
                        pool.tensor_tensor(dd[:, :, 1, :], second, mid, ALU.subtract).then_inc(S["lvl_diff"], 1)
                pool.wait_ge(S["h_pool"], w("h_pool"))


def kernel(**inputs):
    import numpy as np
    import concourse.bacc as bacc
    from concourse.bass_utils import run_bass_kernel_spmd

    a = {k: np.asarray(v) for k, v in inputs.items()}
    f = np.float32

    def cols(v):
        return np.ascontiguousarray(v).reshape(-1, P).T

    def padded(v):
        out = np.zeros((P, 1), f)
        out[:HD, 0] = v
        return out

    def wide(v):
        return np.broadcast_to(np.asarray(v, f).reshape(1, -1), (P, np.size(v)))

    parts = {
        "mu": cols(a["ab_shift_mu"][0]), "w0": cols(a["ab_w0"][0]), "a0": cols(a["ab_a0"][0]),
        "k_k": cols(a["ab_k_k"][0]), "k_a": cols(a["ab_k_a"][0]), "r_k": cols(a["ab_r_k"][0]),
        "lnx_g": cols(a["ab_lnx_g"][0]), "lnx_b": cols(a["ab_lnx_b"][0]),
        "lam_q": np.concatenate([padded(a["ab_lam_q1"][0]), padded(a["ab_lam_q2"][0])], 1),
        "lam_k": np.concatenate([padded(a["ab_lam_k1"][0]), padded(a["ab_lam_k2"][0])], 1),
        "subln_g": cols(a["ab_subln_g"][0]), "c_b_in": cols(a["c_b_in"][0]), "c_ln_g": cols(a["c_ln_g"][0]),
        "c_ln_b": cols(a["c_ln_b"][0]), "ln1_g": cols(a["ln1_g"]), "ln1_b": cols(a["ln1_b"]),
        "ln2_g": cols(a["ln2_g"]), "ln2_b": cols(a["ln2_b"]), "conv_w": cols(a["ffn_conv_w"]),
        "conv_b": cols(a["ffn_conv_b"]),
        "cond": np.stack([cols(a["c_2"][0]), cols(a["c_ctx_2"])], 2).reshape(P, 16),
        "b_mod": cols(a["b_mod_2"]), "norm1_g": cols(a["norm1_g_2"]), "norm2_g": cols(a["norm2_g_2"]),
        "q_norm": np.tile(a["q_norm_g_2"], (1, 2)).T, "k_norm": np.tile(a["k_norm_g_2"], (1, 2)).T,
        "sink": wide(a["attn_sink_2"]), "lb": cols(a["hgrn_lb_logits_2"]), "hgrn_g": a["hgrn_norm_g_2"].T,
        "eps5": wide([1e-5]), "eps6": wide([1e-6]), "eps_gn": wide([64e-5]), "one": wide([1.0]),
        "half": np.stack([np.arange(P) < HD, np.arange(P) >= HD], 1).astype(f),
    }
    par = np.concatenate([parts[n] for n, _ in PARAMS], 1).astype(f)

    i, tok = np.arange(P), np.arange(T)
    same64 = i[:, None] // HD == i[None, :] // HD

    def rope(partner, sign, angle, turned):
        m = np.zeros((P, P), f)
        m[partner[turned], i[turned]] = sign[turned]
        cos = np.where(turned[:, None], np.cos(angle), 1.0)
        sin = np.where(turned[:, None], np.sin(angle), 0.0)
        return m, cos.astype(f), sin.astype(f)

    r = i % HD
    inv = (f(500000.0) ** (-np.arange(0, 16, 2, dtype=f) / f(16))).astype(f)
    rope_a = rope(np.where(r % 16 < 8, i + 8, i - 8), np.where(r % 16 < 8, -1.0, 1.0),
                  (tok.astype(f)[None, :] * inv[r % 8][:, None]).astype(f), r < 16)
    inv = (f(10000.0) ** (-np.arange(0, 32, 2, dtype=f) / f(32))).astype(f)
    place = np.where((r < 32)[:, None], (tok // 64)[None, :], (tok % 64)[None, :]).astype(f)
    rope_b = rope(np.where(r % 32 < 16, i + 16, i - 16), np.where(r % 32 < 16, -1.0, 1.0),
                  (place * inv[r % 16][:, None]).astype(f), r >= 0)
    q = np.arange(2)[None, :, None] * P + i[:, None, None]
    key = tok[None, None, :]
    ad = 2 * np.pi * ((i[:, None] * i[None, :]) % P) / P
    at = 2 * np.pi * ((tok[:, None] * tok[None, :]) % T) / T
    at = at.reshape(2, P, T).transpose(1, 0, 2)
    consts = {
        "ident": np.eye(P), "ones": np.ones((P, P)), "block64": same64,
        "rope_a": rope_a[0], "rope_b": rope_b[0], "cos_a": rope_a[1], "sin_a": rope_a[2],
        "cos_b": rope_b[1], "sin_b": rope_b[2],
        "dup": np.stack([i[:, None] == kv * HD + i[None, :] % HD for kv in range(2)], 1),
        "reset": np.broadcast_to(np.arange(512) % P != 0, (P, 512)),
        "causal": np.where(key <= q, 0.0, -1e30), "window": np.where(abs(key - q) <= P, 0.0, -1e30),
        "dft_d": np.concatenate([np.cos(ad), np.sin(ad)], 1) / np.sqrt(P),
        "dft_t": np.stack([np.cos(at), -np.sin(at)], 2) / np.sqrt(T),
    }
    cst = np.concatenate([np.asarray(consts[n], f).reshape(P, -1) for n, _ in CONSTS], 1)
    s, t = i[:, None], i[None, :]
    fwd = [(s // (2 * b) == t // (2 * b)) & (s % (2 * b) < b) & (t % (2 * b) >= b) for b in 1 << np.arange(LEVELS)]
    masks = {"rwkv": np.concatenate([s < t, s <= t, s < t, s <= t], 1), "fwd": np.concatenate(fwd, 1),
             "bwd": np.concatenate([m.T for m in fwd], 1), "diag": s == t}
    msk = np.concatenate([masks[n] for n, _ in MASKS], 1).astype(f)
    lora = np.zeros((3, P, 512), f)
    lora[0, :HD], lora[1, HD:], lora[2] = a["ab_w2"][0], a["ab_a2"][0], a["ab_g2"][0]

    arrays = {
        "xT": a["x"][0].T, "ctxT": a["ctx_2"][0].T, "par": par, "cst": cst, "msk": msk, "lora": lora,
        "wsT": a["c_w_s"][0].transpose(0, 2, 1), "bsr": a["c_b_s"].reshape(1, -1),
        "ab_w_in": a["ab_w_in"], "ab_w_out": a["ab_w_out"], "c_w_in": a["c_w_in"], "c_w_out": a["c_w_out"],
        "ffn_up": a["ffn_w_up"], "ffn_down": a["ffn_w_down"], "w_mod": a["w_mod_2"], "w_in2": a["w_in_2"],
        "w_branch": a["w_branch_2"], "w_out2": a["w_out_2"], "w_ff1": a["w_ff1_2"], "w_ff2": a["w_ff2_2"],
    }
    arrays = {k: np.ascontiguousarray(v) for k, v in arrays.items()}
    nc = bacc.Bacc("TRN2", target_bir_lowering=False, num_devices=1)
    aps = [nc.dram_tensor(k, v.shape, mybir.dt.from_np(v.dtype), kind="ExternalInput").ap()
           for k, v in arrays.items()]
    out = nc.dram_tensor("out", (D, T), F32, kind="ExternalOutput").ap()
    build(nc, *aps, out)
    res = run_bass_kernel_spmd(nc, [arrays], core_ids=[0])
    return np.ascontiguousarray(res.results[0]["out"].T).reshape(1, T, D)
```

```python
from contextlib import ExitStack

import concourse.bass as bass
from concourse import mybir

F32 = mybir.dt.float32
U8 = mybir.dt.uint8
ALU = mybir.AluOpType
ACT = mybir.ActivationFunctionType
AXX = mybir.AxisListType.X

P = 128
D = 1024
KD = D // P
T = 256
HD = 64
DFF = 2816
NFF = DFF // P
DFF2 = 4096
RWKV_TILES, AB_TILES = 14, 26
STATE_BLOCKS = 7
IN2_TILES = 30
GATE0 = IN2_TILES * P
DEEPNORM = (2 * 2) ** 0.25
LAM_INIT = 0.2
SCALE = HD ** -0.5
EXP_MINUS_HALF = 0.6065306597126334
LN_FLOOR = -69.07755278982137
LN_SMALL = 1e-15
LN_LN_SMALL = -34.538776394910684
LEVELS = 7

CHUNKS = ((2, 3, 0), (3, 2, 1))
ENTERS = ({3: 0, 0: 1, 1: 2}, {2: 0, 1: 1, 0: 2})
MOD_BLOCKS = 6 * D // 256
LVL_BASE = (0, 4 * (LEVELS + 1))
RING, BLK = 4, 256
NBANK = 4

PARAMS = [("mu", 14), ("w0", 4), ("a0", 4), ("k_k", 4), ("k_a", 4), ("r_k", 4), ("lnx_g", 4), ("lnx_b", 4),
          ("lam_q", 2), ("lam_k", 2), ("subln_g", 1), ("c_b_in", 16), ("c_ln_g", 8), ("c_ln_b", 8),
          ("ln1_g", 16), ("ln1_b", 16), ("ln2_g", 16), ("ln2_b", 16), ("conv_w", 6 * NFF), ("conv_b", 2 * NFF),
          ("cond", 16), ("b_mod", 96), ("norm1_g", 16), ("norm2_g", 16), ("q_norm", 2), ("k_norm", 2),
          ("sink", 16), ("lb", 16), ("hgrn_g", 2), ("eps5", 1), ("eps6", 1), ("eps_gn", 1), ("one", 1), ("half", 2)]
PCOL, NPAR = {}, 0
for _name, _n in PARAMS:
    PCOL[_name] = NPAR
    NPAR += _n

CONSTS = [("ident", 128), ("ones", 128), ("block64", 128), ("rope_a", 128), ("rope_b", 128), ("dup", 256),
          ("cos_a", 256), ("sin_a", 256), ("cos_b", 256), ("sin_b", 256), ("reset", 512),
          ("causal", 512), ("window", 512), ("dft_d", 256), ("dft_t", 1024)]
CCOL, NCONST = {}, 0
for _name, _n in CONSTS:
    CCOL[_name] = NCONST
    NCONST += _n
MASKS = [("rwkv", 512), ("fwd", LEVELS * 128), ("bwd", LEVELS * 128), ("diag", 128),
         ("pairs", LEVELS * 128)]
MCOL, NMASK = {}, 0
for _name, _n in MASKS:
    MCOL[_name] = NMASK
    NMASK += _n


class Gemm:

    def __init__(self, w, blocks, col, n, groups=((0, 8),), nf=2, width=None):
        self.w, self.blocks, self.col, self.n, self.groups, self.nf = w, blocks, col, n, groups, nf
        self.width = width or nf * P
        self.g = len(groups)
        self.unroll = 1
        while self.unroll * self.g % RING or self.unroll * nf % NBANK:
            self.unroll += 1


def plan(gemms):
    chunk = step = tile = 0
    ends = []
    for g in gemms:
        g.chunk0, g.step0, g.tile0 = chunk, step, tile
        for _ in range(g.blocks * g.g):
            step += g.nf
            ends.append(step)
        chunk += g.blocks * g.g
        tile += g.blocks * g.nf
    return ends


class Waits:

    def __init__(self):
        self.seen = {}

    def __call__(self, name, n=1):
        self.seen[name] = self.seen.get(name, 0) + n
        return self.seen[name]


class Steps:

    def __init__(self):
        self.n = 0

    def one(self):
        self.n += 1
        return 1


SEMS = """
x_landed par_landed const_landed mask_landed lora_landed ws_landed ctx_landed out_landed
gemm_step tile_free vbank_full vbank_free abank_full abank_free vec_chain act_chain pool_chain
cond_silu lb_shifted lb_exp lb_floored lb_ln lam_prod lam_exp pad_zero
rope_ready scores_ready exp_ready attn_ready o_squares o_rstd yd_ready
masks_ready inv_first xs_ready xs_pool hats_act h_pool lora_in decay_ready a_ready g_out log_ready exp_factors kk_squares kk_root hats_ready pr_zero inv_init
gn_sq gn_rstd bonus_in yr_ready centered squared rstd_ready x_ready ln_tile
conv_ready silu_ready hid_ready mix_in
xsq_ready xrstd_ready h_ready n_squares n_rstd qk_ready qz_ready w_scores w_exp w_probs vz_zero
sp_first sp_sum sp_second k_raw dir_done tot_ready e_tot lf_ready ks_diff ks_exp ks_ready st_ready
lvl_diff lvl_exp lvl_ready qi_diff qi_exp qi_ready q_silu o_sq o_rs hgrn_done
merge_used ff_ready xo_ready
""".split()


def build(nc, xT, ctxT, par, cst, msk, lora, wsT, bsr, ab_w_in, ab_w_out, c_w_in, c_w_out, ffn_up, ffn_down,
          w_mod, w_in2, w_branch, w_out2, w_ff1, w_ff2, out):
    down_groups = ((0, 8), (8, 8), (16, 6))
    G = {}
    G["ab_in"] = Gemm(ab_w_in[0], 13, lambda b, u: b * BLK, T)
    G["ab_out"] = Gemm(ab_w_out[0], 4, lambda b, u: b * BLK, T)

    def up_col(b, u):
        return (b - u) * (BLK // 2) + (u // 2) * BLK + (u % 2) * DFF

    order = ["ab_in", ("mod", 0), "ab_out"]
    for l in range(2):
        G["up", l] = Gemm(ffn_up[l], 22, up_col, T)
        G["down", l] = Gemm(ffn_down[l], 4, lambda b, u: b * BLK, T, down_groups)
    G["c_in"] = Gemm(c_w_in[0], 8, lambda b, u: b * BLK, T)
    G["c_out"] = Gemm(c_w_out[0], 4, lambda b, u: b * BLK, T)
    order += [("up", 0), ("down", 0), "c_in", "c_out", ("up", 1), ("down", 1)]
    for l in range(2):
        full = 2 * T if l == 0 else T
        G["mod", l] = Gemm(w_mod[l], MOD_BLOCKS, lambda b, u: b * BLK, BLK, nf=1, width=BLK)
        G["in_state", l] = Gemm(w_in2[l], STATE_BLOCKS, lambda b, u: b * BLK, 2 * T)
        G["in_rest", l] = Gemm(w_in2[l], 15 - STATE_BLOCKS, lambda b, u: (b + STATE_BLOCKS) * BLK, full)
        order += [("in_state", l), ("in_rest", l)] + [("mod", 1)] * (l == 0)
        for n in range(3):
            for half in range(2):
                G["gate", l, n, half] = Gemm(
                    w_in2[l], 2, lambda b, u, c=GATE0 + n * D + half * 512: c + b * BLK, full)
                G["proj", l, n, half] = Gemm(
                    w_branch[l, n], 1, lambda b, u, c=half * 512: c, full, ((0, 4),), 4)
                order += [("gate", l, n, half), ("proj", l, n, half)]
        G["out2", l] = Gemm(w_out2[l], 4, lambda b, u: b * BLK, full)
        G["ff1", l] = Gemm(w_ff1[l], 16, lambda b, u: b * BLK, full)
        G["ff2", l] = Gemm(w_ff2[l], 4, lambda b, u: b * BLK, full, ((0, 8), (8, 8), (16, 8), (24, 8)))
        order += [("out2", l), ("ff1", l), ("ff2", l)]
    chunk_end = plan([G[o] for o in order])

    with ExitStack() as ctx:
        def sb(name, shape, dt=F32):
            return ctx.enter_context(nc.sbuf_tensor(name, shape, dt))

        ring = sb("ring", [P, RING, 8 * BLK])
        X = sb("X", [P, KD, 2 * T])
        arena = sb("arena", [P, 32768])
        prm = sb("prm", [P, NPAR])
        con = sb("con", [P, NCONST])
        mk = sb("mk", [P, NMASK], U8)
        sm = sb("sm", [P, 512])
        mod_row = sb("mod_row", [2, 2, BLK])
        bank = [ctx.enter_context(nc.psum_tensor(f"bank{i}", [P, 512], F32)) for i in range(NBANK)]
        vbank = [ctx.enter_context(nc.psum_tensor(f"vbank{i}", [P, 512], F32)) for i in range(2)]
        abank = [ctx.enter_context(nc.psum_tensor(f"abank{i}", [P, 512], F32)) for i in range(2)]
        S = {n: ctx.enter_context(nc.semaphore(n)) for n in SEMS}
        landed = [ctx.enter_context(nc.semaphore(f"slot_landed{i}")) for i in range(RING)]
        block = ctx.enter_context(nc.Block())

        def ar(off, *shape):
            n = 1
            for s in shape:
                n *= s
            v = arena[:, off:off + n]
            if len(shape) == 1:
                return v
            names = "abcde"[:len(shape)]
            return v.rearrange(f"p ({' '.join(names)}) -> p {' '.join(names)}",
                               **{c: s for c, s in zip(names, shape)})

        def pcol(name, i=0, n=1):
            return prm[:, PCOL[name] + i:PCOL[name] + i + n]

        def cc(name, *shape):
            n = dict(CONSTS)[name]
            v = con[:, CCOL[name]:CCOL[name] + n]
            if shape:
                names = "abcd"[:len(shape)]
                v = v.rearrange(f"p ({' '.join(names)}) -> p {' '.join(names)}", **{c: s for c, s in zip(names, shape)})
            return v

        def mask(name, i=0, n=128):
            return mk[:, MCOL[name] + i * 128:MCOL[name] + i * 128 + n]

        def rep(ap, n):
            return ap.unsqueeze(1).to_broadcast([P, n, ap.shape[-1]])

        ident, ones, block64 = cc("ident"), cc("ones"), cc("block64")

        PRJ = ar(0, AB_TILES, T + 1)
        PR = ar(0, 16, 4, P)
        XS = ar(8192, RWKV_TILES, T)
        DT = ar(11776, RWKV_TILES, T)
        GG, BH, KH = ar(11776, 4, T), ar(12800, 4, T), ar(13824, 4, T)
        TW, SG = ar(14848, T), ar(15104, T)
        LD, AA, LL, LP = (ar(15360 + 1024 * i, 4, T) for i in range(4))
        E1, E2, E3, KK = (ar(19456 + 1024 * i, 4, T) for i in range(4))
        KSQ, BON = ar(23552, 4, T), ar(15360, 4, T)
        XI, YI, T1 = (ar(15360 + 2048 * i, 16, P) for i in range(3))
        RH, UU, SB = ar(21504, 512), ar(22016, 2, 512), ar(23040, 4, P)
        AR = ar(23552, 8, 2, P)
        BZ, KZ = ar(25600, 4, 2, T), ar(27648, 4, 2, T)
        WL = ar(27648, 3, 512)
        VT, BT, KT = ar(29696, 2, 512), ar(30720, 512), ar(31232, 512)
        YT, YF = ar(25600, 2, 512), ar(26624, 4, T)
        GSQ, GRS = ar(27648, 4, T), ar(28672, 4, T)
        MKF = ar(20480, NMASK)
        QZ1, KR1, R2, R3 = ar(15360, 4, 2, T), ar(17408, 4, T), ar(18432, 2, T), ar(18944, 2, T)
        VT1 = ar(19456, 2, 4, P)
        SM1, EE1, AT1 = ar(20480, 2, 2, T), ar(21504, 2, 2, T), ar(22528, 2, T)
        PT1, OO1, OSQ, ORS = ar(23552, 2, 2, T), ar(24576, 4, T), ar(25600, 4, T), ar(26624, 4, T)
        YAB = X[:, :, T:2 * T]
        Z, ZSQ, ZRS = ar(0, KD, T), ar(2048, KD, T), ar(4096, T)
        HF = ar(8192, NFF, T)
        GP = ar(14336, 4, T + 2)
        CV, VAL = ar(15872, 4, T), ar(16896, 4, T)
        UV = ar(8192, 16, T)
        WS, BS = ar(20480, 8, P), ar(21504, 1024)
        VTC, MU = ar(14336, 2, 1024), ar(18432, 8, T)
        P2 = ar(0, IN2_TILES, 2 * T)
        SCR = 15360
        HB = ar(28672, KD, 2 * T)
        XSQ = ar(24576, KD, 2 * T)
        XRS = ar(23552, 2 * T)
        KZ2, VZ = ar(SCR + 4096, 2, 2, 2 * T), ar(SCR + 6144, 4, 2, 2, P)
        SM2 = ar(SCR + 8192, 2, 2, 2 * T)
        PT2 = ar(SCR + 10240, 2, 4, T)
        NSQ = NRS = ar(SCR + 10240, 5, 2 * T)
        RT = ar(SCR + 8192, 2, T)
        FB = ar(SCR + 12288, 2, 2, 2, P)
        LF = ar(SCR, 8, 2 * T)
        TA, TB, TC, TD = (ar(SCR + 4096 + 2048 * i, 4, 2 * T) for i in range(4))
        VTK = ar(SCR + 4096, 4, 4, P)
        KST = ar(SCR + 6144, 2, 3, 4, P)
        KSF = ar(SCR + 9216, 4, 2 * T)
        LDF = ar(SCR + 8192, 2, 2, 2 * T)
        LQE, LKE = (ar(SCR + 10240 + 1024 * i, 2, 2 * T) for i in range(2))
        ATT = ar(SCR + 12288, 2, 4, P)
        QI = ar(SCR + 6144, 2, 2, 2 * T)
        HSQ, HRS = ar(SCR + 9216, 4, 2 * T), ar(SCR + 6144, 4, 2 * T)
        ACC = ar(SCR, KD, 2 * T)
        GB, PB = ar(SCR + 4096, 2, 4, 2 * T), ar(SCR + 8192, 2, 4, 2 * T)
        HF2 = ar(0, DFF2 // P, 2 * T)
        STATE = ar(0, 2, 3, 4, P)
        GATE0B = P2[:, 6:10, :]

        MOD = [sm[:, 96 * l:96 * l + 96].rearrange("p (a b) -> p a b", b=2) for l in range(2)]
        SC = [sm[:, 192 + 16 * i:208 + 16 * i].rearrange("p (a b) -> p a b", b=2) for i in range(4)]
        CS = sm[:, 256:272]
        LAMP, NLAM, OMKA = sm[:, 272:274], sm[:, 275:276], sm[:, 276:280]
        LAME, G08, LAME2 = sm[:, 280:282], sm[:, 282:283], sm[:, 440:442]
        GMS = sm[:, 442:450]
        EGM, FST = sm[:, 284:292], sm[:, 292:296]
        MX, NM, SU = sm[:, 296:300], sm[:, 300:304], sm[:, 304:308]
        ES = sm[:, 308:312]
        TOT, ETOT = sm[:, 312:344], sm[:, 344:376]
        LB, OMLB, LLB, LBT = (sm[:, 376 + 16 * i:392 + 16 * i] for i in range(4))

        def rows(w, k0, nk, c0, n):
            v = w.rearrange("(k p) f -> p k f", p=P)
            return v[:, k0:k0 + nk, bass.ds(c0, n)]

        def each_block(eng, g, emit, peel):
            rounds = g.blocks // g.unroll
            first = min(peel, rounds)
            for i in range(first):
                for u in range(g.unroll):
                    emit(i, u)
            if rounds - first >= 2:
                with eng.Fori(first, rounds, 1) as i:
                    for u in range(g.unroll):
                        emit(i, u)
            else:
                for i in range(first, rounds):
                    for u in range(g.unroll):
                        emit(i, u)
            for u in range(g.blocks - rounds * g.unroll):
                emit(rounds, u)

        @block.sync
        def _(sp):
            def stream(g):
                per_round = g.unroll * g.g

                def emit(i, u):
                    for n, (k0, nk) in enumerate(g.groups):
                        c = g.chunk0 + u * g.g + n
                        slot = c % RING
                        if isinstance(i, int):
                            cc_ = c + i * per_round
                            if cc_ >= RING:
                                sp.wait_ge(S["gemm_step"], chunk_end[cc_ - RING])
                        else:
                            done = g.step0 + (c - RING - g.chunk0 + 1) * g.nf
                            sp.wait_ge(S["gemm_step"], i * (per_round * g.nf) + done)
                        width = g.width
                        col = g.col(i * g.unroll + u, u)
                        dst = ring[:, slot, 0:nk * width].rearrange("p (k f) -> p k f", f=width)
                        sp.dma_start(dst, rows(g.w, k0, nk, col, width)).then_inc(landed[slot], 16)

                each_block(sp, g, emit, 1)

            for o in order:
                stream(G[o])
            w = Waits()
            sp.wait_ge(S["xo_ready"], w("xo_ready"))
            sp.dma_start(out.rearrange("(k p) t -> p k t", p=P), X[:, :, 0:T]).then_inc(S["out_landed"], 16)
            sp.wait_ge(S["out_landed"], 16)

        @block.tensor
        def _(pe):
            w = Waits()
            jobs = {"v": 0, "a": 0}

            def take(kind):
                n = jobs[kind]
                jobs[kind] += 1
                if n >= 2:
                    pe.wait_ge(S[kind + "bank_free"], n - 1)
                return (vbank if kind == "v" else abank)[n % 2]

            def post(kind, ins):
                ins.then_inc(S[kind + "bank_full"], 1)
                return jobs[kind]

            def gemm(key, act, wait_free=True, by_tile=None):
                g = G[key]
                ready = w(by_tile, KD) - KD if by_tile else 0
                if wait_free and g.tile0:
                    pe.wait_ge(S["tile_free"], g.tile0)
                per_round = g.unroll * g.g

                def emit(i, u):
                    for n, (k0, nk) in enumerate(g.groups):
                        c = g.chunk0 + u * g.g + n
                        slot = c % RING
                        pe.wait_ge(landed[slot], i * (16 * per_round // RING) + 16 * (c // RING + 1))
                        if by_tile and isinstance(i, int) and i == 0 and u == 0:
                            wt = ring[:, slot, 0:nk * g.nf * P].rearrange("p (k f) -> p k f", k=nk)
                            for k in range(nk):
                                pe.wait_ge(S[by_tile], ready + k + 1)
                                for f in range(g.nf):
                                    mm = pe.matmul(bank[(g.tile0 + f) % NBANK][:, 0:g.n], wt[:, k, f * P:(f + 1) * P],
                                                   act(k), start=(k == 0), stop=(k == nk - 1))
                                    if k == nk - 1:
                                        mm.then_inc(S["gemm_step"], 1)
                            continue
                        for f in range(g.nf):
                            t = g.tile0 + u * g.nf + f
                            if n == 0 and (not isinstance(i, int) or t + i * g.unroll * g.nf >= NBANK):
                                pe.wait_ge(S["tile_free"], i * (g.unroll * g.nf) + t - NBANK + 1)
                            wt = ring[:, slot, 0:nk * g.nf * P].rearrange("p (k f) -> p k f", k=nk)
                            for k in range(nk):
                                mm = pe.matmul(bank[t % NBANK][:, 0:g.n], wt[:, k, f * P:(f + 1) * P],
                                               act(k0 + k), start=(n == 0 and k == 0),
                                               stop=(n == g.g - 1 and k == nk - 1))
                            mm.then_inc(S["gemm_step"], 1)

                each_block(pe, g, emit, 1 if g.tile0 == 0 or by_tile else 0)

            def mod_fill(l, k):
                g = G["mod", l]
                if 2 <= k < g.blocks + 2:
                    pe.wait_ge(S["tile_free"], g.tile0 + k - 1)
                    b = take("v")
                    for i in range(2):
                        mm = pe.transpose(b[:, 2 * i:2 * i + 2], mod_row[:, k % 2, i * P:(i + 1) * P], ident[0:2, 0:2])
                    post("v", mm)
                if k < g.blocks:
                    c, t = g.chunk0 + k, g.tile0 + k
                    pe.wait_ge(landed[c % RING], 16 * (c // RING + 1))
                    pe.wait_ge(S["tile_free"], t - NBANK + 1)
                    wt = ring[:, c % RING, :].rearrange("p (k f) -> p k f", k=KD)
                    for i in range(KD):
                        mm = pe.matmul(bank[t % NBANK][0:2, 0:BLK], CS[:, 2 * i:2 * i + 2], wt[:, i, :],
                                       start=(i == 0), stop=(i == KD - 1))
                    mm.then_inc(S["gemm_step"], 1)

            def column_sum(kind, src, n, mat=ones):
                b = take(kind)
                for k in range(KD):
                    mm = pe.matmul(b[:, 0:n], mat, src(k), start=(k == 0), stop=(k == KD - 1))
                post(kind, mm)

            def one(kind, lhs, rhs, n):
                b = take(kind)
                post(kind, pe.matmul(b[:, 0:n], lhs, rhs, start=True, stop=True))

            def turn(kind, srcs):
                b = take(kind)
                for i, s in enumerate(srcs):
                    mm = pe.transpose(b[:, i * P:(i + 1) * P], s, ident)
                post(kind, mm)

            def layer_norm(z, key):
                pe.wait_ge(S["tile_free"], G[key].tile0 + G[key].blocks * G[key].nf)
                column_sum("v", z, T)
                b = take("a")
                for k in range(KD):
                    pe.wait_ge(S["squared"], w("squared"))
                    mm = pe.matmul(b[:, 0:T], ones, ZSQ[:, k, :], start=(k == 0), stop=(k == KD - 1))
                post("a", mm)

            def rms(n):
                b = take("a")
                for k in range(KD):
                    pe.wait_ge(S["xsq_ready"], w("xsq_ready"))
                    mm = pe.matmul(b[:, 0:n], ones, XSQ[:, k, 0:n], start=(k == 0), stop=(k == KD - 1))
                post("a", mm)

            pe.wait_ge(S["const_landed"], 16)
            pe.wait_ge(S["x_landed"], 16)
            gemm("ab_in", lambda k: X[:, k, 0:T])

            pe.wait_ge(S["cond_silu"], w("cond_silu"))

            pe.wait_ge(S["lam_prod"], w("lam_prod"))
            one("a", ones, LAMP, 2)
            pe.wait_ge(S["tile_free"], AB_TILES)
            for i in range(4):
                b = take("v")
                for j in range(2):
                    mm = pe.matmul(b[:, j * T:(j + 1) * T], cc("rope_a"), PRJ[:, 14 + 2 * i + j, 1:T + 1],
                                   start=True, stop=True)
                post("v", mm)
            for j in range(2):
                turn("a", [PRJ[:, 22 + h, 1 + j * P:1 + (j + 1) * P] for h in range(4)])
            pe.wait_ge(S["rope_ready"], w("rope_ready"))

            def score(u):
                h, qt = u // 2, u % 2
                b = take("v")
                for c in range(2):
                    mm = pe.matmul(b[:, c * T:(c + 1) * T], QZ1[:, h, c, qt * P:(qt + 1) * P], KR1[:, h, :],
                                   start=True, stop=True)
                post("v", mm)

            score(0)
            pe.wait_ge(S["abank_free"], jobs["a"])
            for u in range(8):
                h, qt = u // 2, u % 2
                if u < 7:
                    score(u + 1)
                mod_fill(0, u)
                pe.wait_ge(S["attn_ready"], w("attn_ready"))
                turn("a", [AT1[:, u % 2, k * P:(k + 1) * P] for k in range(2)])
                if qt == 1:
                    pe.wait_ge(S["abank_free"], jobs["a"])
                    b = take("v")
                    for k in range(2):
                        mm = pe.matmul(b[:, 0:T], VT1[:, k, h, :], PT1[:, h % 2, k, :], start=(k == 0), stop=(k == 1))
                    post("v", mm)
            pe.wait_ge(S["o_squares"], w("o_squares"))
            for i in range(2):
                one("a", ones, OSQ[:, 2 * i:2 * i + 2, :], 512)

            for k in range(8, 12):
                mod_fill(0, k)
            pe.wait_ge(S["lora_in"], w("lora_in", 2))
            pe.wait_ge(S["lora_landed"], 16)
            for i, src in ((0, TW), (1, XS[:, 12, :]), (2, SG)):
                for f in range(2):
                    b = take("a")
                    for j in range(2):
                        mm = pe.matmul(b[:, j * T:(j + 1) * T], WL[:, i, (2 * f + j) * P:(2 * f + j + 1) * P], src,
                                       start=True, stop=True)
                    post("a", mm)
            pe.wait_ge(S["kk_squares"], w("kk_squares"))
            for i in range(2):
                one("a", block64, KSQ[:, 2 * i:2 * i + 2, :], 512)
            for k in range(12, MOD_BLOCKS + 2):
                mod_fill(0, k)
            pe.wait_ge(S["hats_ready"], w("hats_ready"))
            for j in range(2):
                turn("a", [XS[:, 8 + t, j * P:(j + 1) * P] for t in range(4)])
            turn("a", [BH[:, t, 0:P] for t in range(4)])
            turn("a", [KH[:, t, 0:P] for t in range(4)])
            pe.wait_ge(S["pr_zero"], w("pr_zero"))
            for u in range(16):
                h, j = u // 2, u % 2
                t, par = h // 2, h % 2
                b = take("v")
                rhs = AR[:, 2 * t + j, :, :]
                pe.matmul(b[:, 0:256], BZ[:, t, par, j * P:(j + 1) * P], rhs, start=True, stop=True)
                post("v", pe.matmul(b[:, 256:512], KZ[:, t, par, j * P:(j + 1) * P], rhs, start=True, stop=True))
            pe.wait_ge(S["inv_init"], w("inv_init", 2))
            pe.wait_ge(S["vbank_free"], jobs["v"])
            y_in, t1_in = [0] * 4, [0] * 4
            for l in range(LEVELS):
                for q in range(4):
                    if l == 1:
                        pe.wait_ge(S["inv_first"], w("inv_first"))
                    elif l:
                        pe.wait_ge(S["vbank_free"], y_in[q])
                    b = take("v")
                    for i in range(4):
                        u = 4 * q + i
                        mm = pe.matmul(b[:, i * P:(i + 1) * P], PR[:, u, 0, :], XI[:, u, :], start=True, stop=True)
                    t1_in[q] = post("v", mm)
                for q in range(4 if l else 0):
                    pe.wait_ge(S["vbank_free"], t1_in[q])
                    if l < LEVELS - 1:
                        b = take("v")
                        for i in range(4):
                            u = 4 * q + i
                            mm = pe.matmul(b[:, i * P:(i + 1) * P], YI[:, u, :], T1[:, u, :], start=True, stop=True)
                        post("v", mm)
                    b = take("v")
                    for i in range(4):
                        u = 4 * q + i
                        mm = pe.matmul(b[:, i * P:(i + 1) * P], T1[:, u, :], YI[:, u, :], start=True, stop=True)
                    y_in[q] = post("v", mm)
            pe.wait_ge(S["vbank_free"], jobs["v"])
            pe.wait_ge(S["abank_free"], jobs["a"])

            def head(h):
                return slice(h * HD, (h + 1) * HD)

            def solve(j):
                b = take("a")
                for h in range(8):
                    mm = pe.matmul(b[:, head(h)], YI[:, 2 * h + j, :], RH[:, head(h)], start=True, stop=True)
                post("a", mm)

            def outputs(j):
                b = take("a")
                for t in range(4):
                    if j:
                        pe.matmul(b[:, t * P:(t + 1) * P], AR[:, 2 * t + 1, 1, :], SB[:, t, :],
                                  start=True, stop=False, skip_group_check=True)
                    for h in (2 * t, 2 * t + 1):
                        pe.matmul(b[:, head(h)], PR[:, 2 * h + j, 1, :], UU[:, j, head(h)],
                                  start=(j == 0), stop=False, skip_group_check=True)
                        mm = pe.matmul(b[:, head(h)], PR[:, 2 * h + j, 3, :], VT[:, j, head(h)],
                                       start=False, stop=True, skip_group_check=True)
                post("a", mm)

            b = take("a")
            for h in range(8):
                mm = pe.matmul(b[:, head(h)], PR[:, 2 * h, 2, :], VT[:, 0, head(h)], start=True, stop=True)
            post("a", mm)
            pe.wait_ge(S["abank_free"], jobs["a"])
            solve(0)
            pe.wait_ge(S["abank_free"], jobs["a"])
            b = take("v")
            for t in range(4):
                pe.matmul(b[:, t * P:(t + 1) * P], BT[:, t * P:(t + 1) * P], UU[:, 0, t * P:(t + 1) * P],
                          start=True, stop=False)
                mm = pe.matmul(b[:, t * P:(t + 1) * P], KT[:, t * P:(t + 1) * P], VT[:, 0, t * P:(t + 1) * P],
                               start=False, stop=True)
            post("v", mm)
            outputs(0)
            pe.wait_ge(S["vbank_free"], jobs["v"])
            b = take("a")
            for t in range(4):
                pe.matmul(b[:, t * P:(t + 1) * P], AR[:, 2 * t + 1, 0, :], SB[:, t, :],
                          start=True, stop=False, skip_group_check=True)
                for h in (2 * t, 2 * t + 1):
                    mm = pe.matmul(b[:, head(h)], PR[:, 2 * h + 1, 2, :], VT[:, 1, head(h)],
                                   start=False, stop=True, skip_group_check=True)
            post("a", mm)
            pe.wait_ge(S["abank_free"], jobs["a"])
            solve(1)
            pe.wait_ge(S["abank_free"], jobs["a"])
            outputs(1)
            pe.wait_ge(S["abank_free"], jobs["a"])
            for j in range(2):
                turn("a", [YT[:, j, t * P:(t + 1) * P] for t in range(4)])
            pe.wait_ge(S["abank_free"], jobs["a"])
            for i in range(2):
                one("v", block64, YF[:, 2 * i:2 * i + 2, :], 512)
            pe.wait_ge(S["gn_sq"], w("gn_sq"))
            for i in range(2):
                one("a", block64, GSQ[:, 2 * i:2 * i + 2, :], 512)
            pe.wait_ge(S["bonus_in"], w("bonus_in"))
            for i in range(2):
                one("v", block64, BON[:, 2 * i:2 * i + 2, :], 512)
            pe.wait_ge(S["yr_ready"], w("yr_ready"))
            pe.wait_ge(S["yd_ready"], w("yd_ready"))
            gemm("ab_out", lambda k: YAB[:, k, :])
            layer_norm(lambda k: Z[:, k, :], "ab_out")

            def ffn(l):
                gemm(("up", l), lambda k: X[:, k, 0:T], by_tile="ln_tile")
                pe.wait_ge(S["hid_ready"], w("hid_ready", NFF))
                gemm(("down", l), lambda k: HF[:, k, :])
                layer_norm(lambda k: Z[:, k, :], ("down", l))

            ffn(0)
            gemm("c_in", lambda k: X[:, k, 0:T], by_tile="ln_tile")
            layer_norm(lambda k: UV[:, 8 + k, :], "c_in")
            pe.wait_ge(S["ln_tile"], w("ln_tile", KD))
            for j in range(2):
                for q in range(2):
                    turn("a", [UV[:, 8 + 4 * q + g, j * P:(j + 1) * P] for g in range(4)])
            pe.wait_ge(S["mix_in"], w("mix_in"))
            pe.wait_ge(S["abank_free"], jobs["a"])
            for j in range(2):
                for q in range(2):
                    b = take("v")
                    for i in range(4):
                        g = 4 * q + i
                        pe.matmul(b[:, i * P:(i + 1) * P], ones[0:1, :], BS[0:1, g * P:(g + 1) * P],
                                  start=True, stop=False)
                        mm = pe.matmul(b[:, i * P:(i + 1) * P], VTC[:, j, g * P:(g + 1) * P], WS[:, g, :],
                                       start=False, stop=True)
                    post("v", mm)
            pe.wait_ge(S["vbank_free"], jobs["v"])
            gemm("c_out", lambda k: MU[:, k, :])
            layer_norm(lambda k: Z[:, k, :], "c_out")
            ffn(1)

            for l in range(2):
                last = l == 1
                n = T if last else 2 * T
                rms(2 * T)
                gemm(("in_state", l), lambda k: HB[:, k, :], by_tile="h_ready")
                gemm(("in_rest", l), lambda k, n=n: HB[:, k, 0:n])
                pe.wait_ge(S["tile_free"], G["in_rest", l].tile0 + 2 * G["in_rest", l].blocks)

                pe.wait_ge(S["n_squares"], w("n_squares", 2))
                for i in range(5):
                    m = n if i < 4 else 2 * T
                    one("a", block64, NSQ[:, i, 0:m], m)
                pe.wait_ge(S["qk_ready"], w("qk_ready"))
                for i in range(5):
                    one("v", cc("rope_b"), P2[:, (14 + i) if i < 4 else 0, 0:T], T)
                turn("v", [P2[:, 1, c * P:(c + 1) * P] for c in range(4)])
                pe.wait_ge(S["qz_ready"], w("qz_ready"))
                for kv in range(2):
                    one("a", cc("dup", 2, P)[:, kv, :], P2[:, 0, :], 2 * T)
                pe.wait_ge(S["abank_free"], jobs["a"])
                pe.wait_ge(S["vbank_free"], jobs["v"])
                units = [(s, t, h) for s in range(2 if not last else 1) for t in range(4) for h in range(2)]

                def wscore(s, t, h):
                    lhs = [P2[:, 14 + t, s * T + q * P:s * T + (q + 1) * P] for q in range(2)]
                    if s == 0:
                        for q in range(2):
                            one("v", lhs[q], KZ2[:, t // 2, h, :], 2 * T)
                    else:
                        b = take("v")
                        for q in range(2):
                            mm = pe.matmul(b[:, q * T:(q + 1) * T], lhs[q], KZ2[:, t // 2, h, T:2 * T],
                                           start=True, stop=True)
                        post("v", mm)

                wscore(*units[0])
                for i, (s, t, h) in enumerate(units):
                    if i + 1 < len(units):
                        wscore(*units[i + 1])
                    fill = l == 0 and 2 * i < MOD_BLOCKS + 2
                    if fill:
                        mod_fill(1, 2 * i)
                    pe.wait_ge(S["w_probs"], w("w_probs", 2))
                    nk = 4 if s == 0 else 2
                    for k0 in range(0, nk, 2):
                        turn("a", [SM2[:, i % 2, q, k * P:(k + 1) * P] for k in (k0, k0 + 1) for q in range(2)])
                    if fill:
                        mod_fill(1, 2 * i + 1)
                    if h == 1:
                        pe.wait_ge(S["abank_free"], jobs["a"])
                        b = take("v")
                        for hh in range(2):
                            for k in range(nk):
                                c = k + (4 - nk)
                                mm = pe.matmul(b[:, 0:T], VZ[:, c, t // 2, hh, :], PT2[:, hh, k, :],
                                               start=(hh == 0 and k == 0), stop=(hh == 1 and k == nk - 1))
                        post("v", mm)

                for s in range(1 if last else 2):
                    for g in range(4):
                        b = take("a")
                        for j in range(2):
                            c0 = s * T + j * P
                            mm = pe.matmul(b[:, j * T:(j + 1) * T], P2[:, 26 + g, c0:c0 + P], cc("dft_d"),
                                           start=True, stop=True)
                        post("a", mm)
                        pe.wait_ge(S["abank_free"], jobs["a"])
                        i = (s * 4 + g) % 2
                        b = take("v")
                        for j in range(2):
                            for m in range(2):
                                mm = pe.matmul(b[:, 0:T], FB[:, i, j, m, :], cc("dft_t", 2, 2, T)[:, j, m, :],
                                               start=(j == 0 and m == 0), stop=(j == 1 and m == 1))
                        post("v", mm)

                pe.wait_ge(S["lf_ready"], w("lf_ready"))
                for c in range(4):
                    turn("a", [P2[:, 2 + h, c * P:(c + 1) * P] for h in range(4)])
                for d in range(2):
                    pe.wait_ge(S["ks_ready"], w("ks_ready"))
                    for c in CHUNKS[d]:
                        turn("a", [KSF[:, h, c * P:(c + 1) * P] for h in range(4)])
                pe.wait_ge(S["abank_free"], jobs["a"])
                for st in range(3):
                    for d in range(2):
                        b = take("v")
                        for h in range(4):
                            mm = pe.matmul(b[:, h * P:(h + 1) * P], KST[:, d, st, h, :],
                                           VTK[:, CHUNKS[d][st], h, :], start=True, stop=True)
                        post("v", mm)
                nc_ = n // P
                for h in range(4):
                    for i in range(LEVELS + 1):
                        pe.wait_ge(S["lvl_ready"], w("lvl_ready"))
                        b = take("v")
                        for c in range(nc_):
                            tok = slice(c * P, (c + 1) * P)
                            rhs = LQE[:, i % 2, tok] if i < LEVELS else P2[:, 18 + h, tok]
                            mm = pe.matmul(b[:, tok], LKE[:, i % 2, tok], rhs, start=True, stop=True)
                        post("v", mm)
                        g = G["gate", l, 0, 0]
                        c, t = g.chunk0 + h // 2, g.tile0 + h
                        if h == 0 and i == 0:
                            pe.wait_ge(S["tile_free"], g.tile0)
                        if h % 2 == 0 and i == 0:
                            pe.wait_ge(landed[c % RING], 16 * (c // RING + 1))
                        wt = ring[:, c % RING, :].rearrange("p (k f) -> p k f", k=KD)
                        mm = pe.matmul(bank[t % NBANK][:, 0:n], wt[:, i, h % 2 * P:(h % 2 + 1) * P], HB[:, i, 0:n],
                                       start=(i == 0), stop=(i == KD - 1))
                        if i == KD - 1:
                            mm.then_inc(S["gemm_step"], 1)
                    pe.wait_ge(S["vbank_free"], jobs["v"])
                    pe.wait_ge(S["qi_ready"], w("qi_ready"))
                    b = take("a")
                    for c in range(nc_):
                        tok = slice(c * P, (c + 1) * P)
                        mm = pe.matmul(b[:, tok], VTK[:, c, h, :], ATT[:, h % 2, c, :], start=True, stop=False)
                        for d in range(2):
                            st = ENTERS[d].get(c)
                            if st is not None:
                                lastd = d == 1 or ENTERS[1].get(c) is None
                                mm = pe.matmul(b[:, tok], STATE[:, d, st, h, :], QI[:, h % 2, d, tok],
                                               start=False, stop=lastd)
                    post("a", mm)
                pe.wait_ge(S["o_sq"], w("o_sq"))
                for h in range(4):
                    one("a", ones, HSQ[:, h, 0:n], n)
                pe.wait_ge(S["hgrn_done"], w("hgrn_done"))

                for br in range(3):
                    src = (26, 14, 18)[br]
                    for half in range(2):
                        if br + half:
                            gemm(("gate", l, br, half), lambda k, n=n: HB[:, k, 0:n], wait_free=False)
                        gemm(("proj", l, br, half), lambda k, n=n, src=src: P2[:, src + k, 0:n], wait_free=False)
                pe.wait_ge(S["merge_used"], w("merge_used", 6))
                gemm(("out2", l), lambda k, n=n: ACC[:, k, 0:n])
                rms(n)
                gemm(("ff1", l), lambda k, n=n: HB[:, k, 0:n], by_tile="h_ready")
                pe.wait_ge(S["ff_ready"], w("ff_ready", DFF2 // P))
                gemm(("ff2", l), lambda k, n=n: HF2[:, k, 0:n])

        class Reader:

            def __init__(self, eng, banks):
                self.eng, self.banks, self.n = eng, banks, 0

            def take(self):
                self.n += 1
                return self.n

            def bank(self):
                return self.banks[(self.n - 1) % 2]

            def tiles(self, key, read):
                g = G[key]
                for b in range(g.blocks):
                    for f in range(g.nf):
                        self.eng.wait_ge(S["gemm_step"], g.step0 + (b * g.g + g.g - 1) * g.nf + f + 1)
                        k = b * g.nf + f
                        read(k, bank[(g.tile0 + k) % NBANK]).then_inc(S["tile_free"], 1)

            def tiles_read(self, key, n=None):
                g = G[key]
                self.eng.wait_ge(S["tile_free"], g.tile0 + (g.blocks * g.nf if n is None else n))

        @block.scalar
        def _(act):
            w = Waits()
            st = Steps()
            rd = Reader(act, abank)

            def fn(out_, in_, f, **kw):
                return act.activation(out_, in_, f, **kw)

            def copy_bank(out_, n=512, shape=None):
                act.wait_ge(S["abank_full"], rd.take())
                b = rd.bank()[:, 0:n]
                if shape:
                    b = b.rearrange(shape[0], **shape[1])
                fn(out_, b, ACT.Copy).then_inc(S["abank_free"], 1)

            def rstd_of(out_, n, scale, eps):
                act.wait_ge(S["abank_full"], rd.take())
                fn(out_, rd.bank()[:, 0:n], ACT.Ln, scale=scale, bias=pcol(eps)).then_inc(S["abank_free"], 1)

            def layer_norm(z):
                for k in range(KD):
                    act.wait_ge(S["centered"], w("centered"))
                    fn(ZSQ[:, k, :], z[:, k, :], ACT.Square).then_inc(S["squared"], 1)
                rstd_of(ZRS, T, 1.0 / D, "eps5")
                act.wait_ge(S["abank_free"], rd.n)
                fn(ZRS, ZRS, ACT.Exp, scale=-0.5).then_inc(S["rstd_ready"], 1)

            act.dma_start(con[:, :], cst).then_inc(S["const_landed"], 16)
            act.dma_start(X[:, :, 0:T], xT.rearrange("(k p) t -> p k t", p=P)).then_inc(S["x_landed"], 16)
            act.dma_start(WL, lora.rearrange("i p n -> p i n")).then_inc(S["lora_landed"], 16)
            act.wait_ge(S["par_landed"], 16)
            fn(CS, pcol("cond", 0, 16), ACT.Silu).then_inc(S["cond_silu"], 1)
            act.wait_ge(S["lb_shifted"], w("lb_shifted"))
            fn(LB, LB, ACT.Exp).then_inc(S["lb_exp"], 1)
            act.wait_ge(S["lb_floored"], w("lb_floored"))
            fn(LLB, LBT, ACT.Ln).then_inc(S["lb_ln"], 1)

            rd.tiles("ab_in", lambda k, b: fn(PRJ[:, k, 1:T + 1], b[:, 0:T], ACT.Copy))

            act.wait_ge(S["abank_full"], rd.take())
            fn(LAME, rd.bank()[:, 0:2], ACT.Exp).then_inc(S["abank_free"], 1)
            act.wait_ge(S["abank_free"], rd.n)
            fn(LAME2, LAME, ACT.Copy).then_inc(S["lam_exp"], 1)
            for j in range(2):
                copy_bank(VT1[:, j, :, :].rearrange("p a b -> p (a b)"))

            def exps(u):
                act.wait_ge(S["scores_ready"], w("scores_ready"))
                for c in range(2):
                    i = 2 * (u % 2) + c
                    ins = fn(EE1[:, u % 2, c, :], SM1[:, u % 2, c, :], ACT.Exp, scale=SCALE, bias=NM[:, i:i + 1],
                             accum_out=SU[:, i:i + 1])
                    ins.then_inc(S["exp_ready"], 1)

            exps(0)
            for u in range(8):
                if u < 7:
                    exps(u + 1)
                h, qt = u // 2, u % 2
                copy_bank(PT1[:, h % 2, :, qt * P:(qt + 1) * P], 2 * P, ("p (a b) -> p a b", dict(a=2)))
            for i in range(2):
                rstd_of(ORS[:, 2 * i:2 * i + 2, :].rearrange("p a b -> p (a b)"), 512, 1.0 / P, "eps5")
            act.wait_ge(S["abank_free"], rd.n)
            fn(ORS[:, :, :], ORS[:, :, :], ACT.Exp, scale=-0.5).then_inc(S["o_rstd"], 1)

            act.wait_ge(S["xs_ready"], w("xs_ready"))
            fn(TW, XS[:, 12, :], ACT.Tanh).then_inc(S["lora_in"], 1)
            fn(SG, XS[:, 13, :], ACT.Sigmoid).then_inc(S["lora_in"], 1)
            for dst, name, said in ((LD, "w0", "decay_ready"), (AA, "a0", "a_ready"), (GG, None, "g_out")):
                for f in range(2):
                    act.wait_ge(S["abank_full"], rd.take())
                    b = rd.bank()
                    if name is None:
                        fn(dst[:, 2 * f:2 * f + 2, :].rearrange("p a b -> p (a b)"), b[:, :], ACT.Copy)\
                            .then_inc(S["abank_free"], 1)
                        continue
                    fn(dst[:, 2 * f, :], b[:, 0:T], ACT.Sigmoid, bias=pcol(name, 2 * f))\
                        .then_inc(S["act_chain"], st.one())
                    fn(dst[:, 2 * f + 1, :], b[:, T:2 * T], ACT.Sigmoid, bias=pcol(name, 2 * f + 1))\
                        .then_inc(S["abank_free"], 1)
                act.wait_ge(S["act_chain"], st.n)
                act.wait_ge(S["abank_free"], rd.n)
                act.sem_inc(S[said], 1)
            for i in range(2):
                act.wait_ge(S["abank_full"], rd.take())
                fn(E1[:, 2 * i:2 * i + 2, :].rearrange("p a b -> p (a b)"), rd.bank()[:, :], ACT.Sqrt)\
                    .then_inc(S["abank_free"], 1)
            act.wait_ge(S["abank_free"], rd.n)
            act.sem_inc(S["kk_root"], 1)
            act.wait_ge(S["log_ready"], w("log_ready"))
            fn(E1, LL, ACT.Exp).then_inc(S["act_chain"], st.one())
            fn(E2, LL, ACT.Exp, scale=-1.0).then_inc(S["act_chain"], st.one())
            fn(E3, LP, ACT.Exp).then_inc(S["act_chain"], st.one())
            fn(EGM, GMS, ACT.Exp).then_inc(S["act_chain"], st.one())
            act.wait_ge(S["act_chain"], st.n)
            act.sem_inc(S["exp_factors"], 1)
            act.wait_ge(S["hats_act"], w("hats_act"))
            for dst in (VT[:, 0, :], VT[:, 1, :], BT, KT):
                copy_bank(dst)
            for dst in (RH, UU[:, 0, :], YT[:, 0, :], RH, UU[:, 1, :], YT[:, 1, :]):
                copy_bank(dst)
            for j in range(2):
                copy_bank(YF[:, :, j * P:(j + 1) * P], 512, ("p (a b) -> p a b", dict(a=4)))
            act.wait_ge(S["gn_sq"], w("gn_sq"))
            for i in range(2):
                rstd_of(GRS[:, 2 * i:2 * i + 2, :].rearrange("p a b -> p (a b)"), 512, 1.0 / HD, "eps_gn")
            act.wait_ge(S["abank_free"], rd.n)
            fn(GRS, GRS, ACT.Exp, scale=-0.5).then_inc(S["gn_rstd"], 1)
            layer_norm(Z)

            def ffn(l):
                g = G["up", l]

                def tile_in(k, dst):
                    act.wait_ge(S["gemm_step"], g.step0 + k + 1)
                    fn(dst, bank[(g.tile0 + k) % NBANK][:, 0:T], ACT.Copy).then_inc(S["tile_free"], 1)

                for pair in range(NFF // 2):
                    for f in range(2):
                        tile_in(4 * pair + f, GP[:, (2 * pair + f) % 4, 2:T + 2])
                    for f in range(2):
                        if pair >= 2:
                            act.wait_ge(S["hid_ready"], w("hid_ready"))
                        tile_in(4 * pair + 2 + f, VAL[:, (2 * pair + f) % 4, :])
                    for f in range(2):
                        act.wait_ge(S["conv_ready"], w("conv_ready"))
                        c = CV[:, (2 * pair + f) % 4, :]
                        fn(c, c, ACT.Silu).then_inc(S["silu_ready"], 1)
                act.wait_ge(S["hid_ready"], w("hid_ready", 4))
                layer_norm(Z)

            ffn(0)
            rd.tiles("c_in", lambda k, b: fn(UV[:, k, :], b[:, 0:T], ACT.Gelu, bias=pcol("c_b_in", k)))
            layer_norm(UV[:, 8:16, :])
            for j in range(2):
                for q in range(2):
                    copy_bank(VTC[:, j, q * 512:(q + 1) * 512])
            layer_norm(Z)
            ffn(1)

            act.wait_ge(S["ctx_landed"], 16)
            act.wait_ge(S["x_ready"], w("x_ready", 4))
            for l in range(2):
                last = l == 1
                n = T if last else 2 * T

                def rms(m, key=None):
                    for k in range(KD):
                        if key:
                            act.wait_ge(S["tile_free"], G[key].tile0 + k + 1)
                        fn(XSQ[:, k, 0:m], X[:, k, 0:m], ACT.Square).then_inc(S["xsq_ready"], 1)
                    rstd_of(XRS[:, 0:m], m, 1.0 / D, "eps6")
                    act.wait_ge(S["abank_free"], rd.n)
                    fn(XRS[:, 0:m], XRS[:, 0:m], ACT.Exp, scale=-0.5).then_inc(S["xrstd_ready"], 1)

                rms(2 * T, ("ff2", 0) if last else None)
                rd.tiles(("in_state", l), lambda k, b: fn(P2[:, k, :], b[:, :], ACT.Copy))
                rd.tiles_read(("in_state", l))

                def softplus(d, i):
                    z = P2[:, 6 + 4 * d:10 + 4 * d, :]
                    if i == 0:
                        if d:
                            act.wait_ge(S["dir_done"], w("dir_done"))
                        fn(TA, z, ACT.Abs).then_inc(S["act_chain"], st.one())
                    if i == 1:
                        act.wait_ge(S["act_chain"], st.n)
                        fn(TA, TA, ACT.Exp, scale=-1.0).then_inc(S["act_chain"], st.one())
                    if i == 2:
                        fn(TB, z, ACT.Relu, scale=-1.0).then_inc(S["act_chain"], st.one())
                        act.wait_ge(S["act_chain"], st.n)
                        fn(TA, TA, ACT.Ln, bias=pcol("one")).then_inc(S["sp_first"], 1)
                    if i in (3, 4):
                        for h in range(2 * i - 6, 2 * i - 4):
                            lb = LLB[:, 8 * l + 4 * d + h:8 * l + 4 * d + h + 1]
                            fn(TC[:, h, :], z[:, h, :], ACT.Abs, scale=-1.0, bias=lb)\
                                .then_inc(S["act_chain"], st.one())
                            fn(TD[:, h, :], z[:, h, :], ACT.Relu, scale=-1.0, bias=lb)\
                                .then_inc(S["act_chain"], st.one())
                    if i == 5:
                        act.wait_ge(S["act_chain"], st.n)
                        fn(TC, TC, ACT.Exp, scale=-1.0).then_inc(S["act_chain"], st.one())
                    if i == 6:
                        act.wait_ge(S["act_chain"], st.n)
                        fn(TC, TC, ACT.Ln, bias=pcol("one")).then_inc(S["sp_second"], 1)
                    if i == 7:
                        act.wait_ge(S["sp_sum"], w("sp_sum"))
                        fn(TB, TB, ACT.Exp, scale=-1.0).then_inc(S["k_raw"], 1)

                g = G["in_rest", l]
                for k in range(g.blocks * g.nf):
                    act.wait_ge(S["gemm_step"], g.step0 + k + 1)
                    fn(P2[:, 2 * STATE_BLOCKS + k, 0:n], bank[(g.tile0 + k) % NBANK][:, 0:n], ACT.Copy)\
                        .then_inc(S["tile_free"], 1)
                    if k < 16:
                        softplus(k // 8, k % 8)
                rd.tiles_read(("in_rest", l))

                fn(NSQ[:, 0:4, 0:n], P2[:, 14:18, 0:n], ACT.Square).then_inc(S["n_squares"], 1)
                fn(NSQ[:, 4, :], P2[:, 0, :], ACT.Square).then_inc(S["n_squares"], 1)
                for i in range(5):
                    m = n if i < 4 else 2 * T
                    rstd_of(NRS[:, i, 0:m], m, 1.0 / HD, "eps6")
                act.wait_ge(S["abank_free"], rd.n)
                fn(NRS[:, 0:4, 0:n], NRS[:, 0:4, 0:n], ACT.Exp, scale=-0.5).then_inc(S["n_rstd"], 1)
                fn(NRS[:, 4, :], NRS[:, 4, :], ACT.Exp, scale=-0.5).then_inc(S["n_rstd"], 1)
                act.wait_ge(S["dir_done"], w("dir_done"))
                act.wait_ge(S["tot_ready"], w("tot_ready"))
                fn(ETOT, TOT, ACT.Exp).then_inc(S["e_tot"], 1)
                act.wait_ge(S["vz_zero"], w("vz_zero"))
                for kv in range(2):
                    act.wait_ge(S["abank_full"], rd.take())
                    b = rd.bank()
                    fn(KZ2[0:HD, kv, 0, :], b[0:HD, :], ACT.Copy).then_inc(S["act_chain"], st.one())
                    act.wait_ge(S["act_chain"], st.n)
                    fn(KZ2[HD:P, kv, 1, :], b[HD:P, :], ACT.Copy).then_inc(S["abank_free"], 1)
                units = [(s, t, h) for s in range(1 if last else 2) for t in range(4) for h in range(2)]

                def exps2(i):
                    s, t, h = units[i]
                    m = 2 * T if s == 0 else T
                    act.wait_ge(S["w_scores"], w("w_scores"))
                    c = i % 2
                    fn(ES[:, 2 * c:2 * c + 2], NM[:, 2 * c:2 * c + 2], ACT.Exp, bias=pcol("sink", 8 * l + 2 * t + h))\
                        .then_inc(S["w_exp"], 1)
                    for q in range(2):
                        j = 2 * c + q
                        fn(SM2[:, c, q, 0:m], SM2[:, c, q, 0:m], ACT.Exp, scale=SCALE, bias=NM[:, j:j + 1],
                           accum_out=SU[:, j:j + 1]).then_inc(S["w_exp"], 1)

                exps2(0)
                for i, (s, t, h) in enumerate(units):
                    if i + 1 < len(units):
                        exps2(i + 1)
                    if i == 1:
                        fn(P2[:, 22:26, 0:n], P2[:, 22:26, 0:n], ACT.Silu).then_inc(S["q_silu"], 1)
                        fn(P2[:, 18:22, 0:n], P2[:, 18:22, 0:n], ACT.Silu).then_inc(S["q_silu"], 1)
                    for k in range(0, 4 if s == 0 else 2, 2):
                        copy_bank(PT2[:, h, k:k + 2, :].rearrange("p a b -> p (a b)"))

                for s in range(1 if last else 2):
                    for g in range(4):
                        copy_bank(FB[:, (s * 4 + g) % 2].rearrange("p a b c -> p (a b c)"))

                for c in range(4):
                    copy_bank(VTK[:, c].rearrange("p a b -> p (a b)"))
                for d in range(2):
                    if d == 0:
                        act.wait_ge(S["ks_diff"], w("ks_diff"))
                        fn(KSF, KSF, ACT.Exp).then_inc(S["ks_exp"], 1)
                    else:
                        fn(KSF, LF[:, 4:8, :], ACT.Exp).then_inc(S["ks_exp"], 1)
                    for i in range(3):
                        copy_bank(KST[:, d, i].rearrange("p a b -> p (a b)"))
                for h in range(4):
                    act.wait_ge(S["qi_diff"], w("qi_diff"))
                    fn(QI[:, h % 2, 0, 0:n], LF[:, h, 0:n], ACT.Exp).then_inc(S["qi_exp"], 1)
                    fn(QI[:, h % 2, 1, 0:n], QI[:, h % 2, 1, 0:n], ACT.Exp).then_inc(S["qi_exp"], 1)
                    for i in range(LEVELS):
                        act.wait_ge(S["lvl_diff"], w("lvl_diff", 4))
                        fn(LDF[:, i % 2, :, 0:n], LDF[:, i % 2, :, 0:n], ACT.Exp).then_inc(S["lvl_exp"], 1)
                    g = G["gate", l, 0, 0]
                    act.wait_ge(S["gemm_step"], g.step0 + h + 1)
                    fn(GATE0B[:, h, 0:n], bank[(g.tile0 + h) % NBANK][:, 0:n], ACT.Copy).then_inc(S["tile_free"], 1)
                    copy_bank(P2[:, 18 + h, 0:n], n)
                act.wait_ge(S["abank_free"], rd.n)
                fn(HSQ[:, :, 0:n], P2[:, 18:22, 0:n], ACT.Square).then_inc(S["o_sq"], 1)
                for h in range(4):
                    rstd_of(HRS[:, h, 0:n], n, 1.0 / P, "eps6")
                act.wait_ge(S["abank_free"], rd.n)
                fn(HRS[:, :, 0:n], HRS[:, :, 0:n], ACT.Exp, scale=-0.5).then_inc(S["o_rs"], 1)

                for br in range(3):
                    for half in range(2):
                        i = 2 * br + half
                        if i >= 2:
                            act.wait_ge(S["merge_used"], w("merge_used"))
                        if i == 0:
                            rd.tiles_read(("gate", l, 0, 0))
                            fn(GATE0B[:, :, 0:n], GATE0B[:, :, 0:n], ACT.Sigmoid).then_inc(S["act_chain"], st.one())
                        else:
                            rd.tiles(("gate", l, br, half),
                                     lambda k, b, i=i, n=n: fn(GB[:, i % 2, k, 0:n], b[:, 0:n], ACT.Sigmoid))
                        rd.tiles(("proj", l, br, half),
                                 lambda k, b, i=i, n=n: fn(PB[:, i % 2, k, 0:n], b[:, 0:n], ACT.Copy))
                act.wait_ge(S["merge_used"], w("merge_used", 2))
                rms(n, ("out2", l))
                rd.tiles(("ff1", l), lambda k, b, n=n: fn(HF2[:, k, 0:n], b[:, 0:n], ACT.Relu))

        @block.vector
        def _(ve):
            w = Waits()
            st = Steps()
            rd = Reader(ve, vbank)
            tt, ts, stt = ve.tensor_tensor, ve.tensor_scalar, ve.scalar_tensor_tensor
            MUL, ADD, SUB, MAX = ALU.mult, ALU.add, ALU.subtract, ALU.max

            def say(sem):
                ve.drain().then_inc(sem, 1)

            def layer_norm(z, gain, bias, dst):
                ve.wait_ge(S["vbank_full"], rd.take())
                b = rd.bank()[:, 0:T]
                for k in range(KD):
                    stt(z[:, k, :], b, -1.0 / D, z[:, k, :], MUL, ADD).then_inc(S["centered"], 1)
                ve.wait_ge(S["centered"], w("centered", KD))
                ve.sem_inc(S["vbank_free"], 1)
                ve.wait_ge(S["rstd_ready"], w("rstd_ready"))

                def scaled(k):
                    tt(z[:, k, :], z[:, k, :], ZRS, MUL).then_inc(S["vec_chain"], st.one())
                    return st.n

                done = scaled(0)
                for k in range(KD):
                    mine, done = done, scaled(k + 1) if k + 1 < KD else done
                    ve.wait_ge(S["vec_chain"], mine)
                    ts(dst(k), z[:, k, :], pcol(*gain(k)), pcol(*bias(k)), MUL, ADD).then_inc(S["ln_tile"], 1)
                ve.wait_ge(S["ln_tile"], w("ln_tile", KD))

            def residual(key):
                rd.tiles(key, lambda k, b: stt(Z[:, k, :], X[:, k, 0:T], DEEPNORM, b[:, 0:T], MUL, ADD))
                rd.tiles_read(key)

            def mod_fill(l, k):
                g = G["mod", l]
                if 1 <= k <= g.blocks:
                    ve.wait_ge(S["gemm_step"], g.step0 + k)
                    ve.tensor_copy(mod_row[:, (k - 1) % 2, :], bank[(g.tile0 + k - 1) % NBANK][0:2, 0:BLK])\
                        .then_inc(S["tile_free"], 1)
                if 2 <= k < g.blocks + 2:
                    j = 2 * (k - 2)
                    ve.wait_ge(S["vbank_full"], rd.take())
                    b = rd.bank()[:, 0:4].rearrange("p (a b) -> p a b", b=2)
                    tt(MOD[l][:, j:j + 2, :], b, pcol("b_mod", 48 * l + j, 2).unsqueeze(2).to_broadcast([P, 2, 2]),
                       ADD).then_inc(S["vbank_free"], 1)

            ve.wait_ge(S["par_landed"], 16)
            tt(LAMP, pcol("lam_q", 0, 2), pcol("lam_k", 0, 2), MUL).then_inc(S["lam_prod"], 1)
            ts(OMKA, pcol("k_a", 0, 4), -1.0, 1.0, MUL, ADD).then_inc(S["vec_chain"], st.one())
            ts(G08, pcol("subln_g"), 1.0 - LAM_INIT, None, MUL).then_inc(S["vec_chain"], st.one())
            tt(LBT[:, 0:8], pcol("lb", 0, 8), pcol("lb", 8, 8), MAX).then_inc(S["vec_chain"], st.one())
            ve.wait_ge(S["vec_chain"], st.n)
            tt(LB[:, 0:8], pcol("lb", 0, 8), LBT[:, 0:8], SUB).then_inc(S["vec_chain"], st.one())
            tt(LB[:, 8:16], pcol("lb", 8, 8), LBT[:, 0:8], SUB).then_inc(S["lb_shifted"], 1)
            ve.wait_ge(S["lb_exp"], w("lb_exp"))
            tt(LBT[:, 0:8], LB[:, 0:8], LB[:, 8:16], ADD).then_inc(S["vec_chain"], st.one())
            ve.wait_ge(S["vec_chain"], st.n)
            ve.reciprocal(LBT[:, 8:16], LBT[:, 0:8]).then_inc(S["vec_chain"], st.one())
            ve.wait_ge(S["vec_chain"], st.n)
            tt(LB[:, 0:8], LB[:, 0:8], LBT[:, 8:16], MUL).then_inc(S["vec_chain"], st.one())
            tt(LB[:, 8:16], LB[:, 8:16], LBT[:, 8:16], MUL).then_inc(S["vec_chain"], st.one())
            ve.wait_ge(S["vec_chain"], st.n)
            tt(LB[:, 8:16], LB[:, 8:16], LB[:, 0:8], ADD).then_inc(S["vec_chain"], st.one())
            ve.wait_ge(S["vec_chain"], st.n)
            tt(LB[:, 8:16], LB[:, 8:16], LB[:, 0:8], SUB).then_inc(S["vec_chain"], st.one())
            ve.wait_ge(S["vec_chain"], st.n)
            tt(LB[:, 0:8], LB[:, 0:8], LB[:, 0:8], SUB).then_inc(S["vec_chain"], st.one())
            ve.wait_ge(S["vec_chain"], st.n)
            ts(OMLB, LB, -1.0, 1.0, MUL, ADD).then_inc(S["vec_chain"], st.one())
            ts(LBT, LB, LN_SMALL, None, MAX).then_inc(S["lb_floored"], 1)
            ve.wait_ge(S["lb_ln"], w("lb_ln"))
            ts(LBT, LB, LN_SMALL, LN_FLOOR - LN_LN_SMALL, ALU.is_lt, MUL).then_inc(S["vec_chain"], st.one())
            ve.wait_ge(S["vec_chain"], st.n)
            tt(LLB, LLB, LBT, ADD).then_inc(S["vec_chain"], st.one())
            ve.wait_ge(S["vec_chain"], st.n)

            ve.wait_ge(S["lam_exp"], w("lam_exp"))
            tt(NLAM, LAME2[:, 1:2], LAME2[:, 0:1], SUB).then_inc(S["vec_chain"], st.one())
            ve.wait_ge(S["vec_chain"], st.n)
            ts(NLAM, NLAM, -LAM_INIT, None, ADD).then_inc(S["vec_chain"], st.one())
            ve.wait_ge(S["const_landed"], 16)
            ve.wait_ge(S["masks_ready"], w("masks_ready"))
            for i in range(4):
                ve.wait_ge(S["vbank_full"], rd.take())
                b = rd.bank()[:, :].rearrange("p (a b) -> p a b", a=2)
                tt(R2, PRJ[:, 14 + 2 * i:16 + 2 * i, 1:T + 1], rep(cc("cos_a"), 2), MUL)\
                    .then_inc(S["vec_chain"], st.one())
                tt(R3, b, rep(cc("sin_a"), 2), MUL).then_inc(S["vbank_free"], 1)
                ve.wait_ge(S["vec_chain"], st.n)
                ve.wait_ge(S["vbank_free"], rd.n)
                if i >= 2:
                    tt(KR1[:, 2 * i - 4:2 * i - 2, :], R2, R3, ADD).then_inc(S["vec_chain"], st.one())
                    ve.wait_ge(S["vec_chain"], st.n)
                else:
                    tt(R2, R2, R3, ADD).then_inc(S["vec_chain"], st.one())
                    ve.wait_ge(S["vec_chain"], st.n)
                    for c in range(2):
                        ts(QZ1[:, 2 * i:2 * i + 2, c, :], R2, pcol("half", c), None, MUL)\
                            .then_inc(S["vec_chain"], st.one())
                        ve.wait_ge(S["vec_chain"], st.n)
            say(S["rope_ready"])

            def score(u):
                ve.wait_ge(S["vbank_full"], rd.take())
                b = rd.bank()[:, :].rearrange("p (a b) -> p a b", a=2)
                c = 2 * (u % 2)
                tt(SM1[:, u % 2], b, rep(cc("causal", 2, T)[:, u % 2, :], 2), ADD).then_inc(S["vbank_free"], 1)
                ve.wait_ge(S["vbank_free"], rd.n)
                ve.tensor_reduce(MX[:, c:c + 2], SM1[:, u % 2], AXX, MAX).then_inc(S["vec_chain"], st.one())
                ve.wait_ge(S["vec_chain"], st.n)
                ts(NM[:, c:c + 2], MX[:, c:c + 2], -SCALE, None, MUL).then_inc(S["scores_ready"], 1)

            score(0)
            for u in range(8):
                if u < 7:
                    score(u + 1)
                mod_fill(0, u)
                h, qt = u // 2, u % 2
                c = 2 * qt
                ve.wait_ge(S["exp_ready"], w("exp_ready", 2))
                ve.reciprocal(SU[:, c:c + 2], SU[:, c:c + 2]).then_inc(S["vec_chain"], st.one())
                ve.wait_ge(S["vec_chain"], st.n)
                tt(SU[:, c + 1:c + 2], SU[:, c + 1:c + 2], NLAM, MUL).then_inc(S["vec_chain"], st.one())
                ts(AT1[:, qt, :], EE1[:, qt, 0, :], SU[:, c:c + 1], None, MUL).then_inc(S["vec_chain"], st.one())
                ve.wait_ge(S["vec_chain"], st.n)
                stt(AT1[:, qt, :], EE1[:, qt, 1, :], SU[:, c + 1:c + 2], AT1[:, qt, :], MUL, ADD)\
                    .then_inc(S["attn_ready"], 1)
                if qt:
                    ve.wait_ge(S["vbank_full"], rd.take())
                    b = rd.bank()
                    ve.tensor_copy(OO1[:, h, :], b[:, 0:T]).then_inc(S["vbank_free"], 1)
            ve.wait_ge(S["vbank_free"], rd.n)
            tt(OSQ, OO1, OO1, MUL).then_inc(S["o_squares"], 1)
            ve.wait_ge(S["o_rstd"], w("o_rstd"))
            for h in range(4):
                ins = stt(YAB[:, 4 + h, :], OO1[:, h, :], G08, ORS[:, h, :], MUL, MUL)
                if h < 3:
                    ins.then_inc(S["vec_chain"], st.one())
            ins.then_inc(S["yd_ready"], 1)

            mod_fill(0, 8)
            ve.wait_ge(S["pad_zero"], w("pad_zero"))
            tt(DT, PRJ[:, 0:RWKV_TILES, 0:T], PRJ[:, 0:RWKV_TILES, 1:T + 1], SUB).then_inc(S["vec_chain"], st.one())
            ve.wait_ge(S["vec_chain"], st.n)
            for t in range(RWKV_TILES):
                stt(XS[:, t, :], DT[:, t, :], pcol("mu", t), PRJ[:, t, 1:T + 1], MUL, ADD)\
                    .then_inc(S["vec_chain"], st.one())
            ve.wait_ge(S["vec_chain"], st.n)
            ve.sem_inc(S["xs_ready"], 1)
            ve.sem_inc(S["xs_pool"], 1)
            for k in range(9, 12):
                mod_fill(0, k)
            for t in range(4):
                ts(KK[:, t, :], XS[:, 4 + t, :], pcol("k_k", t), None, MUL).then_inc(S["vec_chain"], st.one())
            ve.wait_ge(S["vec_chain"], st.n)
            tt(KSQ, KK, KK, MUL).then_inc(S["kk_squares"], 1)
            mod_fill(0, 12)
            ve.wait_ge(S["kk_root"], w("kk_root"))
            ts(E1, E1, 1e-12, None, MAX).then_inc(S["vec_chain"], st.one())
            ve.wait_ge(S["vec_chain"], st.n)
            ve.reciprocal(E1, E1).then_inc(S["vec_chain"], st.one())
            ve.wait_ge(S["vec_chain"], st.n)
            tt(KK, KK, E1, MUL).then_inc(S["vec_chain"], st.one())
            ve.wait_ge(S["vec_chain"], st.n)
            mod_fill(0, 13)
            ve.wait_ge(S["decay_ready"], w("decay_ready"))
            ts(LD, LD, -EXP_MINUS_HALF, None, MUL).then_inc(S["vec_chain"], st.one())
            ve.wait_ge(S["vec_chain"], st.n)
            for t in range(4):
                ve.tensor_tensor_scan(LL[:, t, :], cc("reset")[:, 0:T], LD[:, t, :], 0.0, MUL, ADD)\
                    .then_inc(S["vec_chain"], st.one())
            ve.wait_ge(S["vec_chain"], st.n)
            for k in (14, 15):
                mod_fill(0, k)
            LL8, LP8 = (v.rearrange("p a (c b) -> p (a c) b", c=2) for v in (LL, LP))
            tt(LP, LL, LD, SUB).then_inc(S["vec_chain"], st.one())
            ve.tensor_copy(GMS.unsqueeze(2), LL8[:, :, 63:64]).then_inc(S["vec_chain"], st.one())
            ve.wait_ge(S["vec_chain"], st.n)
            mid = GMS.unsqueeze(2).to_broadcast([P, 8, P])
            tt(LL8, LL8, mid, SUB).then_inc(S["vec_chain"], st.one())
            tt(LP8, LP8, mid, SUB).then_inc(S["log_ready"], 1)
            for k in (16, 17):
                mod_fill(0, k)
            ve.wait_ge(S["a_ready"], w("a_ready"))
            for t in range(4):
                ts(LD[:, t, :], AA[:, t, :], pcol("k_a", t), OMKA[:, t:t + 1], MUL, ADD)\
                    .then_inc(S["vec_chain"], st.one())
            ve.wait_ge(S["vec_chain"], st.n)
            tt(XS[:, 4:8, :], XS[:, 4:8, :], LD, MUL).then_inc(S["vec_chain"], st.one())
            ve.wait_ge(S["vec_chain"], st.n)
            for k in (18, 19):
                mod_fill(0, k)
            ve.wait_ge(S["exp_factors"], w("exp_factors"))
            stt(AR[:, :, 0, :], KK.rearrange("p a (c b) -> p (a c) b", c=2), -1.0,
                E3.rearrange("p a (c b) -> p (a c) b", c=2), MUL, MUL).then_inc(S["vec_chain"], st.one())
            tt(AR[:, :, 1, :], XS[:, 0:4, :].rearrange("p a (c b) -> p (a c) b", c=2),
               E1.rearrange("p a (c b) -> p (a c) b", c=2), MUL).then_inc(S["vec_chain"], st.one())
            tt(BH, KK, AA, MUL).then_inc(S["vec_chain"], st.one())
            tt(KH, XS[:, 4:8, :], E2, MUL).then_inc(S["vec_chain"], st.one())
            ve.wait_ge(S["vec_chain"], st.n)
            tt(BH, BH, E2, MUL).then_inc(S["vec_chain"], st.one())
            ve.wait_ge(S["vec_chain"], st.n)
            for k in (20, 21):
                mod_fill(0, k)
            ve.wait_ge(S["g_out"], w("g_out"))
            for par_ in range(2):
                ts(BZ[:, :, par_, :], BH, pcol("half", par_), None, MUL).then_inc(S["vec_chain"], st.one())
                ts(KZ[:, :, par_, :], KH, pcol("half", par_), None, MUL).then_inc(S["vec_chain"], st.one())
            tt(FST.unsqueeze(2), E1[:, :, P - 1:P], EGM.rearrange("p (a b) -> p a b", b=2)[:, :, 1:2], MUL)\
                .then_inc(S["vec_chain"], st.one())
            ve.wait_ge(S["vec_chain"], st.n)
            ve.sem_inc(S["hats_ready"], 1)
            ve.sem_inc(S["hats_act"], 1)
            for k in range(22, MOD_BLOCKS + 2):
                mod_fill(0, k)
            for dst in (XI, YI):
                ve.tensor_copy(dst, rep(ident, 16)).then_inc(S["inv_init"], 1)
            ve.wait_ge(S["pr_zero"], w("pr_zero"))
            for u in range(16):
                ve.wait_ge(S["vbank_full"], rd.take())
                b = rd.bank()
                ve.copy_predicated(PR[:, u].rearrange("p a b -> p (a b)"), mask("rwkv", 0, 512), b[:, :])\
                    .then_inc(S["vbank_free"], 1)
            for l in range(LEVELS):
                for q in range(4):
                    four = slice(4 * q, 4 * q + 4)
                    ve.wait_ge(S["vbank_full"], rd.take())
                    b = rd.bank()[:, :].rearrange("p (a b) -> p a b", a=4)
                    tt(T1[:, four, :], b, rep(mask("bwd", l), 4), MUL).then_inc(S["vbank_free"], 1)
                    if l == 0:
                        ve.wait_ge(S["vbank_free"], rd.n)
                        tt(XI[:, four, :], XI[:, four, :], T1[:, four, :], ADD).then_inc(S["vec_chain"], st.one())
                        ve.wait_ge(S["vec_chain"], st.n)
                        tt(T1[:, four, :], PR[:, four, 0, :], rep(mask("fwd", 0), 4), MUL)\
                            .then_inc(S["vec_chain"], st.one())
                        ve.wait_ge(S["vec_chain"], st.n)
                        tt(YI[:, four, :], YI[:, four, :], T1[:, four, :], ADD).then_inc(S["inv_first"], 1)
                for q in range(4 if l else 0):
                    four = slice(4 * q, 4 * q + 4)
                    for dst in ((XI, YI) if l < LEVELS - 1 else (YI,)):
                        ve.wait_ge(S["vbank_full"], rd.take())
                        b = rd.bank()[:, :].rearrange("p (a b) -> p a b", a=4)
                        tt(dst[:, four, :], dst[:, four, :], b, ADD).then_inc(S["vbank_free"], 1)
            ve.wait_ge(S["vbank_full"], rd.take())
            b = rd.bank()
            for t in range(4):
                ins = stt(SB[:, t, :], b[:, t * P:(t + 1) * P], FST[:, t:t + 1], block64, MUL, MUL)
                if t < 3:
                    ins.then_inc(S["vec_chain"], st.one())
            ins.then_inc(S["vbank_free"], 1)
            for t in range(4):
                ins = stt(BON[:, t, :], XS[:, t, :], pcol("r_k", t), XS[:, 4 + t, :], MUL, MUL)
                if t < 3:
                    ins.then_inc(S["vec_chain"], st.one())
            ins.then_inc(S["bonus_in"], 1)
            for i in range(2):
                ve.wait_ge(S["vbank_full"], rd.take())
                b = rd.bank()[:, :].rearrange("p (a b) -> p a b", a=2)
                y = YF[:, 2 * i:2 * i + 2, :]
                stt(y, b, -1.0 / HD, y, MUL, ADD).then_inc(S["vbank_free"], 1)
            ve.wait_ge(S["vbank_free"], rd.n)
            tt(GSQ, YF, YF, MUL).then_inc(S["gn_sq"], 1)
            for i in range(2):
                ve.wait_ge(S["vbank_full"], rd.take())
                b = rd.bank()[:, :].rearrange("p (a b) -> p a b", a=2)
                tt(BON[:, 2 * i:2 * i + 2, :], b, XS[:, 8 + 2 * i:10 + 2 * i, :], MUL).then_inc(S["vbank_free"], 1)
            ve.wait_ge(S["gn_rstd"], w("gn_rstd"))
            tt(YF, YF, GRS, MUL).then_inc(S["vec_chain"], st.one())
            ve.wait_ge(S["vec_chain"], st.n)
            for t in range(4):
                ts(YF[:, t, :], YF[:, t, :], pcol("lnx_g", t), pcol("lnx_b", t), MUL, ADD)\
                    .then_inc(S["vec_chain"], st.one())
            ve.wait_ge(S["vec_chain"], st.n)
            ve.wait_ge(S["vbank_free"], rd.n)
            tt(YF, YF, BON, ADD).then_inc(S["vec_chain"], st.one())
            ve.wait_ge(S["vec_chain"], st.n)
            tt(YAB[:, 0:4, :], YF, GG, MUL).then_inc(S["yr_ready"], 1)
            residual("ab_out")
            layer_norm(Z, lambda k: ("ln1_g", k), lambda k: ("ln1_b", k), lambda k: X[:, k, 0:T])
            ve.sem_inc(S["x_ready"], 1)

            def ffn(l):
                g = G["up", l]
                ve.memset(GP[:, :, 0:2], 0.0).then_inc(S["vec_chain"], st.one())
                ve.wait_ge(S["vec_chain"], st.n)
                for pair in range(NFF // 2):
                    for f in range(2):
                        k = 2 * pair + f
                        i = k % 4
                        ve.wait_ge(S["tile_free"], g.tile0 + 4 * pair + f + 1)
                        cw = [pcol("conv_w", (3 * l + j) * NFF + k) for j in range(3)]
                        ts(CV[:, i, :], GP[:, i, 2:T + 2], cw[2], pcol("conv_b", l * NFF + k), MUL, ADD)\
                            .then_inc(S["vec_chain"], st.one())
                        ve.wait_ge(S["vec_chain"], st.n)
                        stt(CV[:, i, :], GP[:, i, 1:T + 1], cw[1], CV[:, i, :], MUL, ADD)\
                            .then_inc(S["vec_chain"], st.one())
                        ve.wait_ge(S["vec_chain"], st.n)
                        stt(CV[:, i, :], GP[:, i, 0:T], cw[0], CV[:, i, :], MUL, ADD).then_inc(S["conv_ready"], 1)
                    for f in range(2):
                        k = 2 * pair + f
                        ve.wait_ge(S["silu_ready"], w("silu_ready"))
                        ve.wait_ge(S["tile_free"], g.tile0 + 4 * pair + 2 + f + 1)
                        tt(HF[:, k, :], CV[:, k % 4, :], VAL[:, k % 4, :], MUL).then_inc(S["hid_ready"], 1)
                residual(("down", l))
                layer_norm(Z, lambda k: ("ln2_g", 8 * l + k), lambda k: ("ln2_b", 8 * l + k),
                           lambda k: X[:, k, 0:T])
                ve.sem_inc(S["x_ready"], 1)

            ffn(0)
            rd.tiles_read("c_in")
            layer_norm(UV[:, 8:16, :], lambda k: ("c_ln_g", k), lambda k: ("c_ln_b", k), lambda k: UV[:, 8 + k, :])
            ve.wait_ge(S["ws_landed"], 32)
            tt(WS, WS, rep(mask("rwkv", 1), 8), MUL).then_inc(S["mix_in"], 1)
            for j in range(2):
                for q in range(2):
                    ve.wait_ge(S["vbank_full"], rd.take())
                    b = rd.bank()[:, :].rearrange("p (a b) -> p a b", a=4)
                    tok = slice(j * P, (j + 1) * P)
                    tt(MU[:, 4 * q:4 * q + 4, tok], UV[:, 4 * q:4 * q + 4, tok], b, MUL).then_inc(S["vbank_free"], 1)
            residual("c_out")
            layer_norm(Z, lambda k: ("ln1_g", 8 + k), lambda k: ("ln1_b", 8 + k), lambda k: X[:, k, 0:T])
            ve.sem_inc(S["x_ready"], 1)
            ffn(1)

            for l in range(2):
                last = l == 1
                n = T if last else 2 * T
                streams = 1 if last else 2
                mod = MOD[l]
                for i, name in enumerate(("norm1_g", "norm2_g")):
                    sc = SC[2 * l + i]
                    ts(sc, mod[:, 8 + 24 * i:16 + 24 * i, :], 1.0, None, ADD).then_inc(S["vec_chain"], st.one())
                    ve.wait_ge(S["vec_chain"], st.n)
                    tt(sc, sc, pcol(name, 8 * l, 8).unsqueeze(2).to_broadcast([P, 8, 2]), MUL)\
                        .then_inc(S["vec_chain"], st.one())
                    ve.wait_ge(S["vec_chain"], st.n)

                def adaln(which, m):
                    ve.wait_ge(S["xrstd_ready"], w("xrstd_ready"))
                    def scaled(k):
                        tt(HB[:, k, 0:m], X[:, k, 0:m], XRS[:, 0:m], MUL).then_inc(S["vec_chain"], st.one())
                        return st.n

                    done = scaled(0)
                    for k in range(KD):
                        mine, done = done, scaled(k + 1) if k + 1 < KD else done
                        ve.wait_ge(S["vec_chain"], mine)
                        for s in range(m // T):
                            h = HB[:, k, s * T:(s + 1) * T]
                            ins = ts(h, h, SC[2 * l + which][:, k, s:s + 1], mod[:, 24 * which + k, s:s + 1],
                                     MUL, ADD)
                            if s < m // T - 1:
                                ins.then_inc(S["vec_chain"], st.one())
                        ins.then_inc(S["h_ready"], 1)
                    ve.sem_inc(S["h_pool"], 1)

                def gated(key, gate):
                    def read(k, b):
                        for s in range(streams):
                            x = X[:, k, s * T:(s + 1) * T]
                            ins = stt(x, b[:, s * T:(s + 1) * T], mod[:, gate + k, s:s + 1], x, MUL, ADD)
                            if s < streams - 1:
                                ins.then_inc(S["vec_chain"], st.one())
                        return ins
                    rd.tiles(key, read)
                    rd.tiles_read(key)
                    ve.wait_ge(S["vec_chain"], st.n)

                adaln(0, 2 * T)

                for d in range(2):
                    z = P2[:, 6 + 4 * d:10 + 4 * d, :]
                    ve.wait_ge(S["sp_first"], w("sp_first"))
                    tt(TA, TA, TB, ADD).then_inc(S["vec_chain"], st.one())
                    ve.wait_ge(S["vec_chain"], st.n)
                    tt(TB, TA, z, ADD).then_inc(S["vec_chain"], st.one())
                    ve.wait_ge(S["sp_second"], w("sp_second"))
                    tt(TC, TC, TD, ADD).then_inc(S["vec_chain"], st.one())
                    ve.wait_ge(S["vec_chain"], st.n)
                    ve.sem_inc(S["sp_sum"], 1)
                    tt(LF[:, 4 * d:4 * d + 4, :], TC, TA, SUB).then_inc(S["vec_chain"], st.one())
                    ve.wait_ge(S["k_raw"], w("k_raw"))
                    for h in range(4):
                        ts(z[:, h, :], TB[:, h, :], OMLB[:, 8 * l + 4 * d + h:8 * l + 4 * d + h + 1],
                           None, MUL).then_inc(S["vec_chain"], st.one())
                    ve.wait_ge(S["vec_chain"], st.n)
                    src = LF if d == 0 else TA
                    for h in range(4):
                        dst = LF[:, h, :] if d == 0 else TA[:, h, :]
                        ve.tensor_tensor_scan(dst, cc("reset"), LF[:, 4 * d + h, :], 0.0, MUL, ADD)\
                            .then_inc(S["vec_chain"], st.one())
                    ve.wait_ge(S["vec_chain"], st.n)
                    tot = TOT.rearrange("p (h c b) -> p h c b", c=4, b=1)[:, 4 * d:4 * d + 4]
                    ve.tensor_copy(tot, src[:, 0:4, :].rearrange("p h (c b) -> p h c b", c=4)[:, :, :, P - 1:P])\
                        .then_inc(S["vec_chain"], st.one())
                    if d:
                        tt(LF[:, 4:8, :], TA, LF[:, 4:8, :], SUB).then_inc(S["vec_chain"], st.one())
                    ve.wait_ge(S["vec_chain"], st.n)
                    ve.sem_inc(S["dir_done"], 1)
                ve.sem_inc(S["tot_ready"], 1)
                ve.sem_inc(S["lf_ready"], 1)

                ve.wait_ge(S["n_rstd"], w("n_rstd", 2))
                for i in range(5):
                    m = n if i < 4 else 2 * T
                    t = 14 + i if i < 4 else 0
                    name = "q_norm" if i < 4 else "k_norm"
                    stt(P2[:, t, 0:m], P2[:, t, 0:m], pcol(name, l), NRS[:, i, 0:m], MUL, MUL)\
                        .then_inc(S["vec_chain"], st.one())
                ve.wait_ge(S["vec_chain"], st.n)
                ve.sem_inc(S["qk_ready"], 1)
                for i in range(5):
                    ve.wait_ge(S["vbank_full"], rd.take())
                    b = rd.bank()
                    x = P2[:, 14 + i if i < 4 else 0, 0:T]
                    tt(RT[:, 0, :], x, cc("cos_b"), MUL).then_inc(S["vec_chain"], st.one())
                    tt(RT[:, 1, :], b[:, 0:T], cc("sin_b"), MUL).then_inc(S["vbank_free"], 1)
                    ve.wait_ge(S["vec_chain"], st.n)
                    ve.wait_ge(S["vbank_free"], rd.n)
                    tt(x, RT[:, 0, :], RT[:, 1, :], ADD).then_inc(S["vec_chain"], st.one())
                    ve.wait_ge(S["vec_chain"], st.n)
                ve.wait_ge(S["vz_zero"], w("vz_zero"))
                ve.wait_ge(S["vbank_full"], rd.take())
                b = rd.bank()[:, :].rearrange("p (c v d) -> p c v d", c=4, v=2)
                ve.tensor_copy(VZ[:, :, :, 0, 0:HD], b).then_inc(S["vec_chain"], st.one())
                ve.tensor_copy(VZ[:, :, :, 1, HD:2 * HD], b).then_inc(S["vbank_free"], 1)
                ve.wait_ge(S["vbank_free"], rd.n)
                ve.wait_ge(S["vec_chain"], st.n)
                ve.sem_inc(S["qz_ready"], 1)
                units = [(s, t, h) for s in range(streams) for t in range(4) for h in range(2)]

                def score2(i):
                    s, t, h = units[i]
                    c = i % 2
                    if s == 0:
                        m = 2 * T
                        for q in range(2):
                            ve.wait_ge(S["vbank_full"], rd.take())
                            b = rd.bank()
                            tt(SM2[:, c, q, 0:T], b[:, 0:T], cc("window", 2, T)[:, q, :], ADD)\
                                .then_inc(S["vec_chain"], st.one())
                            ve.tensor_copy(SM2[:, c, q, T:m], b[:, T:m]).then_inc(S["vbank_free"], 1)
                        ve.wait_ge(S["vec_chain"], st.n)
                    else:
                        m = T
                        ve.wait_ge(S["vbank_full"], rd.take())
                        b = rd.bank()[:, :].rearrange("p (a b) -> p a b", a=2)
                        ve.tensor_copy(SM2[:, c, :, 0:T], b).then_inc(S["vbank_free"], 1)
                    ve.wait_ge(S["vbank_free"], rd.n)
                    mx, nm = MX[:, 2 * c:2 * c + 2], NM[:, 2 * c:2 * c + 2]
                    ve.tensor_reduce(mx, SM2[:, c, :, 0:m], AXX, MAX).then_inc(S["vec_chain"], st.one())
                    ve.wait_ge(S["vec_chain"], st.n)
                    ts(mx, mx, SCALE, pcol("sink", 8 * l + 2 * t + h), MUL, MAX).then_inc(S["vec_chain"], st.one())
                    ve.wait_ge(S["vec_chain"], st.n)
                    ts(nm, mx, -1.0, None, MUL).then_inc(S["w_scores"], 1)

                score2(0)
                for i, (s, t, h) in enumerate(units):
                    if i + 1 < len(units):
                        score2(i + 1)
                    fill = l == 0 and 2 * i < MOD_BLOCKS + 2
                    if fill:
                        mod_fill(1, 2 * i)
                    c = i % 2
                    m = 2 * T if s == 0 else T
                    su = SU[:, 2 * c:2 * c + 2]
                    ve.wait_ge(S["w_exp"], w("w_exp", 3))
                    tt(su, su, ES[:, 2 * c:2 * c + 2], ADD).then_inc(S["vec_chain"], st.one())
                    ve.wait_ge(S["vec_chain"], st.n)
                    ve.reciprocal(su, su).then_inc(S["vec_chain"], st.one())
                    ve.wait_ge(S["vec_chain"], st.n)
                    for q in range(2):
                        ts(SM2[:, c, q, 0:m], SM2[:, c, q, 0:m], su[:, q:q + 1], None, MUL)\
                            .then_inc(S["w_probs"], 1)
                    if fill:
                        mod_fill(1, 2 * i + 1)
                    if h:
                        ve.wait_ge(S["vbank_full"], rd.take())
                        b = rd.bank()
                        ve.tensor_copy(P2[:, 14 + t, s * T:(s + 1) * T], b[:, 0:T]).then_inc(S["vbank_free"], 1)

                for s in range(streams):
                    for g in range(4):
                        ve.wait_ge(S["vbank_full"], rd.take())
                        b = rd.bank()
                        ve.tensor_copy(P2[:, 26 + g, s * T:(s + 1) * T], b[:, 0:T]).then_inc(S["vbank_free"], 1)

                tot0 = TOT.rearrange("p (h c b) -> p h c b", c=4, b=1)[:, 0:4].to_broadcast([P, 4, 4, P])
                tt(KSF.rearrange("p h (c b) -> p h c b", c=4), tot0,
                   LF[:, 0:4, :].rearrange("p h (c b) -> p h c b", c=4), SUB).then_inc(S["ks_diff"], 1)
                for d in range(2):
                    ve.wait_ge(S["ks_exp"], w("ks_exp"))
                    tt(KSF, KSF, P2[:, 6 + 4 * d:10 + 4 * d, :], MUL).then_inc(S["ks_ready"], 1)
                ve.wait_ge(S["e_tot"], w("e_tot"))
                for i in range(3):
                    for d in range(2):
                        ve.wait_ge(S["vbank_full"], rd.take())
                        b = rd.bank()
                        if i == 0:
                            ve.tensor_copy(STATE[:, d, 0].rearrange("p h b -> p (h b)"), b[:, :])\
                                .then_inc(S["vbank_free"], 1)
                            continue
                        for h in range(4):
                            col = 4 * (4 * d + h) + CHUNKS[d][i]
                            ins = stt(STATE[:, d, i, h, :], STATE[:, d, i - 1, h, :], ETOT[:, col:col + 1],
                                      b[:, h * P:(h + 1) * P], MUL, ADD)
                            if h < 3:
                                ins.then_inc(S["vec_chain"], st.one())
                        ins.then_inc(S["vbank_free"], 1)
                say(S["st_ready"])
                ve.wait_ge(S["q_silu"], w("q_silu", 2))

                def halves(v, b_):
                    v = v[:, 0:n].rearrange("p (m s b) -> p m s b", s=2, b=b_)
                    return v[:, :, 0, :], v[:, :, 1, :]

                def level(h, i):
                    q, kf, kb = P2[:, 18 + h, :], P2[:, 6 + h, :], P2[:, 10 + h, :]
                    c = i % 2
                    if i == LEVELS:
                        tt(LKE[:, c, 0:n], kf[:, 0:n], kb[:, 0:n], ADD).then_inc(S["lvl_ready"], 1)
                        return
                    b_ = 1 << i
                    ve.wait_ge(S["lvl_exp"], w("lvl_exp"))
                    for half, k in ((0, kf), (1, kb)):
                        tt(halves(LKE[:, c, :], b_)[half], halves(k, b_)[half], halves(LDF[:, c, 0, :], b_)[half],
                           MUL).then_inc(S["vec_chain"], st.one())
                    tt(LQE[:, c, 0:n], q[:, 0:n], LDF[:, c, 1, 0:n], MUL).then_inc(S["lvl_ready"], 1)

                for h in range(4):
                    ve.wait_ge(S["qi_exp"], w("qi_exp", 2))
                    tt(QI[:, h % 2, 0, 0:n], QI[:, h % 2, 0, 0:n], P2[:, 18 + h, 0:n], MUL)\
                        .then_inc(S["vec_chain"], st.one())
                    tt(QI[:, h % 2, 1, 0:n], QI[:, h % 2, 1, 0:n], P2[:, 18 + h, 0:n], MUL).then_inc(S["qi_ready"], 1)
                    level(h, 0)
                    for i in range(LEVELS + 1):
                        if i < LEVELS:
                            level(h, i + 1)
                        m = mask("pairs", i) if i < LEVELS else mask("diag")
                        ve.wait_ge(S["vbank_full"], rd.take())
                        b = rd.bank()[:, 0:n].rearrange("p (c t) -> p c t", t=P)
                        ve.wait_ge(S["vbank_free"], rd.n - 1)
                        ve.copy_predicated(ATT[:, h % 2, 0:n // P, :], rep(m, n // P), b).then_inc(S["vbank_free"], 1)
                ve.wait_ge(S["o_rs"], w("o_rs"))
                for h in range(4):
                    o = P2[:, 18 + h, 0:n]
                    stt(o, o, pcol("hgrn_g", l), HRS[:, h, 0:n], MUL, MUL).then_inc(S["vec_chain"], st.one())
                ve.wait_ge(S["vec_chain"], st.n)
                tt(P2[:, 18:22, 0:n], P2[:, 18:22, 0:n], P2[:, 22:26, 0:n], MUL).then_inc(S["hgrn_done"], 1)

                for br in range(3):
                    for half in range(2):
                        i = 2 * br + half
                        rd.tiles_read(("proj", l, br, half))
                        acc = ACC[:, 4 * half:4 * half + 4, 0:n]
                        gb, pb = GB[:, i % 2, :, 0:n] if i else GATE0B[:, :, 0:n], PB[:, i % 2, :, 0:n]
                        if br == 0:
                            tt(acc, gb, pb, MUL).then_inc(S["merge_used"], 1)
                        else:
                            tt(pb, gb, pb, MUL).then_inc(S["vec_chain"], st.one())
                            ve.wait_ge(S["vec_chain"], st.n)
                            tt(acc, acc, pb, ADD).then_inc(S["merge_used"], 1)
                gated(("out2", l), 16)
                say(S["x_ready"])
                adaln(1, n)
                for k in range(DFF2 // P):
                    rd.tiles_read(("ff1", l), k + 1)
                    tt(HF2[:, k, 0:n], HF2[:, k, 0:n], HF2[:, k, 0:n], MUL).then_inc(S["ff_ready"], 1)
                gated(("ff2", l), 40)
                say(S["xo_ready"] if last else S["x_ready"])

        @block.gpsimd
        def _(pool):
            w = Waits()
            pool.dma_start(prm[:, :], par).then_inc(S["par_landed"], 16)
            pool.dma_start(MKF, msk).then_inc(S["mask_landed"], 16)
            pool.memset(PRJ[:, :, 0:1], 0.0).then_inc(S["pad_zero"], 1)
            pool.wait_ge(S["mask_landed"], 16)
            pool.tensor_copy(mk[:, :], MKF).then_inc(S["masks_ready"], 1)
            pool.wait_ge(S["xs_pool"], w("xs_pool"))
            pool.memset(ar(0, 8192), 0.0).then_inc(S["pr_zero"], 1)
            pool.wait_ge(S["x_ready"], w("x_ready"))
            pool.dma_start(WS, wsT.rearrange("g s t -> s g t")).then_inc(S["ws_landed"], 16)
            pool.dma_start(BS[0:1, :], bsr).then_inc(S["ws_landed"], 16)
            pool.dma_start(X[:, :, T:2 * T], ctxT.rearrange("(k p) t -> p k t", p=P)).then_inc(S["ctx_landed"], 16)
            for l in range(2):
                n = 2 * T if l == 0 else T
                pool.wait_ge(S["h_pool"], w("h_pool"))
                pool.wait_ge(S["lf_ready"], w("lf_ready"))
                pool.memset(ar(SCR + 4096, 4096), 0.0).then_inc(S["vz_zero"], 1)
                pool.wait_ge(S["st_ready"], w("st_ready"))
                for h in range(4):
                    gf, gb = LF[:, h, 0:n], LF[:, 4 + h, 0:n]
                    tot = TOT.rearrange("p (h c b) -> p h c b", c=4, b=1)[:, 4 + h, 0:n // P, :]
                    pool.tensor_tensor(QI[:, h % 2, 1, 0:n].rearrange("p (c t) -> p c t", t=P),
                                       tot.to_broadcast([P, n // P, P]), gb.rearrange("p (c t) -> p c t", t=P),
                                       ALU.subtract).then_inc(S["qi_diff"], 1)
                    for i in range(LEVELS):
                        b_ = 1 << i
                        if h > 0 or i >= 2:
                            pool.wait_ge(S["lvl_ready"], LVL_BASE[l] + h * (LEVELS + 1) + (i - 1 if i >= 2 else -1 - i))
                        for g, c0, c1, mid in ((gf, 0, 1, 0), (gb, 1, 0, 1)):
                            g = g.rearrange("p (m s b) -> p m s b", s=2, b=b_)
                            ea, eb = (LDF[:, i % 2, c, 0:n].rearrange("p (m s b) -> p m s b", s=2, b=b_)
                                      for c in (c0, c1))
                            first, second = g[:, :, 0, :], g[:, :, 1, :]
                            m = (first[:, :, b_ - 1:b_] if mid == 0 else second[:, :, 0:1])\
                                .to_broadcast([P, n // (2 * b_), b_])
                            pool.tensor_tensor(ea[:, :, 0, :], m, first, ALU.subtract).then_inc(S["lvl_diff"], 1)
                            pool.tensor_tensor(eb[:, :, 1, :], second, m, ALU.subtract).then_inc(S["lvl_diff"], 1)
                pool.wait_ge(S["h_pool"], w("h_pool"))


def kernel(**inputs):
    import numpy as np
    import concourse.bacc as bacc
    from concourse.bass_utils import run_bass_kernel_spmd

    a = {k: np.asarray(v) for k, v in inputs.items()}
    f = np.float32

    def cols(v):
        return np.ascontiguousarray(v).reshape(-1, P).T

    def padded(v):
        out = np.zeros((P, 1), f)
        out[:HD, 0] = v
        return out

    def wide(v):
        return np.broadcast_to(np.asarray(v, f).reshape(1, -1), (P, np.size(v)))

    parts = {
        "mu": cols(a["ab_shift_mu"][0]), "w0": cols(a["ab_w0"][0]), "a0": cols(a["ab_a0"][0]),
        "k_k": cols(a["ab_k_k"][0]), "k_a": cols(a["ab_k_a"][0]), "r_k": cols(a["ab_r_k"][0]),
        "lnx_g": cols(a["ab_lnx_g"][0]), "lnx_b": cols(a["ab_lnx_b"][0]),
        "lam_q": np.concatenate([padded(a["ab_lam_q1"][0]), padded(a["ab_lam_q2"][0])], 1),
        "lam_k": np.concatenate([padded(a["ab_lam_k1"][0]), padded(a["ab_lam_k2"][0])], 1),
        "subln_g": cols(a["ab_subln_g"][0]), "c_b_in": cols(a["c_b_in"][0]), "c_ln_g": cols(a["c_ln_g"][0]),
        "c_ln_b": cols(a["c_ln_b"][0]), "ln1_g": cols(a["ln1_g"]), "ln1_b": cols(a["ln1_b"]),
        "ln2_g": cols(a["ln2_g"]), "ln2_b": cols(a["ln2_b"]), "conv_w": cols(a["ffn_conv_w"]),
        "conv_b": cols(a["ffn_conv_b"]),
        "cond": np.stack([cols(a["c_2"][0]), cols(a["c_ctx_2"])], 2).reshape(P, 16),
        "b_mod": cols(a["b_mod_2"]), "norm1_g": cols(a["norm1_g_2"]), "norm2_g": cols(a["norm2_g_2"]),
        "q_norm": np.tile(a["q_norm_g_2"], (1, 2)).T, "k_norm": np.tile(a["k_norm_g_2"], (1, 2)).T,
        "sink": wide(a["attn_sink_2"]), "lb": cols(a["hgrn_lb_logits_2"]), "hgrn_g": a["hgrn_norm_g_2"].T,
        "eps5": wide([1e-5]), "eps6": wide([1e-6]), "eps_gn": wide([64e-5]), "one": wide([1.0]),
        "half": np.stack([np.arange(P) < HD, np.arange(P) >= HD], 1).astype(f),
    }
    par = np.concatenate([parts[n] for n, _ in PARAMS], 1).astype(f)

    i, tok = np.arange(P), np.arange(T)
    same64 = i[:, None] // HD == i[None, :] // HD

    def rope(partner, sign, angle, turned):
        m = np.zeros((P, P), f)
        m[partner[turned], i[turned]] = sign[turned]
        cos = np.where(turned[:, None], np.cos(angle), 1.0)
        sin = np.where(turned[:, None], np.sin(angle), 0.0)
        return m, cos.astype(f), sin.astype(f)

    r = i % HD
    inv = (f(500000.0) ** (-np.arange(0, 16, 2, dtype=f) / f(16))).astype(f)
    rope_a = rope(np.where(r % 16 < 8, i + 8, i - 8), np.where(r % 16 < 8, -1.0, 1.0),
                  (tok.astype(f)[None, :] * inv[r % 8][:, None]).astype(f), r < 16)
    inv = (f(10000.0) ** (-np.arange(0, 32, 2, dtype=f) / f(32))).astype(f)
    place = np.where((r < 32)[:, None], (tok // 64)[None, :], (tok % 64)[None, :]).astype(f)
    rope_b = rope(np.where(r % 32 < 16, i + 16, i - 16), np.where(r % 32 < 16, -1.0, 1.0),
                  (place * inv[r % 16][:, None]).astype(f), r >= 0)
    q = np.arange(2)[None, :, None] * P + i[:, None, None]
    key = tok[None, None, :]
    ad = 2 * np.pi * ((i[:, None] * i[None, :]) % P) / P
    at = 2 * np.pi * ((tok[:, None] * tok[None, :]) % T) / T
    at = at.reshape(2, P, T).transpose(1, 0, 2)
    consts = {
        "ident": np.eye(P), "ones": np.ones((P, P)), "block64": same64,
        "rope_a": rope_a[0], "rope_b": rope_b[0], "cos_a": rope_a[1], "sin_a": rope_a[2],
        "cos_b": rope_b[1], "sin_b": rope_b[2],
        "dup": np.stack([i[:, None] == kv * HD + i[None, :] % HD for kv in range(2)], 1),
        "reset": np.broadcast_to(np.arange(512) % P != 0, (P, 512)),
        "causal": np.where(key <= q, 0.0, -1e30), "window": np.where(abs(key - q) <= P, 0.0, -1e30),
        "dft_d": np.concatenate([np.cos(ad), np.sin(ad)], 1) / np.sqrt(P),
        "dft_t": np.stack([np.cos(at), -np.sin(at)], 2) / np.sqrt(T),
    }
    cst = np.concatenate([np.asarray(consts[n], f).reshape(P, -1) for n, _ in CONSTS], 1)
    s, t = i[:, None], i[None, :]
    fwd = [(s // (2 * b) == t // (2 * b)) & (s % (2 * b) < b) & (t % (2 * b) >= b) for b in 1 << np.arange(LEVELS)]
    masks = {"rwkv": np.concatenate([s < t, s <= t, s < t, s <= t], 1), "fwd": np.concatenate(fwd, 1),
             "bwd": np.concatenate([m.T for m in fwd], 1), "diag": s == t,
             "pairs": np.concatenate([m | m.T for m in fwd], 1)}
    msk = np.concatenate([masks[n] for n, _ in MASKS], 1).astype(f)
    lora = np.zeros((3, P, 512), f)
    lora[0, :HD], lora[1, HD:], lora[2] = a["ab_w2"][0], a["ab_a2"][0], a["ab_g2"][0]

    arrays = {
        "xT": a["x"][0].T, "ctxT": a["ctx_2"][0].T, "par": par, "cst": cst, "msk": msk, "lora": lora,
        "wsT": a["c_w_s"][0].transpose(0, 2, 1), "bsr": a["c_b_s"].reshape(1, -1),
        "ab_w_in": a["ab_w_in"], "ab_w_out": a["ab_w_out"], "c_w_in": a["c_w_in"], "c_w_out": a["c_w_out"],
        "ffn_up": a["ffn_w_up"], "ffn_down": a["ffn_w_down"], "w_mod": a["w_mod_2"], "w_in2": a["w_in_2"],
        "w_branch": a["w_branch_2"], "w_out2": a["w_out_2"], "w_ff1": a["w_ff1_2"], "w_ff2": a["w_ff2_2"],
    }
    arrays = {k: np.ascontiguousarray(v) for k, v in arrays.items()}
    nc = bacc.Bacc("TRN2", target_bir_lowering=False, num_devices=1)
    aps = [nc.dram_tensor(k, v.shape, mybir.dt.from_np(v.dtype), kind="ExternalInput").ap()
           for k, v in arrays.items()]
    out = nc.dram_tensor("out", (D, T), F32, kind="ExternalOutput").ap()
    build(nc, *aps, out)
    res = run_bass_kernel_spmd(nc, [arrays], core_ids=[0])
    return np.ascontiguousarray(res.results[0]["out"].T).reshape(1, T, D)
```
